# Optimizing a Trainium2 kernel written in Bass

```python
import math
import jax, jax.numpy as jnp
from jax import lax
import numpy as np

D_MODEL = 1024
BATCH = 1
SEQ = 256
DEPTH = 4

CTX_LEN = 256
GRID_W = 64
N_MIXERS = 4
QBLOCK = 128
ROPE_THETA = 10000.0
NORM_EPS = 1e-6
LN_EPS = 1e-5
N_MOD = 6
A_HEADS = 16
A_KV_HEADS = 4
A_HEAD_DIM = 64
B_HEADS = 8
B_HEAD_DIM = 64
C_HEADS = 4
C_KEY_DIM = D_MODEL // 2
C_VAL_DIM = D_MODEL
C_GATE_RANK = 16
C_GATE_NORMALIZER = 16.0
C_CHUNK = 64
D_HEADS = 16
D_HEAD_DIM = 64
WIN_R = 8
WIN_C = 16
FF_DIM = 2816
CONV_W = 3
DEEPNORM_ALPHA = (2 * DEPTH) ** 0.25
DEEPNORM_BETA = (8 * DEPTH) ** -0.25

kernel_name = "hybrid_diffusion_interleaved_block"

def rms_norm(x, g, eps=NORM_EPS):
    xf = x.astype(jnp.float32)
    y = xf * lax.rsqrt(jnp.mean(xf * xf, axis=-1, keepdims=True) + eps)
    return (y * g.astype(jnp.float32)).astype(x.dtype)

def layer_norm(x, g, b):
    xf = x.astype(jnp.float32)
    mu = jnp.mean(xf, axis=-1, keepdims=True)
    var = jnp.mean(jnp.square(xf - mu), axis=-1, keepdims=True)
    y = (xf - mu) * lax.rsqrt(var + LN_EPS)
    return (y * g.astype(jnp.float32) + b.astype(jnp.float32)).astype(x.dtype)

def _split_heads(x, n_heads):
    b, l, _ = x.shape
    return x.reshape(b, l, n_heads, -1).transpose(0, 2, 1, 3)

def _merge_heads(x):
    b, h, l, d = x.shape
    return x.transpose(0, 2, 1, 3).reshape(b, l, h * d)

def _softmax32(s):
    return jax.nn.softmax(s.astype(jnp.float32), axis=-1)

def axial_rope(n_tokens, head_dim):
    t = jnp.arange(n_tokens)
    row = (t // GRID_W).astype(jnp.float32)
    col = (t % GRID_W).astype(jnp.float32)
    n_freq = head_dim // 4
    inv = 1.0 / (ROPE_THETA ** (jnp.arange(n_freq, dtype=jnp.float32) / n_freq))
    ang = jnp.concatenate([row[:, None] * inv, col[:, None] * inv], axis=-1)
    return jnp.cos(ang), jnp.sin(ang)

def apply_rope(x, cos, sin):
    half = x.shape[-1] // 2
    x1 = x[..., :half].astype(jnp.float32)
    x2 = x[..., half:].astype(jnp.float32)
    return jnp.concatenate([x1 * cos - x2 * sin, x1 * sin + x2 * cos], axis=-1).astype(x.dtype)

def sweep_query_blocks(fn, qs):
    n = qs[0].shape[-2]
    nb = n // QBLOCK

    def split(a):
        a = a.reshape(a.shape[:-2] + (nb, QBLOCK, a.shape[-1]))
        return jnp.moveaxis(a, -3, 0)

    out = lax.map(lambda blk: fn(*blk), tuple(split(a) for a in qs))
    out = jnp.moveaxis(out, 0, -3)
    return out.reshape(out.shape[:-3] + (n, out.shape[-1]))

def gqa_mixer(h_lat, h_ctx, w_qkv, q_norm, k_norm, w_o, cos, sin, with_ctx_out):
    hq, hkv, d = A_HEADS, A_KV_HEADS, A_HEAD_DIM
    grp = hq // hkv
    scale = d ** -0.5
    cuts = [hq * d, hq * d + hkv * d]

    def project(h):
        q, k, v = jnp.split(h @ w_qkv, cuts, axis=-1)
        return _split_heads(q, hq), rms_norm(_split_heads(k, hkv), k_norm), _split_heads(v, hkv)

    q_l, k_l, v_l = project(h_lat)
    q_c, k_c, v_c = project(h_ctx)
    q_l = apply_rope(rms_norm(q_l, q_norm), cos, sin)
    k_l = apply_rope(k_l, cos, sin)
    k_all = jnp.concatenate([k_c, k_l], axis=2)
    v_all = jnp.concatenate([v_c, v_l], axis=2)

    def attend(q, k, v):
        s = jnp.einsum("bkgqd,bkld->bkgql", q, k).astype(jnp.float32) * scale
        p = _softmax32(s).astype(v.dtype)
        return jnp.einsum("bkgql,bkld->bkgqd", p, v)

    bsz, _, n_lat, _ = q_l.shape
    o_l = sweep_query_blocks(lambda qb: attend(qb, k_all, v_all),
                             (q_l.reshape(bsz, hkv, grp, n_lat, d),))
    y_lat = _merge_heads(o_l.reshape(bsz, hq, n_lat, d)) @ w_o
    if not with_ctx_out:
        return y_lat, None
    n_ctx = q_c.shape[2]
    q_c = rms_norm(q_c, q_norm).reshape(bsz, hkv, grp, n_ctx, d)
    o_c = attend(q_c, k_c, v_c)
    y_ctx = _merge_heads(o_c.reshape(bsz, hq, n_ctx, d)) @ w_o
    return y_lat, y_ctx

def diff_mixer(h_lat, h_ctx, w_qkv, lam_q1, lam_k1, lam_q2, lam_k2, subln, w_o,
               cos, sin, layer_idx, with_ctx_out):
    nh, d = B_HEADS, B_HEAD_DIM
    scale = d ** -0.5
    lam_init = 0.8 - 0.6 * math.exp(-0.3 * layer_idx)
    lam = (jnp.exp(jnp.sum(lam_q1.astype(jnp.float32) * lam_k1.astype(jnp.float32)))
           - jnp.exp(jnp.sum(lam_q2.astype(jnp.float32) * lam_k2.astype(jnp.float32)))
           + lam_init)
    cuts = [2 * nh * d, 4 * nh * d]

    def project(h):
        bsz, n, _ = h.shape
        q, k, v = jnp.split(h @ w_qkv, cuts, axis=-1)
        q = q.reshape(bsz, n, nh, 2, d).transpose(3, 0, 2, 1, 4)
        k = k.reshape(bsz, n, nh, 2, d).transpose(3, 0, 2, 1, 4)
        return q, k, _split_heads(v, nh)

    q_l, k_l, v_l = project(h_lat)
    q_c, k_c, v_c = project(h_ctx)
    q_l = apply_rope(q_l, cos, sin)
    k_l = apply_rope(k_l, cos, sin)
    k_all = jnp.concatenate([k_c, k_l], axis=3)
    v_all = jnp.concatenate([v_c, v_l], axis=2)

    def attend(q1, q2, k, v):
        s1 = jnp.einsum("bhqd,bhld->bhql", q1, k[0]).astype(jnp.float32) * scale
        s2 = jnp.einsum("bhqd,bhld->bhql", q2, k[1]).astype(jnp.float32) * scale
        p = _softmax32(s1) - lam * _softmax32(s2)
        return jnp.einsum("bhql,bhle->bhqe", p.astype(v.dtype), v)

    def finish(o):
        return _merge_heads(rms_norm(o, subln) * (1.0 - lam_init)) @ w_o

    o_l = sweep_query_blocks(lambda a, b: attend(a, b, k_all, v_all), (q_l[0], q_l[1]))
    y_lat = finish(o_l)
    if not with_ctx_out:
        return y_lat, None
    y_ctx = finish(attend(q_c[0], q_c[1], k_c, v_c))
    return y_lat, y_ctx

def gla_chunk_scan(q, k, v, g, s0):
    bsz, nh, n_tok, _ = q.shape
    nc = n_tok // C_CHUNK

    def chunks(a):
        return jnp.moveaxis(a.reshape(bsz, nh, nc, C_CHUNK, a.shape[-1]), 2, 0)

    tri = jnp.tril(jnp.ones((C_CHUNK, C_CHUNK), dtype=bool))

    def step(s, blk):
        qc, kc, vc, gc = blk
        b = jnp.cumsum(gc, axis=-2)
        b_last = b[:, :, -1:, :]
        o_inter = jnp.einsum("bhld,bhdv->bhlv", qc * jnp.exp(b), s)
        rel = b[:, :, :, None, :] - b[:, :, None, :, :]
        decay = jnp.exp(jnp.where(tri[:, :, None], rel, -jnp.inf))
        a = jnp.einsum("bhid,bhjd,bhijd->bhij", qc, kc, decay)
        o = o_inter + jnp.einsum("bhij,bhjv->bhiv", a, vc)
        s = (s * jnp.exp(b_last)[:, :, 0, :, None]
             + jnp.einsum("bhld,bhlv->bhdv", kc * jnp.exp(b_last - b), vc))
        return s, o

    s, o = lax.scan(step, s0, (chunks(q), chunks(k), chunks(v), chunks(g)))
    o = jnp.moveaxis(o, 0, 2).reshape(bsz, nh, n_tok, v.shape[-1])
    return o, s

def gla_final_state(k, v, g):
    b = jnp.cumsum(g, axis=-2)
    return jnp.einsum("bhtd,bhtv->bhdv", k * jnp.exp(b[:, :, -1:, :] - b), v)

def gla_mixer(h_lat, h_ctx, w_in, w_gate_fwd, b_gate_fwd, w_gate_bwd, b_gate_bwd,
              norm_g, w_o, with_ctx_out):
    nh = C_HEADS
    dk, dv = C_KEY_DIM // nh, C_VAL_DIM // nh
    cuts = np.cumsum([C_KEY_DIM, C_KEY_DIM, C_VAL_DIM, C_VAL_DIM, C_GATE_RANK]).tolist()

    def heads32(a):
        return _split_heads(a, nh).astype(jnp.float32)

    def log_gate(z, w, b):
        return heads32(jax.nn.log_sigmoid((z @ w + b).astype(jnp.float32)) / C_GATE_NORMALIZER)

    def project(h):
        q, k, v, og, zf, zb = jnp.split(h @ w_in, cuts, axis=-1)
        return (heads32(q) * dk ** -0.5, heads32(k), heads32(v),
                log_gate(zf, w_gate_fwd, b_gate_fwd), log_gate(zb, w_gate_bwd, b_gate_bwd), og)

    def flip(a):
        return jnp.flip(a, axis=2)

    def finish(o, og):
        o = _merge_heads(rms_norm(o, norm_g)).astype(og.dtype)
        return (o * jax.nn.silu(og)) @ w_o

    q_l, k_l, v_l, gf_l, gb_l, og_l = project(h_lat)
    q_c, k_c, v_c, gf_c, gb_c, og_c = project(h_ctx)
    zero = jnp.zeros((q_l.shape[0], nh, dk, dv), jnp.float32)
    if with_ctx_out:
        o_cf, s_f = gla_chunk_scan(q_c, k_c, v_c, gf_c, zero)
        o_cb, s_b = gla_chunk_scan(flip(q_c), flip(k_c), flip(v_c), flip(gb_c), zero)
        y_ctx = finish(o_cf + flip(o_cb), og_c)
    else:
        s_f = gla_final_state(k_c, v_c, gf_c)
        s_b = gla_final_state(flip(k_c), flip(v_c), flip(gb_c))
        y_ctx = None
    o_lf, _ = gla_chunk_scan(q_l, k_l, v_l, gf_l, s_f)
    o_lb, _ = gla_chunk_scan(flip(q_l), flip(k_l), flip(v_l), flip(gb_l), s_b)
    y_lat = finish(o_lf + flip(o_lb), og_l)
    return y_lat, y_ctx

def neighbourhood_mixer(h_lat, h_ctx, w_qkv, rpb, w_o, with_ctx_out):
    nh, d = D_HEADS, D_HEAD_DIM
    scale = d ** -0.5
    cuts = [nh * d, 2 * nh * d]

    def project(h):
        q, k, v = jnp.split(h @ w_qkv, cuts, axis=-1)
        return _split_heads(q, nh), _split_heads(k, nh), _split_heads(v, nh)

    q_l, k_l, v_l = project(h_lat)
    q_c, k_c, v_c = project(h_ctx)
    bsz, _, n_lat, _ = q_l.shape
    rows = n_lat // GRID_W
    wr = min(WIN_R, rows)

    def grid(a):
        return a.reshape(bsz, nh, rows, GRID_W, d)

    k_g, v_g = grid(k_l), grid(v_l)
    cq = np.arange(GRID_W)
    c0 = np.clip(cq - WIN_C // 2, 0, GRID_W - WIN_C)
    col_in = (cq[None, :] >= c0[:, None]) & (cq[None, :] < c0[:, None] + WIN_C)
    dc_idx = np.clip(cq[None, :] - cq[:, None], -(WIN_C - 1), WIN_C - 1) + WIN_C - 1
    n_band = wr * GRID_W

    def row_block(r, q_r):
        r0 = jnp.clip(r - wr // 2, 0, rows - wr)
        k_band = lax.dynamic_slice_in_dim(k_g, r0, wr, axis=2)
        v_band = lax.dynamic_slice_in_dim(v_g, r0, wr, axis=2)
        dr_idx = r0 + jnp.arange(wr) - r + (WIN_R - 1)
        bias = jnp.take(rpb, dr_idx, axis=1)[:, :, dc_idx]
        bias = bias.transpose(0, 2, 1, 3).astype(jnp.float32)
        s_nb = jnp.einsum("bhqd,bhrkd->bhqrk", q_r, k_band).astype(jnp.float32) * scale + bias
        s_nb = jnp.where(col_in[:, None, :], s_nb, -jnp.inf).reshape(bsz, nh, GRID_W, n_band)
        s_c = jnp.einsum("bhqd,bhcd->bhqc", q_r, k_c).astype(jnp.float32) * scale
        p = _softmax32(jnp.concatenate([s_nb, s_c], axis=-1)).astype(v_l.dtype)
        p_nb = p[..., :n_band].reshape(bsz, nh, GRID_W, wr, GRID_W)
        return (jnp.einsum("bhqrk,bhrkd->bhqd", p_nb, v_band)
                + jnp.einsum("bhqc,bhcd->bhqd", p[..., n_band:], v_c))

    q_rows = jnp.moveaxis(grid(q_l), 2, 0)
    o = lax.map(lambda a: row_block(*a), (jnp.arange(rows), q_rows))
    o = jnp.moveaxis(o, 0, 2).reshape(bsz, nh, n_lat, d)
    y_lat = _merge_heads(o) @ w_o
    if not with_ctx_out:
        return y_lat, None
    s = jnp.einsum("bhqd,bhcd->bhqc", q_c, k_c).astype(jnp.float32) * scale
    o_c = jnp.einsum("bhqc,bhcd->bhqd", _softmax32(s).astype(v_c.dtype), v_c)
    return y_lat, _merge_heads(o_c) @ w_o

def dwconv_centred(u, w, b):
    pad = CONV_W // 2
    n = u.shape[1]
    up = jnp.pad(u, ((0, 0), (pad, pad), (0, 0)))
    out = b
    for j in range(CONV_W):
        out = out + up[:, j:j + n] * w[j]
    return out

def conv_ffn(h, w_up, conv_w, conv_b, w_down):
    u = dwconv_centred(h @ w_up, conv_w, conv_b)
    gate, val = jnp.split(u, 2, axis=-1)
    return (jax.nn.silu(gate) * val) @ w_down

def _n_of(kind):
    return len(range(kind, DEPTH, N_MIXERS))

def setup_inputs(seed: int = 0) -> dict:
    key = jax.random.key(seed)
    ks = iter(jax.random.split(key, 48))

    def nrm(shape, scale):
        return jax.random.normal(next(ks), shape, jnp.float32) * scale

    D = D_MODEL
    na, nb, nc, nd = _n_of(0), _n_of(1), _n_of(2), _n_of(3)
    beta = DEEPNORM_BETA
    return {
        "x": nrm((BATCH, SEQ, D), 1.0),
        "c": nrm((BATCH, D), 1.0),
        "ctx": nrm((BATCH, CTX_LEN, D), 1.0),
        "c_ctx": nrm((D,), 1.0),
        "mod_w": nrm((DEPTH, D, N_MOD * D), 0.5 * D ** -0.5),
        "mod_b": nrm((DEPTH, N_MOD * D), 0.02),
        "ln1_g": 1.0 + nrm((DEPTH, D), 0.02),
        "ln1_b": nrm((DEPTH, D), 0.02),
        "ffn_w_up": nrm((DEPTH, D, 2 * FF_DIM), D ** -0.5),
        "ffn_conv_w": nrm((DEPTH, CONV_W, 2 * FF_DIM), CONV_W ** -0.5),
        "ffn_conv_b": nrm((DEPTH, 2 * FF_DIM), 0.02),
        "ffn_w_down": nrm((DEPTH, FF_DIM, D), beta * FF_DIM ** -0.5),
        "ln2_g": 1.0 + nrm((DEPTH, D), 0.02),
        "ln2_b": nrm((DEPTH, D), 0.02),
        "a_w_qkv": nrm((na, D, (A_HEADS + 2 * A_KV_HEADS) * A_HEAD_DIM), D ** -0.5),
        "a_q_norm": 1.0 + nrm((na, A_HEAD_DIM), 0.02),
        "a_k_norm": 1.0 + nrm((na, A_HEAD_DIM), 0.02),
        "a_w_o": nrm((na, A_HEADS * A_HEAD_DIM, D), beta * (A_HEADS * A_HEAD_DIM) ** -0.5),
        "b_w_qkv": nrm((nb, D, 6 * B_HEADS * B_HEAD_DIM), D ** -0.5),
        "b_lambda_q1": nrm((nb, B_HEAD_DIM), 0.1),
        "b_lambda_k1": nrm((nb, B_HEAD_DIM), 0.1),
        "b_lambda_q2": nrm((nb, B_HEAD_DIM), 0.1),
        "b_lambda_k2": nrm((nb, B_HEAD_DIM), 0.1),
        "b_subln": 1.0 + nrm((nb, 2 * B_HEAD_DIM), 0.02),
        "b_w_o": nrm((nb, 2 * B_HEADS * B_HEAD_DIM, D), beta * (2 * B_HEADS * B_HEAD_DIM) ** -0.5),
        "c_w_in": nrm((nc, D, 2 * C_KEY_DIM + 2 * C_VAL_DIM + 2 * C_GATE_RANK), D ** -0.5),
        "c_w_gate_fwd": nrm((nc, C_GATE_RANK, C_KEY_DIM), C_GATE_RANK ** -0.5),
        "c_b_gate_fwd": nrm((nc, C_KEY_DIM), 0.02),
        "c_w_gate_bwd": nrm((nc, C_GATE_RANK, C_KEY_DIM), C_GATE_RANK ** -0.5),
        "c_b_gate_bwd": nrm((nc, C_KEY_DIM), 0.02),
        "c_norm": 1.0 + nrm((nc, C_VAL_DIM // C_HEADS), 0.02),
        "c_w_o": nrm((nc, C_VAL_DIM, D), beta * C_VAL_DIM ** -0.5),
        "d_w_qkv": nrm((nd, D, 3 * D_HEADS * D_HEAD_DIM), D ** -0.5),
        "d_rpb": nrm((nd, D_HEADS, 2 * WIN_R - 1, 2 * WIN_C - 1), 0.02),
        "d_w_o": nrm((nd, D_HEADS * D_HEAD_DIM, D), beta * (D_HEADS * D_HEAD_DIM) ** -0.5),
    }

def reference(x, c, ctx, c_ctx, mod_w, mod_b, ln1_g, ln1_b, ffn_w_up, ffn_conv_w,
              ffn_conv_b, ffn_w_down, ln2_g, ln2_b,
              a_w_qkv, a_q_norm, a_k_norm, a_w_o,
              b_w_qkv, b_lambda_q1, b_lambda_k1, b_lambda_q2, b_lambda_k2, b_subln, b_w_o,
              c_w_in, c_w_gate_fwd, c_b_gate_fwd, c_w_gate_bwd, c_b_gate_bwd, c_norm, c_w_o,
              d_w_qkv, d_rpb, d_w_o):
    bsz, n_lat, dm = x.shape
    cos, sin = axial_rope(n_lat, A_HEAD_DIM)
    cond_lat = jax.nn.silu(c)
    cond_ctx = jax.nn.silu(c_ctx)
    alpha = DEEPNORM_ALPHA
    x_lat, x_ctx = x, ctx
    for i in range(DEPTH):
        kind, j = i % N_MIXERS, i // N_MIXERS
        last = i == DEPTH - 1
        m_lat = (cond_lat @ mod_w[i] + mod_b[i]).reshape(bsz, N_MOD, 1, dm)
        n_ctx_mod = 3 if last else N_MOD
        m_ctx = (cond_ctx @ mod_w[i][:, :n_ctx_mod * dm] + mod_b[i][:n_ctx_mod * dm]).reshape(n_ctx_mod, dm)
        h_lat = x_lat * (1.0 + m_lat[:, 1]) + m_lat[:, 0]
        h_ctx = x_ctx * (1.0 + m_ctx[1]) + m_ctx[0]
        if kind == 0:
            y_lat, y_ctx = gqa_mixer(h_lat, h_ctx, a_w_qkv[j], a_q_norm[j], a_k_norm[j], a_w_o[j],
                                     cos, sin, not last)
        elif kind == 1:
            y_lat, y_ctx = diff_mixer(h_lat, h_ctx, b_w_qkv[j], b_lambda_q1[j], b_lambda_k1[j],
                                      b_lambda_q2[j], b_lambda_k2[j], b_subln[j], b_w_o[j],
                                      cos, sin, i, not last)
        elif kind == 2:
            y_lat, y_ctx = gla_mixer(h_lat, h_ctx, c_w_in[j], c_w_gate_fwd[j], c_b_gate_fwd[j],
                                     c_w_gate_bwd[j], c_b_gate_bwd[j], c_norm[j], c_w_o[j], not last)
        else:
            y_lat, y_ctx = neighbourhood_mixer(h_lat, h_ctx, d_w_qkv[j], d_rpb[j], d_w_o[j], not last)
        x_lat = layer_norm(alpha * x_lat + m_lat[:, 2] * y_lat, ln1_g[i], ln1_b[i])
        h_lat = x_lat * (1.0 + m_lat[:, 4]) + m_lat[:, 3]
        f_lat = conv_ffn(h_lat, ffn_w_up[i], ffn_conv_w[i], ffn_conv_b[i], ffn_w_down[i])
        x_lat = layer_norm(alpha * x_lat + m_lat[:, 5] * f_lat, ln2_g[i], ln2_b[i])
        if not last:
            x_ctx = layer_norm(alpha * x_ctx + m_ctx[2] * y_ctx, ln1_g[i], ln1_b[i])
            h_ctx = x_ctx * (1.0 + m_ctx[4]) + m_ctx[3]
            f_ctx = conv_ffn(h_ctx, ffn_w_up[i], ffn_conv_w[i], ffn_conv_b[i], ffn_w_down[i])
            x_ctx = layer_norm(alpha * x_ctx + m_ctx[5] * f_ctx, ln2_g[i], ln2_b[i])
    return x_lat


_drawn_inputs = setup_inputs


def setup_inputs(seed=0):
    import zlib

    import numpy as np

    out = dict(_drawn_inputs(seed))
    spreads = {}
    factors = {'ctx': 2.7,
     'mod_b': 4.964,
     'ffn_conv_b': 8.0,
     'a_w_qkv': 2.874,
     'a_q_norm': 8.0,
     'a_k_norm': 8.0,
     'a_w_o': 3.238,
     'b_lambda_q1': 8.0,
     'b_lambda_k1': 8.0,
     'b_lambda_q2': 8.0,
     'b_lambda_k2': 8.0,
     'b_subln': 8.0,
     'c_w_gate_fwd': 8.0,
     'c_b_gate_fwd': 33.433,
     'c_w_gate_bwd': 8.0,
     'c_b_gate_bwd': 24.695,
     'c_norm': 27.619,
     'd_w_qkv': 2.732,
     'd_rpb': 31.585,
     'd_w_o': 2.745}
    for name, (base, spread) in spreads.items():
        noise = np.random.default_rng([zlib.crc32(name.encode()), seed]).standard_normal(out[name].shape)
        drawn = base * np.exp(spread * noise) if base else spread * noise
        out[name] = __import__('jax').numpy.asarray(drawn.astype(out[name].dtype))
    for name, factor in factors.items():
        out[name] = (out[name] * factor).astype(out[name].dtype)
    return out
```

```python
import math
from contextlib import ExitStack

import numpy as np

import concourse.bass as bass
import concourse.mybir as mybir

f32, f32r = mybir.dt.float32, mybir.dt.float32r
ACT, ALU = mybir.ActivationFunctionType, mybir.AluOpType
AX = mybir.AxisListType.X

P = 128
D, DEPTH = 1024, 4
CTX, LAT = 256, 256
T = CTX + LAT
DT = D // P
FF = 2816
FT = FF // P
GRID_W = 64
N_MOD = 6
A_HEADS, A_KV, B_HEADS, C_HEADS, D_HEADS, HD = 16, 4, 8, 4, 16, 64
C_KEY, C_VAL, C_RANK, C_NORMALIZER = 512, 1024, 16, 16.0
WIN_C, N_DR, N_DC = 16, 15, 31
NORM_EPS, LN_EPS = 1e-6, 1e-5
ALPHA = (2 * DEPTH) ** 0.25
SCALE = HD ** -0.5
LAM_INIT = 0.8 - 0.6 * math.exp(-0.3 * 1)

R_MODB, R_LN1G, R_LN1B, R_LN2G, R_LN2B, R_CB, R_CW = 0, 48, 56, 64, 72, 80, 124
R_LAYER = 256

K_ID, K_SWAP, K_ONES, K_HEAD, K_COS, K_SIN, K_EPS = 0, 128, 256, 384, 512, 768, 1024
K_N = 1032

SLOTS = 4
AHEAD = SLOTS - 1
SLAB = 1024
NB = 512

CH = 128
LEVELS = 7
C_UNITS = 2 * C_HEADS
C_ITEMS = 2 * C_UNITS
C_HV = C_VAL // C_HEADS


def constants():
    k = np.zeros((P, K_N), np.float32)
    i = np.arange(P)
    k[:, K_ID:K_ID + P] = np.eye(P)
    k[i ^ 32, K_SWAP + i] = 1.0
    k[:, K_ONES:K_ONES + P] = 1.0
    k[:, K_HEAD:K_HEAD + P] = (i[:, None] // HD == i[None, :] // HD)
    t = np.arange(LAT)
    nf = HD // 4
    inv = (np.float32(1.0) / np.float32(10000.0) ** (np.arange(nf, dtype=np.float32) / np.float32(nf))).astype(np.float32)
    ang = np.concatenate([(t // GRID_W).astype(np.float32)[:, None] * inv,
                          (t % GRID_W).astype(np.float32)[:, None] * inv], -1).astype(np.float32)
    pair = i % 32
    k[:, K_COS:K_COS + LAT] = np.cos(ang).T[pair]
    k[:, K_SIN:K_SIN + LAT] = np.sin(ang).T[pair] * np.where(i % HD < 32, -1.0, 1.0)[:, None]
    k[:, K_EPS], k[:, K_EPS + 1], k[:, K_EPS + 2] = NORM_EPS, LN_EPS, 1.0
    k[0:2, K_EPS + 3], k[2:4, K_EPS + 4] = 1.0, 1.0
    cq = np.arange(GRID_W)
    c0 = np.clip(cq - WIN_C // 2, 0, GRID_W - WIN_C)
    col_in = (cq[None, :] >= c0[:, None]) & (cq[None, :] < c0[:, None] + WIN_C)
    window = np.tile(np.where(col_in, 0.0, -1e30).astype(np.float32)[::-1], (2, 1))
    return k, window


def block_masks():
    j, i = np.arange(P)[:, None], np.arange(P)[None, :]
    return np.stack([(i >> (7 - l)) == (j >> (7 - l)) for l in range(8)], 1).astype(np.float32)


class Count:

    def __init__(self, sem):
        self.sem, self.n = sem, 0

    def up(self, ins, by=1):
        ins.then_inc(self.sem, by)
        self.n += by
        return self.n


def make_plan(layers):
    slabs, owner, start = [], [], {}

    def mod_group(layer, g):
        slabs.extend(("mod", layer, g, q) for q in range(4))

    start["mod"] = (0, 0)
    for g in range(4):
        mod_group(0, g)
    for i in range(layers):
        start["qkv", i] = (len(slabs), len(owner))
        if i == 0:
            for ft in range(8):
                slabs.append(("f", "a_w_qkv", ft * P, 0, 8))
                owner.append("dve")
                mod_group(0, 4 + ft)
            for ft in range(8, 10):
                slabs.append(("f", "a_w_qkv", ft * P, 0, 8))
                owner.append("dve")
            slabs.extend(("v", "a_w_qkv", 1280, q) for q in range(2))
            owner += ["dve"] * 2
        elif i == 1 or i == 3:
            name = "b_w_qkv" if i == 1 else "d_w_qkv"
            for ft in range(16):
                slabs.append(("f", name, ft * P, 0, 8))
                owner.append("act")
            for g in range(4):
                slabs.extend(("v", name, 2048 + 256 * g, q) for q in range(2))
                owner += ["dve"] * 2
        else:
            for ft in range(8):
                slabs.append(("f", "c_w_in", ft * P, 0, 8))
                owner.append("act")
            for g in range(4):
                slabs.extend(("v", "c_w_in", 1024 + 256 * g, q) for q in range(2))
                owner += ["dve"] * 2
            for ft in range(8):
                slabs.append(("f", "c_w_in", 2048 + ft * P, 0, 8))
                owner.append("act")
        start["wo", i] = (len(slabs), len(owner))
        for dt in range(DT):
            slabs.append(("f", "abcd"[i] + "_w_o", dt * P, 0, 8))
            owner.append("act")
        start["premod", i] = (len(slabs), len(owner))
        if i + 1 < layers:
            mod_group(i + 1, 0)
        start["up", i] = (len(slabs), len(owner))
        for j in range(FT):
            for c, col in enumerate((j * P, FF + j * P)):
                slabs.append(("up", i, col))
                owner.append("dve")
                if i + 1 < layers:
                    m = 2 * j + c
                    slabs.append(("mod", i + 1, 1 + m // 4, m % 4))
        start["down", i] = (len(slabs), len(owner))
        for dt in range(DT):
            for k0, nk in ((0, 8), (8, 8), (16, 6)):
                slabs.append(("down", i, dt * P, k0, nk))
            owner.append("act")
    freed, seen = [], {"act": 0, "dve": 0}
    for e in owner:
        seen[e] += 1
        freed.append((e, seen[e]))
    return slabs, freed, start


def build_program(nc, a, layers=DEPTH, probe=None):
    slabs, freed, start = make_plan(layers)
    n_slabs = len(slabs)
    ctx = ExitStack()
    with ctx:
        top = [(nc.sbuf_base + 63) // 64 * 64]

        def place(name, shape, dt=f32, at=None):
            size = int(np.prod(shape[1:])) * mybir.dt.size(dt)
            offset = top[0] if at is None else at[0]
            (top if at is None else at)[0] += (size + 63) // 64 * 64
            return nc.alloc_sbuf_tensor_at(name, list(shape), dt, offset=offset)

        xn = place("xn", [P, DT, T])
        h_hi, h_lo = place("h_hi", [P, DT, T], f32r), place("h_lo", [P, DT, T], f32r)
        raw = [place(f"slab_raw{s}", [P, SLAB]) for s in range(SLOTS)]
        whi = [place(f"slab_hi{s}", [P, SLAB], f32r) for s in range(SLOTS)]
        wlo = [place(f"slab_lo{s}", [P, SLAB], f32r) for s in range(SLOTS)]
        rotary_at = [top[0] + 4 * K_COS]
        cst = place("cst", [P, K_N])
        k_end = [place(f"k_end{s}", [P, 2 * CH], at=rotary_at) for s in range(2)]
        prm = place("prm", [P, DEPTH * R_LAYER])
        modT = [place(f"modT{s}", [P, N_MOD * DT, 2]) for s in range(2)]
        coef = [place(f"coef{s}", [P, 6, DT]) for s in range(2)]
        unit_gb = place("unit_gb", [P, 2, DT])
        mod_row_at = [top[0]]
        mod_row = place("mod_row", [4, NB])
        w_gate = place("w_gate", [48, C_KEY], at=mod_row_at)
        small_row = place("small_row", [32, P])
        cond_row = place("cond_row", [16, P])
        cond = place("cond", [P, 2, DT])
        cond4 = place("cond4", [P, DT, 4], f32r)
        small = place("small", [P, 32])
        mean, rstd = place("mean", [P, T]), place("rstd", [P, T])
        work = [top[0]]
        res_t = [place(f"res_t{s}", [P, T], at=work) for s in range(2)]
        acc_s, acc_q = place("acc_s", [P, T], at=work), place("acc_q", [P, T], at=work)
        sq = place("sq", [P, T], at=work)
        conv_at = [top[0]]
        conv = [[place(f"conv{c}{u}", [P, T], at=conv_at) for u in range(2)] for c in range(2)]
        g32 = [place(f"g32_{u}", [P, T], at=conv_at) for u in range(2)]
        gla_at = [top[0]]
        masked = [place(f"masked{s}", [P, 8, CH], at=gla_at) for s in range(2)]
        o_head = [place(f"o_head{v}", [P, T], at=gla_at) for v in range(2)]
        top[0] = max(work[0], conv_at[0])
        arena = top[0]
        at = [arena]
        tok = place("tok", [P, 4, D], at=at)
        rows = place("rows", [P, 8, P], at=at)
        at = [arena]
        g_hi, g_lo = place("g_hi", [P, FT, T], f32r, at=at), place("g_lo", [P, FT, T], f32r, at=at)
        at = [arena]
        qk = place("qk", [P, 16, T], at=at)
        v_tok = place("v_tok", [P, 4, D], at=at)
        p1 = [place(f"p1_{s}", [P, T], at=at) for s in range(3)]
        pt = [place(f"pt{s}", [P, 4, 256], at=at) for s in range(2)]
        stat = place("stat", [P, 6, 128], at=at)
        own = at[0]
        at = [own]
        kd = place("kd", [P, A_KV, T], at=at)
        sqa = [place(f"sqa{s}", [P, T], at=at) for s in range(2)]
        rsa = [place(f"rsa{s}", [P, T], at=at) for s in range(2)]
        rope_t = place("rope_t", [P, LAT], at=at)
        at = [own]
        rope_b = place("rope_b", [P, LAT], at=at)
        p2 = [place(f"p2_{s}", [P, T], at=at) for s in range(3)]
        sqb, rsb, o32 = place("sqb", [P, T], at=at), place("rsb", [P, T], at=at), place("o32", [P, T], at=at)
        at = [own]
        bias = place("bias", [P, D_HEADS, 6 * GRID_W], at=at)
        window = place("window", [P, GRID_W], at=at)
        at = [arena + 4 * (16 * T + 4 * D)]
        right = [place(f"right{s}", [P, LEVELS, 2 * CH], at=at) for s in range(2)]
        left = [place(f"left{s}", [P, LEVELS, 2 * CH], at=at) for s in range(2)]
        same_block = place("same_block", [P, 8, CH], at=at)
        z_at = [at[0]]
        soft = place("soft", [P, T], at=at)
        cum = [place(f"cum{s}", [P, T], at=at) for s in range(2)]
        rel = [place(f"rel{s}", [P, 2 * CH], at=at) for s in range(3)]
        q_dec = [place(f"q_dec{s}", [P, 2 * CH], at=at) for s in range(2)]
        start_dec = [place(f"start_dec{s}", [P, 2 * CH], at=at) for s in range(2)]
        k_endT, scores = place("k_endT", [P, CH], at=at), place("scores", [P, CH], at=at)
        state = [place(f"state{s}", [P, C_HV], at=at) for s in range(2)]
        zT = place("zT", [64, T], at=at)
        z_raw = place("z_raw", [P, DT, 64], at=z_at)
        z_hi, z_lo = place("z_hi", [P, DT, 64], f32r, at=z_at), place("z_lo", [P, DT, 64], f32r, at=z_at)
        gate_min = mean
        assert at[0] <= nc.sbuf_usable_end
        at = [arena]
        out_f = place("out_f", [P, DT, LAT], at=at)
        out_tok = place("out_tok", [P, 2, D], at=at)
        assert at[0] <= nc.sbuf_usable_end

        bank = [nc.alloc_psum_tensor(f"bank{b}", [P, NB], f32) for b in range(8)]
        LN_SUM, LN_SQ, MOD_ACC, MOD_T = bank[4], bank[5], bank[6], bank[7]

        def sem(name):
            return ctx.enter_context(nc.semaphore(name))

        loaded = [sem(f"slab_loaded{s}") for s in range(SLOTS)]
        s_hi, s_lo, s_used = sem("slab_hi_ready"), sem("slab_lo_ready"), sem("slab_used")
        s_free = {"act": sem("group_freed_act"), "dve": sem("group_freed_dve")}
        s_cst, s_cond, s_tok, s_rows, s_small, s_bias_in = (sem(n) for n in (
            "consts_in", "cond_in", "tokens_in", "rows_in", "small_in", "bias_in"))
        s_cond_t, s_cond_a, s_cond_v, s_rows_t, s_rows_v, s_tok_t = (sem(n) for n in (
            "cond_transposed", "cond_act", "cond_split", "rows_transposed", "rows_copied", "tokens_transposed"))
        s_mod_row, s_mod_t, s_mod_in, s_coef = (sem(n) for n in (
            "mod_row_copied", "mod_transposed", "mod_evacuated", "coefficients_ready"))
        s_y, s_sum, s_sqd, s_qsum, s_stats, s_mean, s_var, s_rstd, s_cen, s_xn = (sem(n) for n in (
            "residual_added", "sum_added", "squared", "squares_added", "stats_full",
            "mean_ready", "var_ready", "rstd_ready", "centred", "xn_ready"))
        s_hf, s_hhi, s_hlo = sem("h_modulated"), sem("h_hi_ready"), sem("h_lo_ready")
        s_tap1, s_tap2, s_silu, s_gmul, s_ghi, s_glo = (sem(n) for n in (
            "conv_centre_tap", "conv_left_tap", "silu_done", "gated", "g_hi_ready", "g_lo_ready"))
        s_dve, s_act = sem("dve_step"), sem("act_step")
        s_kd, s_window = sem("keys_doubled"), sem("bias_masked")
        s_lam_p, s_lam_d, s_lam_e, s_gains = (sem(n) for n in (
            "lambda_products", "lambda_dots", "lambda_exps", "gains_ready"))
        s_outf, s_outt, s_outv, s_out = sem("out_scaled"), sem("out_transposed"), sem("out_copied"), sem("out_stored")

        att = {}
        for i in (0, 1, 3):
            att[i] = {n: sem(f"{n}_{i}") for n in (
                "qk_ready", "swapped", "score_full", "biased", "context_copied", "negmax", "exped", "p_ready", "p_turned",
                "pt_ready", "pv_full", "o_hi", "o_lo")}
            if i < 2:
                att[i].update({n: sem(f"{n}_{i}") for n in ("squared_h", "ss_full", "rs_ready", "o_normed")})
        att[2] = {n: sem(f"gla_{n}") for n in (
            "zeroed", "tables_in", "z_hi", "z_lo", "z_full", "z_copied", "gate_full", "gate_soft", "gate_min", "cum",
            "rel", "decay", "q_dec", "k_dec", "score_full", "masked", "scores", "turned", "k_endT", "o_full",
            "update_full", "state", "squared", "ss_full", "rs_ready", "o_normed", "o_gated", "o_hi", "o_lo")}

        block = ctx.enter_context(nc.Block())

        ident, swap, ones, heads = (cst[:, c:c + P] for c in (K_ID, K_SWAP, K_ONES, K_HEAD))
        cos, sin = cst[:, K_COS:K_COS + LAT], cst[:, K_SIN:K_SIN + LAT]
        eps_norm, eps_ln, one = (cst[:, K_EPS + c:K_EPS + c + 1] for c in range(3))
        sel = cst[0:4, K_EPS + 3:K_EPS + 5]

        def cols(i, part):
            return slice(CTX, T) if i == DEPTH - 1 and part == "tail" else slice(0, T)

        def segs(c):
            return [s for s in ((0, slice(0, CTX)), (1, slice(CTX, T))) if s[1].start >= c.start]

        def gain(st):
            if st == 0:
                return unit_gb[:, 0, :], unit_gb[:, 1, :]
            i, second = (st - 1) // 2, (st - 1) % 2
            r = R_LAYER * i + (R_LN2G if second else R_LN1G)
            return prm[:, r:r + DT], prm[:, r + DT:r + 2 * DT]

        def mod(st, which):
            return (3 * (st % 2) + which) * DT

        def src(s):
            kind = s[0]
            if kind == "mod":
                _, i, g, q = s
                return a["mod_w"][i, 2 * q * P:(2 * q + 2) * P, g * NB:(g + 1) * NB].rearrange("(k p) c -> p k c", p=P), 2
            if kind == "f":
                _, name, c, k0, nk = s
                return a[name][0, k0 * P:(k0 + nk) * P, c:c + P].rearrange("(k p) c -> p k c", p=P), nk
            if kind == "v":
                _, name, c, q = s
                return a[name][0, 4 * q * P:(4 * q + 4) * P, c:c + 256].rearrange("(k p) c -> p k c", p=P), 4
            if kind == "up":
                _, i, c = s
                return a["ffn_w_up"][i, :, c:c + P].rearrange("(k p) c -> p k c", p=P), 8
            _, i, c, k0, nk = s
            return a["ffn_w_down"][i, k0 * P:(k0 + nk) * P, c:c + P].rearrange("(k p) c -> p k c", p=P), nk

        def width(s):
            return {"mod": SLAB, "v": SLAB, "up": SLAB}.get(s[0]) or s[4] * P

        def mirrored(ap):
            return ap.rearrange("p (r c) -> p r c", c=GRID_W)[:, :, ::-1]

        def attention_units(i):
            n = (A_HEADS, B_HEADS, 0, D_HEADS)[i]
            return [(hd, s, CTX * s + P * b) for hd in range(n) for s in ((1,) if i == 3 else (0, 1)) for b in (0, 1)]

        def rpb_block(dr):
            t = a["d_rpb"]
            return bass.AP(tensor=t.tensor, offset=dr * N_DC + WIN_C - GRID_W,
                           ap=[[1, GRID_W], [N_DR * N_DC, D_HEADS], [1, GRID_W]])

        def item_of(w):
            return w // 4, w // 2 % 2, slice(CTX * (w % 2), CTX * (w % 2) + 2 * CH)

        def chunk_of(c):
            hd, bwd, cols_w = item_of(c // 2)
            p = c % 2 ^ bwd
            return hd, bwd, p, slice(CH * p, CH * p + CH), slice(cols_w.start + CH * p, cols_w.start + CH * p + CH)

        def states(c):
            return 3 * (c // 4) + min(c % 4 + 1, 3)

        def half(ap, l, right_half):
            v = ap.rearrange("p (n h s) -> p n h s", h=2, s=64 >> l)
            return v[:, :, 1 if right_half else 0, :]

        @block.sync
        def _(sp):
            sp.dma_start(cst[:], a["k_const"]).then_inc(s_cst, 16)
            sp.dma_start(cond_row[0:DT, :], a["c_ctx"].rearrange("(k p) -> k p", p=P)).then_inc(s_cond, 16)
            sp.dma_start(cond_row[DT:2 * DT, :], a["c"][0].rearrange("(k p) -> k p", p=P)).then_inc(s_cond, 16)

            def load(n):
                source, nk = src(slabs[n])
                if n >= SLOTS:
                    sp.wait_ge(s_hi, n - SLOTS + 1)
                    sp.wait_ge(s_lo, n - SLOTS + 1)
                dst = raw[n % SLOTS][:, 0:width(slabs[n])].rearrange("p (k c) -> p k c", k=nk)
                sp.dma_start(dst, source).then_inc(loaded[n % SLOTS], 16)

            n = 0
            while n < n_slabs:
                rolled = [i for i in range(layers) if start["up", i][0] == n]
                if not rolled:
                    load(n)
                    n += 1
                    continue
                i = rolled[0]
                per = 8 if i + 1 < layers else 4
                with sp.Fori(0, FT // 2) as it:
                    for c in range(per):
                        s = slabs[n + c]
                        sp.wait_ge(s_hi, n + c - SLOTS + 1 + per * it)
                        sp.wait_ge(s_lo, n + c - SLOTS + 1 + per * it)
                        if s[0] == "up":
                            source = a["ffn_w_up"][i, :, bass.ds(s[2] + 2 * P * it, P)]
                        else:
                            source = a["mod_w"][i + 1, 2 * s[3] * P:(2 * s[3] + 2) * P, bass.ds(NB + NB * it, NB)]
                        nk = 8 if s[0] == "up" else 2
                        sp.dma_start(raw[c % SLOTS][:].rearrange("p (k c) -> p k c", k=nk),
                                     source.rearrange("(k p) c -> p k c", p=P)).then_inc(loaded[c % SLOTS], 16)
                n += per * (FT // 2)
            sp.wait_ge(s_outv, 4)
            sp.dma_start(a["out"][0].rearrange("(t p) d -> p t d", p=P), out_tok[:]).then_inc(s_out, 16)
            sp.wait_ge(s_out, 16)

        @block.scalar
        def _(act):
            step = Count(s_act)
            act.dma_start(small_row[:], a["small"]).then_inc(s_small, 16)
            act.dma_start(rows[:], a["rows"].rearrange("(r p) d -> p r d", p=P)).then_inc(s_rows, 16)
            act.dma_start(tok[:, 0:2, :], a["ctx"][0].rearrange("(t p) d -> p t d", p=P)).then_inc(s_tok, 16)
            act.dma_start(tok[:, 2:4, :], a["x"][0].rearrange("(t p) d -> p t d", p=P)).then_inc(s_tok, 16)

            def split(n, it=0, per=0):
                if n >= n_slabs:
                    return
                slot = n % SLOTS
                act.wait_ge(loaded[slot], 16 * (n // SLOTS + 1) + 16 * (per // SLOTS) * it)
                if n >= SLOTS:
                    act.wait_ge(s_used, n - SLOTS + 1 + per * it)
                w = SLAB if per else width(slabs[n])
                nc.scalar.activation(whi[slot][:, 0:w], raw[slot][:, 0:w], ACT.Copy).then_inc(s_hi, 1)

            def make_h(st, c):
                cf = coef[st % 2]
                for k in range(DT):
                    act.wait_ge(s_xn, DT * st + k + 1)
                    if k == 0:
                        act.wait_ge(s_coef, st + 1)
                    if k >= 2:
                        act.wait_ge(s_hlo, DT * st + k - 1)
                    for s, cc in segs(c):
                        ins = nc.scalar.activation(res_t[k % 2][:, cc], xn[:, k, cc], ACT.Identity,
                                                   bias=cf[:, 2 + s, k:k + 1], scale=cf[:, s, k:k + 1])
                    ins.then_inc(s_hf, 1)
                    act.wait_ge(s_hf, DT * st + k + 1)
                    nc.scalar.activation(h_hi[:, k, c], res_t[k % 2][:, c], ACT.Copy).then_inc(s_hhi, 1)

            def residual(st, n, fg, per, c):
                i = st // 2

                def square(dt):
                    act.wait_ge(s_y, DT * st + dt + 1)
                    if dt >= 2:
                        act.wait_ge(s_qsum, 7 * st + dt - 1)
                    nc.scalar.activation((sq if dt else acc_q)[:, c], xn[:, dt, c], ACT.Square).then_inc(s_sqd, 1)

                for dt in range(DT):
                    for q in range(per):
                        split(n + per * dt + q + AHEAD)
                    if dt:
                        square(dt - 1)
                    act.wait_ge(s_used, n + per * (dt + 1))
                    if dt == 0:
                        act.wait_ge(s_mod_in, i + 2)
                    for s, cc in segs(c):
                        ins = nc.scalar.activation(
                            res_t[dt % 2][:, cc], bank[(fg + dt) % 4][:, cc], ACT.Identity,
                            bias=coef[st % 2][:, 5, dt:dt + 1],
                            scale=modT[i % 2][:, mod(st, 2) + dt, s:s + 1])
                    ins.then_inc(s_free["act"], 1)
                square(DT - 1)
                if st % 2:
                    nc.scalar.preload_act_table_set("natural_log_exp_and_others")
                act.wait_ge(s_var, st + 1)
                step.up(nc.scalar.activation(rstd[:, c], acc_q[:, c], ACT.Ln))
                act.wait_ge(s_act, step.n)
                nc.scalar.activation(rstd[:, c], rstd[:, c], ACT.Exp, scale=-0.5).then_inc(s_rstd, 1)

            def root(dst, of, scale):
                step.up(nc.scalar.activation(dst, of, ACT.Ln, scale=scale, bias=eps_norm))
                act.wait_ge(s_act, step.n)
                return nc.scalar.activation(dst, dst, ACT.Exp, scale=-0.5)

            def qkv_norm_rope(n, fg):
                S = att[0]

                def roots(ft):
                    act.wait_ge(S["ss_full"], ft + 1)
                    if ft >= 2:
                        act.wait_ge(s_free["dve"], ft - 1)
                    root(rsa[ft % 2][:], bank[4][:], 1.0 / HD).then_inc(S["rs_ready"], 1)

                for ft in range(10):
                    split(n + AHEAD)
                    n += 1
                    act.wait_ge(s_used, n)
                    if ft >= 2:
                        act.wait_ge(S["ss_full"], ft - 1)
                    nc.scalar.activation(sqa[ft % 2][:], bank[(fg + ft) % 4][:], ACT.Square).then_inc(S["squared_h"], 1)
                    if ft:
                        roots(ft - 1)
                    if ft < 8:
                        for q in range(4):
                            split(n + AHEAD)
                            n += 1
                roots(9)
                for q in range(2):
                    split(n + AHEAD)
                    n += 1
                act.wait_ge(S["qk_ready"], 10)
                for kt in range(2):
                    for j in range(2):
                        for half in range(2):
                            ins = nc.scalar.activation(kd[HD * half:HD * half + HD, 2 * kt + j, :],
                                                       qk[HD * j:HD * j + HD, 8 + kt, :], ACT.Copy)
                ins.then_inc(s_kd, 1)

            def qkv_plain(i, n, fg):
                S = att[i]
                for ft in range(16):
                    split(n + ft + AHEAD)
                    act.wait_ge(s_used, n + ft + 1)
                    dst, ps = qk[:, ft, :], bank[(fg + ft) % 4]
                    if i == 3 and ft < 8:
                        dst, source = mirrored(dst[:, CTX:T]), ps[:, CTX:T].rearrange("p (r c) -> p r c", c=GRID_W)
                    else:
                        source = ps[:]
                    nc.scalar.activation(dst, source, ACT.Identity,
                                         scale=SCALE if ft < 8 else 1.0).then_inc(s_free["act"], 1)
                for q in range(8):
                    split(n + 16 + q + AHEAD)

            def attention(i):
                S, U = att[i], attention_units(i)
                maps = 2 if i == 1 else 1
                per_o = len(U) // DT

                def copy_context(u):
                    if u < len(U):
                        act.wait_ge(S["biased"], u + 1)
                        nc.scalar.activation(p1[u % 3][:, 0:CTX], bank[u % 4][:, 0:CTX],
                                             ACT.Copy).then_inc(S["context_copied"], 1)

                if i == 3:
                    copy_context(0)
                for u in range(len(U) + 6):
                    if u < len(U):
                        hd, s, q0 = U[u]
                        nk = CTX if s == 0 else T
                        if u >= 3:
                            act.wait_ge(S["p_turned"], u - 2)
                        if i == 3:
                            copy_context(u + 1)
                        for m in range(maps):
                            act.wait_ge(S["negmax"], maps * u + m + 1)
                            b = bank[(2 * u + m) % 4] if maps == 2 else bank[u % 4]
                            dst = (p1, p2)[m][u % 3]
                            source = p1[u % 3] if i == 3 else b
                            nc.scalar.activation(dst[:, 0:nk], source[:, 0:nk], ACT.Exp,
                                                 bias=stat[:, m, u:u + 1],
                                                 accum_out=stat[:, 2 + m, u:u + 1]).then_inc(S["exped"], 1)
                    if 0 <= u - 2 < len(U):
                        w = u - 2
                        hd, s, q0 = U[w]
                        act.wait_ge(S["p_turned"], w + 1)
                        if w >= 4:
                            act.wait_ge(S["pv_full"], w // 2 - 1)
                        kt = 2 if s == 0 else 4
                        pb = bank[4] if i == 1 else bank[4 + w % 2]
                        nc.scalar.activation(pt[w // 2 % 2][:, 0:kt, P * (w % 2):P * (w % 2) + P],
                                             pb[:, 0:kt * P].rearrange("p (k q) -> p k q", k=kt),
                                             ACT.Copy).then_inc(S["pt_ready"], 1)
                    w = u - 5
                    if w >= 0 and w % per_o == per_o - 1:
                        o = w // per_o
                        c = slice(CTX, T) if i == 3 else slice(0, T)
                        act.wait_ge(S["pv_full"], (w + 1) // 2)
                        if i == 1:
                            nc.scalar.activation(sqb[:], bank[6 + o % 2][:], ACT.Square).then_inc(S["squared_h"], 1)
                            act.wait_ge(S["ss_full"], o + 1)
                            root(rsb[:], bank[5][:], 1.0 / (2 * HD)).then_inc(S["rs_ready"], 1)
                            act.wait_ge(S["o_normed"], o + 1)
                            nc.scalar.activation(h_hi[:, o, :], o32[:], ACT.Copy).then_inc(S["o_hi"], 1)
                        elif i == 0:
                            nc.scalar.activation(h_hi[:, o, :], bank[6 + o % 2][:], ACT.Copy).then_inc(S["o_hi"], 1)
                        else:
                            nc.scalar.activation(h_hi[:, o, c].rearrange("p (r c) -> p r c", c=GRID_W),
                                                 mirrored(bank[6 + o % 2][:, c]), ACT.Copy).then_inc(S["o_hi"], 1)

            def gate(S, u):
                b = 16 + C_HEADS * (u % 2) + u // 2
                act.wait_ge(S["gate_full"], u + 1)
                if u:
                    act.wait_ge(S["cum"], u)
                step.up(nc.scalar.activation(soft[:], bank[7][:], ACT.Abs, bias=small[:, b:b + 1]))
                act.wait_ge(s_act, step.n)
                step.up(nc.scalar.activation(soft[:], soft[:], ACT.Exp, scale=-1.0))
                act.wait_ge(s_act, step.n)
                nc.scalar.activation(soft[:], soft[:], ACT.Ln, bias=one).then_inc(S["gate_soft"], 1)

            def gla_tables():
                S = att[2]
                act.wait_ge(S["zeroed"], 1)
                act.dma_start(z_raw[:, :, 0:C_RANK], a["c_w_in"][0, :, 3072:3088].rearrange("(k p) c -> p k c", p=P)
                              ).then_inc(S["tables_in"], 16)
                act.dma_start(z_raw[:, :, 32:32 + C_RANK], a["c_w_in"][0, :, 3088:3104].rearrange("(k p) c -> p k c", p=P)
                              ).then_inc(S["tables_in"], 16)
                act.dma_start(w_gate[0:C_RANK, :], a["c_w_gate_fwd"][0]).then_inc(S["tables_in"], 16)
                act.dma_start(w_gate[32:32 + C_RANK, :], a["c_w_gate_bwd"][0]).then_inc(S["tables_in"], 16)
                act.dma_start(same_block[:], a["k_blocks"]).then_inc(S["tables_in"], 16)

            def qkv_gla(n, fg):
                S = att[2]
                for ft in range(8):
                    split(n + ft + AHEAD)
                    act.wait_ge(s_used, n + ft + 1)
                    nc.scalar.activation(qk[:, ft, :], bank[(fg + ft) % 4][:], ACT.Identity,
                                         scale=CH ** -0.5 if ft < 4 else 1.0).then_inc(s_free["act"], 1)
                    if ft == 3:
                        act.wait_ge(S["tables_in"], 80)
                        nc.scalar.activation(z_hi[:], z_raw[:], ACT.Copy).then_inc(S["z_hi"], 1)
                gate(S, 0)
                nc.scalar.preload_act_table_set("silu_and_others")
                for q in range(8):
                    split(n + 8 + q + AHEAD)
                for ft in range(8):
                    split(n + 16 + ft + AHEAD)
                    act.wait_ge(s_used, n + 16 + ft + 1)
                    nc.scalar.activation(qk[:, 8 + ft, :], bank[(fg + 16 + ft) % 4][:],
                                         ACT.Silu).then_inc(s_free["act"], 1)
                nc.scalar.preload_act_table_set("natural_log_exp_and_others")

            def gla():
                S = att[2]

                def decays(w, l0, l1):
                    hd, bwd, cw = item_of(w)
                    for l in range(l0, l1):
                        act.wait_ge(S["rel"], 8 * w + l + 1)
                        r = rel[(8 * w + l) % 3]
                        if l < LEVELS:
                            for is_q in (1, 0):
                                v = half(r[:], l, is_q ^ bwd)
                                ins = nc.scalar.activation(v, v, ACT.Exp, scale=(1 if is_q else -1) / C_NORMALIZER)
                        else:
                            if w >= 2:
                                act.wait_ge(S["state"], states(2 * w - 3))
                            nc.scalar.activation(r[:], r[:], ACT.Exp, scale=-1 / C_NORMALIZER)
                            ins = nc.scalar.activation(start_dec[w % 2][:], cum[w // 2 % 2][:, cw], ACT.Exp,
                                                       scale=1 / C_NORMALIZER)
                        ins.then_inc(S["decay"], 1)

                def key_end(c):
                    if c % 4 < 3:
                        act.wait_ge(S["turned"], states(c))
                        if c:
                            act.wait_ge(S["update_full"], states(c) - 1)
                        nc.scalar.activation(k_endT[:], bank[6][:, 0:CH], ACT.Copy).then_inc(S["k_endT"], 1)

                decays(0, 0, 8)
                decays(1, 0, 4)
                for w in range(C_ITEMS):
                    if w % 2 == 0 and w // 2 + 1 < C_UNITS:
                        gate(S, w // 2 + 1)
                    key_end(2 * w)
                    if w + 1 < C_ITEMS:
                        decays(w + 1, 4, 8)
                    key_end(2 * w + 1)
                    if w + 2 < C_ITEMS:
                        decays(w + 2, 0, 4)
                    if w % 4 == 3:
                        hd = w // 4
                        act.wait_ge(S["o_full"], 2 * w + 2)
                        if hd:
                            act.wait_ge(S["o_lo"], 2 * hd)
                        for v in range(2):
                            ins = nc.scalar.activation(o_head[v][:], bank[4 + v][:], ACT.Square)
                        ins.then_inc(S["squared"], 1)
                        act.wait_ge(S["ss_full"], hd + 1)
                        root(rstd[:], bank[6][:], 1.0 / C_HV).then_inc(S["rs_ready"], 1)
                        for v in range(2):
                            act.wait_ge(S["o_gated"], 2 * hd + v + 1)
                            nc.scalar.activation(h_hi[:, 2 * hd + v, :], o_head[v][:], ACT.Copy).then_inc(S["o_hi"], 1)

            for n in range(AHEAD):
                split(n)
            act.wait_ge(s_lam_d, 1)
            nc.scalar.activation(small[:, 11:13], bank[5][:, 0:2], ACT.Exp).then_inc(s_lam_e, 1)
            act.wait_ge(s_cond_t, 1)
            nc.scalar.activation(cond[:].rearrange("p s k -> p (s k)"), bank[4][:, 0:16], ACT.Silu).then_inc(s_cond_a, 1)
            act.wait_ge(s_cond_a, 1)
            for s in range(2):
                ins = nc.scalar.activation(cond4[:, :, 2 * s], cond[:, s, :], ACT.Copy)
            ins.then_inc(s_cond_a, 1)
            for n in range(16):
                split(n + AHEAD)
            for i in range(layers):
                st = 2 * i
                nc.scalar.preload_act_table_set("natural_log_exp_and_others")
                make_h(st, cols(i, "head"))
                n, fg = start["qkv", i]
                if i == 0:
                    qkv_norm_rope(n, fg)
                elif i == 2:
                    gla_tables()
                    qkv_gla(n, fg)
                else:
                    if i == 3:
                        for par in range(2):
                            for r in range(6):
                                act.dma_start(bias[64 * par:64 * par + 64, :, GRID_W * r:GRID_W * r + GRID_W],
                                              rpb_block((5, 4)[par] + r)).then_inc(s_bias_in, 16)
                        act.dma_start(window[:], a["k_window"]).then_inc(s_bias_in, 16)
                    qkv_plain(i, n, fg)
                gla() if i == 2 else attention(i)
                n, fg = start["wo", i]
                residual(st, n, fg, 1, cols(i, "tail"))
                make_h(st + 1, cols(i, "tail"))
                nc.scalar.preload_act_table_set("silu_and_others")
                n, fg = start["premod", i]
                c = cols(i, "tail")
                w = c.stop - c.start
                if i + 1 < layers:
                    for q in range(4):
                        split(n + q + AHEAD)
                n, fg = start["up", i]
                per = 8 if i + 1 < layers else 4
                with act.Fori(0, FT // 2) as it:
                    for u in range(2):
                        for k in range(2):
                            at_slab = n + (4 * u + 2 * k if per == 8 else 2 * u + k)
                            split(at_slab + AHEAD, it, per)
                            act.wait_ge(s_used, at_slab + 1 + per * it)
                            tile = FT * k + u + 2 * it
                            nc.scalar.activation(
                                conv[k][u][:, c], bank[2 * u + k][:, c], ACT.Identity,
                                bias=prm[:, bass.ds(R_LAYER * i + R_CB + tile, 1)],
                                scale=prm[:, bass.ds(R_LAYER * i + R_CW + 2 * FT + tile, 1)]).then_inc(s_tap1, 1)
                            if per == 8:
                                split(at_slab + 1 + AHEAD, it, per)
                            if k == 0:
                                act.wait_ge(s_free["dve"], freed[fg][1] + 2 * u + 4 * it)
                                nc.scalar.activation(conv[0][u][:, c], conv[0][u][:, c], ACT.Silu).then_inc(s_silu, 1)
                        act.wait_ge(s_gmul, FT * i + u + 1 + 2 * it)
                        nc.scalar.activation(g_hi[:, bass.ds(u + 2 * it, 1), c], g32[u][:, c].unsqueeze(1),
                                             ACT.Copy).then_inc(s_ghi, 1)
                n, fg = start["down", i]
                residual(st + 1, n, fg, 3, c)
            for k in range(DT):
                act.wait_ge(s_xn, DT * 2 * layers + k + 1)
                g, b = gain(2 * layers)
                nc.scalar.activation(out_f[:, k, :], xn[:, k, CTX:T], ACT.Identity, bias=b[:, k:k + 1],
                                     scale=g[:, k:k + 1]).then_inc(s_outf, 1)

        @block.vector
        def _(dve):
            step = Count(s_dve)

            def link(ins):
                step.up(ins)
                dve.wait_ge(s_dve, step.n)

            def split(n, it=0, per=0):
                if n >= n_slabs:
                    return
                slot = n % SLOTS
                dve.wait_ge(s_hi, n + 1 + per * it)
                w = SLAB if per else width(slabs[n])
                nc.vector.tensor_tensor(wlo[slot][:, 0:w], raw[slot][:, 0:w], whi[slot][:, 0:w].bitcast(f32),
                                        ALU.subtract).then_inc(s_lo, 1)

            def mod_row_copy(group, n):
                dve.wait_ge(s_used, n + 1)
                if group:
                    dve.wait_ge(s_mod_t, group)
                nc.vector.tensor_copy(mod_row[:], MOD_ACC[0:4, :]).then_inc(s_mod_row, 1)

            def mod_evacuate(i, c0, c1, turned):
                dve.wait_ge(s_mod_t, turned)
                v = MOD_T[:, 0:N_MOD * DT * 2].rearrange("p (c s) -> p c s", s=2)
                for s in range(2):
                    ins = nc.vector.tensor_tensor(modT[i % 2][:, c0:c1, s], v[:, c0:c1, s],
                                                  prm[:, R_LAYER * i + c0:R_LAYER * i + c1], ALU.add)
                ins.then_inc(s_mod_in, 1)

            def coefficients(st, events):
                dve.wait_ge(s_mod_in, events)
                cf, m = coef[st % 2], modT[st // 2 % 2]
                g, b = gain(st)
                sh, sc = mod(st, 0), mod(st, 1)
                for s in range(2):
                    nc.vector.scalar_tensor_tensor(cf[:, s, :], m[:, sc:sc + DT, s], 1.0, g, ALU.add, ALU.mult)
                    ins = nc.vector.scalar_tensor_tensor(cf[:, 2 + s, :], m[:, sc:sc + DT, s], 1.0, b, ALU.add, ALU.mult)
                link(ins)
                nc.vector.tensor_scalar(cf[:, 4, :], g, ALPHA, None, ALU.mult)
                nc.vector.tensor_scalar(cf[:, 5, :], b, ALPHA, None, ALU.mult)
                for s in range(2):
                    ins = nc.vector.tensor_tensor(cf[:, 2 + s, :], cf[:, 2 + s, :], m[:, sh:sh + DT, s], ALU.add)
                ins.then_inc(s_coef, 1)

            def scale_xn(st, k, c):
                dve.wait_ge(s_cen, DT * (st - 1) + k + 1)
                if k == 0:
                    dve.wait_ge(s_rstd, st)
                nc.vector.tensor_tensor(xn[:, k, c], xn[:, k, c], rstd[:, c], ALU.mult).then_inc(s_xn, 1)

            def make_h(st, c):
                if st:
                    scale_xn(st, 0, c)
                for k in range(DT):
                    if st and k + 1 < DT:
                        scale_xn(st, k + 1, c)
                    dve.wait_ge(s_hhi, DT * st + k + 1)
                    nc.vector.tensor_tensor(h_lo[:, k, c], res_t[k % 2][:, c], h_hi[:, k, c].bitcast(f32),
                                            ALU.subtract).then_inc(s_hlo, 1)

            def residual(st, n, fg, per, c):

                def add_square(dt):
                    dve.wait_ge(s_sqd, DT * st + dt + 1)
                    if dt >= 2:
                        dve.wait_ge(s_qsum, 7 * st + dt - 1)
                    nc.vector.tensor_tensor(acc_q[:, c], acc_q[:, c], sq[:, c], ALU.add).then_inc(s_qsum, 1)

                for dt in range(DT):
                    for q in range(per):
                        split(n + per * dt + q + AHEAD)
                    dve.wait_ge(s_free["act"], freed[fg + dt][1])
                    nc.vector.scalar_tensor_tensor(xn[:, dt, c], xn[:, dt, c], coef[st % 2][:, 4, dt:dt + 1],
                                                   res_t[dt % 2][:, c], ALU.mult, ALU.add).then_inc(s_y, 1)
                    if dt >= 2:
                        add_square(dt - 1)
                add_square(DT - 1)
                dve.wait_ge(s_stats, st + 1)
                nc.vector.tensor_scalar(mean[:, c], LN_SUM[:, c], 1.0 / D, None, ALU.mult).then_inc(s_mean, 1)
                dve.wait_ge(s_mean, st + 1)
                link(nc.vector.scalar_tensor_tensor(acc_s[:, c], mean[:, c], -1.0, mean[:, c], ALU.mult, ALU.mult))
                link(nc.vector.scalar_tensor_tensor(acc_q[:, c], LN_SQ[:, c], 1.0 / D, acc_s[:, c], ALU.mult, ALU.add))
                nc.vector.tensor_scalar(acc_q[:, c], acc_q[:, c], 0.0, LN_EPS, ALU.max, ALU.add).then_inc(s_var, 1)

            def v_out(n, fg, groups):
                for g in range(groups):
                    for q in range(2):
                        split(n + 2 * g + q + AHEAD)
                    dve.wait_ge(s_used, n + 2 * g + 2)
                    for half in range(2):
                        nc.vector.tensor_copy(v_tok[:, 2 * half:2 * half + 2, 256 * g:256 * g + 256],
                                              bank[(fg + 2 * g + half) % 4][:].rearrange("p (t c) -> p t c", t=2)
                                              ).then_inc(s_free["dve"], 1)

            def rope(S, ft, ps, tmp):
                dve.wait_ge(S["swapped"], ft + 1)
                if ft:
                    dve.wait_ge(S["qk_ready"], ft)
                nc.vector.tensor_tensor(tmp[:], ps, sin, ALU.mult)
                link(nc.vector.tensor_tensor(qk[:, ft, CTX:T], qk[:, ft, CTX:T], cos, ALU.mult))
                nc.vector.tensor_tensor(qk[:, ft, CTX:T], qk[:, ft, CTX:T], tmp[:], ALU.add).then_inc(S["qk_ready"], 1)

            def qkv_norm_rope(n, fg):
                S = att[0]

                def norm(ft):
                    dve.wait_ge(S["rs_ready"], ft + 1)
                    nc.vector.scalar_tensor_tensor(qk[:, ft, :], bank[(fg + ft) % 4][:],
                                                   small[:, 14:15] if ft < 8 else small[:, 1:2],
                                                   rsa[ft % 2][:], ALU.mult, ALU.mult).then_inc(s_free["dve"], 1)

                for ft in range(10):
                    split(n + AHEAD)
                    n += 1
                    if ft >= 1:
                        norm(ft - 1)
                    if ft >= 2:
                        rope(S, ft - 2, bank[5][:, 0:LAT], rope_t)
                    if ft < 8:
                        for q in range(4):
                            split(n + AHEAD)
                            n += 1
                        mod_row_copy(4 + ft, n - 1)
                norm(9)
                mod_evacuate(0, 16, 48, 12)
                rope(S, 8, bank[5][:, 0:LAT], rope_t)
                rope(S, 9, bank[5][:, 0:LAT], rope_t)
                v_out(n, fg + 10, 1)

            def qkv_plain(i, n, fg):
                S = att[i]
                for ft in range(16):
                    split(n + ft + AHEAD)
                    if i == 1 and ft >= 1:
                        rope(S, ft - 1, bank[4 + (ft - 1) % 2][:, 0:LAT], rope_b)
                if i == 1:
                    rope(S, 15, bank[5][:, 0:LAT], rope_b)
                v_out(n + 16, fg + 16, 4)

            def attention(i):
                S, U = att[i], attention_units(i)
                maps = 2 if i == 1 else 1
                per_o = len(U) // DT

                def add_bias(u):
                    if u < len(U):
                        hd, s, q0 = U[u]
                        dve.wait_ge(S["score_full"], u + 1)
                        if u >= 3:
                            dve.wait_ge(S["p_turned"], u - 2)
                        r = 2 * GRID_W if q0 == CTX else 0
                        nc.vector.tensor_tensor(p1[u % 3][:, CTX:T], bank[u % 4][:, CTX:T],
                                                bias[:, hd, r:r + LAT], ALU.add).then_inc(S["biased"], 1)

                if i == 3:
                    add_bias(0)
                for u in range(len(U) + 6):
                    if u < len(U):
                        hd, s, q0 = U[u]
                        nk = CTX if s == 0 else T
                        if i == 3:
                            add_bias(u + 1)
                            dve.wait_ge(S["biased"], u + 1)
                            dve.wait_ge(S["context_copied"], u + 1)
                            nc.vector.tensor_reduce(stat[:, 0, u:u + 1], p1[u % 3][:], AX, ALU.max,
                                                    negate=True).then_inc(S["negmax"], 1)
                        else:
                            for m in range(maps):
                                dve.wait_ge(S["score_full"], maps * u + m + 1)
                                b = bank[(2 * u + m) % 4] if maps == 2 else bank[u % 4]
                                nc.vector.tensor_reduce(stat[:, m, u:u + 1], b[:, 0:nk], AX, ALU.max,
                                                        negate=True).then_inc(S["negmax"], 1)
                    w = u - 1
                    if 0 <= w < len(U):
                        nk = CTX if U[w][1] == 0 else T
                        dve.wait_ge(S["exped"], maps * (w + 1))
                        for m in range(maps):
                            ins = nc.vector.reciprocal(stat[:, 4 + m, w:w + 1], stat[:, 2 + m, w:w + 1])
                        link(ins)
                        r1 = stat[:, 4, w:w + 1]
                        if maps == 1:
                            nc.vector.tensor_scalar(p1[w % 3][:, 0:nk], p1[w % 3][:, 0:nk], r1, None,
                                                    ALU.mult).then_inc(S["p_ready"], 1)
                        else:
                            nc.vector.tensor_scalar(p1[w % 3][:, 0:nk], p1[w % 3][:, 0:nk], r1, None, ALU.mult)
                            link(nc.vector.tensor_tensor(stat[:, 5, w:w + 1], stat[:, 5, w:w + 1], small[:, 13:14],
                                                         ALU.mult))
                            nc.vector.scalar_tensor_tensor(p1[w % 3][:, 0:nk], p2[w % 3][:, 0:nk],
                                                           stat[:, 5, w:w + 1], p1[w % 3][:, 0:nk],
                                                           ALU.mult, ALU.add).then_inc(S["p_ready"], 1)
                    w = u - 5
                    if w >= 0 and w % per_o == per_o - 1:
                        o = w // per_o
                        c = slice(CTX, T) if i == 3 else slice(0, T)
                        if i == 1:
                            dve.wait_ge(S["rs_ready"], o + 1)
                            if o:
                                dve.wait_ge(S["o_lo"], o)
                            nc.vector.scalar_tensor_tensor(o32[:], bank[6 + o % 2][:], small[:, 15:16], rsb[:],
                                                           ALU.mult, ALU.mult).then_inc(S["o_normed"], 1)
                        dve.wait_ge(S["o_hi"], o + 1)
                        lo, source, hi = h_lo[:, o, c], (o32 if i == 1 else bank[6 + o % 2])[:, c], h_hi[:, o, c].bitcast(f32)
                        if i == 3:
                            rows_of = "p (r c) -> p r c"
                            lo, source, hi = lo.rearrange(rows_of, c=GRID_W), mirrored(source), hi.rearrange(rows_of, c=GRID_W)
                        nc.vector.tensor_tensor(lo, source, hi, ALU.subtract).then_inc(S["o_lo"], 1)

            def gate(S, u):
                b, bwd = 16 + C_HEADS * (u % 2) + u // 2, u % 2
                dve.wait_ge(S["gate_soft"], u + 1)
                nc.vector.tensor_scalar(gate_min[:], bank[7][:], small[:, b:b + 1], 0.0, ALU.add,
                                        ALU.min).then_inc(S["gate_min"], 1)
                dve.wait_ge(S["gate_min"], u + 1)
                link(nc.vector.tensor_tensor(gate_min[:], gate_min[:], soft[:], ALU.subtract))
                for c in range(4):
                    v = slice(CH * c, CH * c + CH)
                    src_c, dst_c = gate_min[:, v], cum[u % 2][:, v]
                    if bwd:
                        src_c, dst_c = src_c[:, ::-1], dst_c[:, ::-1]
                    ins = nc.vector.tensor_tensor_scan(dst_c, ones, src_c, 0.0, ALU.mult, ALU.add)
                ins.then_inc(S["cum"], 1)

            def qkv_gla(n, fg):
                S = att[2]
                for ft in range(8):
                    split(n + ft + AHEAD)
                    if ft == 3:
                        dve.wait_ge(S["z_hi"], 1)
                        nc.vector.tensor_tensor(z_lo[:], z_raw[:], z_hi[:].bitcast(f32), ALU.subtract).then_inc(S["z_lo"], 1)
                dve.wait_ge(S["z_full"], 1)
                nc.vector.tensor_copy(zT[:], bank[4][0:64, :]).then_inc(S["z_copied"], 1)
                gate(S, 0)
                v_out(n + 8, fg + 8, 4)
                for ft in range(8):
                    split(n + 16 + ft + AHEAD)

            def gla():
                S = att[2]

                def relative(w, l):
                    hd, bwd, cw = item_of(w)
                    j = 8 * w + l
                    if j >= 3:
                        dve.wait_ge(S["k_dec"], j - 2)
                        dve.wait_ge(S["q_dec"], j - 2)
                    s = 64 >> min(l, 6)
                    n2 = 2 * s if l < LEVELS else CH
                    ref = (s if bwd else s - 1) if l < LEVELS else (0 if bwd else CH - 1)
                    v = cum[w // 2 % 2][:, cw].rearrange("p (n s) -> p n s", s=n2)
                    nc.vector.tensor_tensor(rel[j % 3][:].rearrange("p (n s) -> p n s", s=n2), v,
                                            v[:, :, ref:ref + 1].broadcast_to([P, 2 * CH // n2, n2]),
                                            ALU.subtract).then_inc(S["rel"], 1)

                def query(w, l):
                    hd, bwd, cw = item_of(w)
                    j = 8 * w + l
                    dve.wait_ge(S["decay"], j + 1)
                    if l < LEVELS:
                        if l == 0 and w >= 2:
                            dve.wait_ge(S["score_full"], 2 * w - 2)
                        dst = (left if bwd else right)[w % 2][:, l, :]
                        nc.vector.tensor_tensor(half(dst, l, not bwd), half(qk[:, hd, cw], l, not bwd),
                                                half(rel[j % 3][:], l, not bwd), ALU.mult).then_inc(S["q_dec"], 1)
                    else:
                        if w >= 2:
                            dve.wait_ge(S["o_full"], 2 * w - 2)
                        nc.vector.tensor_tensor(q_dec[w % 2][:], qk[:, hd, cw], start_dec[w % 2][:],
                                                ALU.mult).then_inc(S["q_dec"], 1)

                def build(w, l0, l1):
                    if w % 2 == 0 and l0 == 0:
                        dve.wait_ge(S["cum"], w // 2 + 1)
                    relative(w, l0)
                    for l in range(l0, l1):
                        if l + 1 < l1:
                            relative(w, l + 1)
                        query(w, l)

                def add_levels(c):
                    dve.wait_ge(S["score_full"], c + 1)
                    if c >= 2:
                        dve.wait_ge(S["scores"], c - 1)
                    for h in range(2):
                        v = slice(4 * h, 4 * h + 4)
                        ins = nc.vector.tensor_tensor(masked[c % 2][:, v, :],
                                                      bank[2 * (c % 2) + h][:].rearrange("p (l i) -> p l i", l=4),
                                                      same_block[:, v, :], ALU.mult)
                    ins.then_inc(S["masked"], 1)
                    dve.wait_ge(S["masked"], c + 1)
                    if c:
                        dve.wait_ge(S["o_full"], c)
                    nc.vector.tensor_reduce(scores[:], masked[c % 2][:].rearrange("p l i -> p i l"), AX,
                                            ALU.add).then_inc(S["scores"], 1)

                def next_state(c):
                    if c % 4 == 3:
                        return
                    hd, bwd, p, ci, cs = chunk_of(c)
                    dve.wait_ge(S["update_full"], states(c))
                    if c % 4 == 0:
                        nc.vector.tensor_copy(state[0][:], bank[7][:, 0:C_HV]).then_inc(S["state"], 1)
                    else:
                        dve.wait_ge(S["state"], states(c) - 1)
                        end = ci.start if bwd else ci.stop - 1
                        nc.vector.scalar_tensor_tensor(state[c % 4 % 2][:], state[(c % 4 - 1) % 2][:],
                                                       start_dec[c // 2 % 2][:, end:end + 1], bank[7][:, 0:C_HV],
                                                       ALU.mult, ALU.add).then_inc(S["state"], 1)

                dve.wait_ge(s_free["act"], freed[start["qkv", 2][1] + 7][1])
                dve.wait_ge(S["zeroed"], 2)
                build(0, 0, 8)
                build(1, 0, 4)
                for w in range(C_ITEMS):
                    if w % 2 == 0 and w // 2 + 1 < C_UNITS:
                        gate(S, w // 2 + 1)
                    add_levels(2 * w)
                    if w + 1 < C_ITEMS:
                        build(w + 1, 4, 8)
                    next_state(2 * w)
                    add_levels(2 * w + 1)
                    if w + 2 < C_ITEMS:
                        build(w + 2, 0, 4)
                    next_state(2 * w + 1)
                    if w % 4 == 3:
                        hd = w // 4
                        dve.wait_ge(S["rs_ready"], hd + 1)
                        for v in range(2):
                            nc.vector.scalar_tensor_tensor(o_head[v][:], bank[4 + v][:], small[:, 3 + v:4 + v], rstd[:],
                                                           ALU.mult, ALU.mult).then_inc(S["o_normed"], 1)
                        for v in range(2):
                            dve.wait_ge(S["o_normed"], 2 * hd + v + 1)
                            nc.vector.tensor_tensor(o_head[v][:], o_head[v][:], qk[:, 8 + 2 * hd + v, :],
                                                    ALU.mult).then_inc(S["o_gated"], 1)
                        for v in range(2):
                            dve.wait_ge(S["o_hi"], 2 * hd + v + 1)
                            nc.vector.tensor_tensor(h_lo[:, 2 * hd + v, :], o_head[v][:],
                                                    h_hi[:, 2 * hd + v, :].bitcast(f32), ALU.subtract).then_inc(S["o_lo"], 1)

            nc.vector.memset(unit_gb[:, 0, :], 1.0)
            link(nc.vector.memset(unit_gb[:, 1, :], 0.0))
            dve.wait_ge(s_cond_t, 2)
            link(nc.vector.tensor_copy(small[:], bank[5][:, 0:32]))
            nc.vector.tensor_tensor(small[0:HD, 9:10], small[0:HD, 5:6], small[0:HD, 6:7], ALU.mult)
            nc.vector.tensor_tensor(small[0:HD, 10:11], small[0:HD, 7:8], small[0:HD, 8:9], ALU.mult).then_inc(s_lam_p, 1)
            nc.vector.tensor_scalar(small[:, 14:15], small[:, 0:1], SCALE, None, ALU.mult)
            link(nc.vector.tensor_scalar(small[:, 15:16], small[:, 2:3], 1.0 - LAM_INIT, None, ALU.mult))
            dve.wait_ge(s_lam_e, 1)
            link(nc.vector.tensor_tensor(small[:, 13:14], small[:, 12:13], small[:, 11:12], ALU.subtract))
            link(nc.vector.tensor_scalar(small[:, 13:14], small[:, 13:14], LAM_INIT, None, ALU.subtract))
            for n in range(AHEAD):
                split(n)
            dve.wait_ge(s_cond_a, 2)
            for s in range(2):
                ins = nc.vector.tensor_tensor(cond4[:, :, 2 * s + 1], cond[:, s, :],
                                              cond4[:, :, 2 * s].bitcast(f32), ALU.subtract)
            ins.then_inc(s_cond_v, 1)
            for b in range(2):
                dve.wait_ge(s_rows_t, b + 1)
                nc.vector.tensor_copy(prm[:, NB * b:NB * b + NB], bank[2 + b][:]).then_inc(s_rows_v, 1)
            dve.wait_ge(s_rows_v, 2)
            for k in range(DT):
                dve.wait_ge(s_tok_t, k + 1)
                nc.vector.tensor_copy(xn[:, k, :], bank[k % 2][:]).then_inc(s_xn, 1)
            for g in range(4):
                for q in range(4):
                    split(4 * g + q + AHEAD)
                mod_row_copy(g, 4 * g + 3)
            mod_evacuate(0, 0, 16, 4)
            for i in range(layers):
                st = 2 * i
                coefficients(st, 1 if i == 0 else i + 2)
                make_h(st, cols(i, "head"))
                n, fg = start["qkv", i]
                if i == 0:
                    qkv_norm_rope(n, fg)
                elif i == 2:
                    qkv_gla(n, fg)
                else:
                    qkv_plain(i, n, fg)
                gla() if i == 2 else attention(i)
                n, fg = start["wo", i]
                c = cols(i, "tail")
                residual(st, n, fg, 1, c)
                coefficients(st + 1, i + 2)
                make_h(st + 1, c)
                n, fg = start["premod", i]
                if i + 1 < layers:
                    for q in range(4):
                        split(n + q + AHEAD)
                    mod_row_copy(12 * (i + 1), n + 3)
                n, fg = start["up", i]
                per = 8 if i + 1 < layers else 4
                base = freed[fg][1] - 1
                with dve.Fori(0, FT // 2) as it:
                    for u in range(2):
                        for k in range(2):
                            at_slab = n + (4 * u + 2 * k if per == 8 else 2 * u + k)
                            split(at_slab + AHEAD, it, per)
                            group = 2 * u + k
                            dve.wait_ge(s_tap1, 2 * FT * i + group + 1 + 4 * it)
                            w = R_LAYER * i + R_CW + FT * k + u + 2 * it
                            runs = "p (s t) -> p s t"
                            ps = bank[group][:, c].rearrange(runs, t=LAT)
                            dst = conv[k][u][:, c].rearrange(runs, t=LAT)
                            nc.vector.scalar_tensor_tensor(dst[:, :, 1:LAT], ps[:, :, 0:LAT - 1], prm[:, bass.ds(w, 1)],
                                                           dst[:, :, 1:LAT], ALU.mult, ALU.add).then_inc(s_tap2, 1)
                            dve.wait_ge(s_tap2, 2 * FT * i + group + 1 + 4 * it)
                            nc.vector.scalar_tensor_tensor(dst[:, :, 0:LAT - 1], ps[:, :, 1:LAT],
                                                           prm[:, bass.ds(4 * FT + w, 1)],
                                                           dst[:, :, 0:LAT - 1], ALU.mult, ALU.add).then_inc(s_free["dve"], 1)
                            if per == 8:
                                split(at_slab + 1 + AHEAD, it, per)
                        dve.wait_ge(s_ghi, FT * i + u + 1 + 2 * it)
                        nc.vector.tensor_tensor(g_lo[:, bass.ds(u + 2 * it, 1), c], g32[u][:, c].unsqueeze(1),
                                                g_hi[:, bass.ds(u + 2 * it, 1), c].bitcast(f32),
                                                ALU.subtract).then_inc(s_glo, 1)
                    if per == 8:
                        group = 12 * (i + 1) + 1
                        dve.wait_ge(s_used, n + per + per * it)
                        dve.wait_ge(s_mod_t, group + it)
                        nc.vector.tensor_copy(mod_row[:], MOD_ACC[0:4, :]).then_inc(s_mod_row, 1)
                if i + 1 < layers:
                    mod_evacuate(i + 1, 0, N_MOD * DT, 12 * (i + 2))
                n, fg = start["down", i]
                residual(st + 1, n, fg, 3, c)
            for k in range(DT):
                scale_xn(2 * layers, k, slice(CTX, T))
            for q in range(4):
                dve.wait_ge(s_outt, q + 1)
                nc.vector.tensor_copy(out_tok[:, q // 2, NB * (q % 2):NB * (q % 2) + NB], bank[q][:]).then_inc(s_outv, 1)

        @block.gpsimd
        def _(pool):
            def residual(st, c):
                for dt in range(DT):
                    pool.wait_ge(s_y, DT * st + dt + 1)
                    if dt == 0:
                        nc.gpsimd.tensor_copy(acc_s[:, c], xn[:, 0, c]).then_inc(s_sum, 1)
                    else:
                        pool.wait_ge(s_sum, DT * st + dt)
                        nc.gpsimd.tensor_tensor(acc_s[:, c], acc_s[:, c], xn[:, dt, c], ALU.add).then_inc(s_sum, 1)
                pool.wait_ge(s_mean, st + 1)
                for k in range(DT):
                    nc.gpsimd.tensor_tensor(xn[:, k, c], xn[:, k, c], mean[:, c], ALU.subtract).then_inc(s_cen, 1)

            def gla():
                S = att[2]
                nc.gpsimd.memset(z_raw[:], 0.0).then_inc(S["zeroed"], 1)
                for s in range(2):
                    nc.gpsimd.memset(right[s][:], 0.0)
                    ins = nc.gpsimd.memset(left[s][:], 0.0)
                ins.then_inc(S["zeroed"], 1)
                pool.wait_ge(S["zeroed"], 2)
                pool.wait_ge(s_free["act"], freed[start["qkv", 2][1] + 7][1])
                for w in range(C_ITEMS):
                    hd, bwd, cw = item_of(w)
                    for l in range(8):
                        j = 8 * w + l
                        pool.wait_ge(S["decay"], j + 1)
                        if l < LEVELS:
                            if l == 0 and w >= 2:
                                pool.wait_ge(S["score_full"], 2 * w - 2)
                            dst = (right if bwd else left)[w % 2][:, l, :]
                            nc.gpsimd.tensor_tensor(half(dst, l, bwd), half(qk[:, 4 + hd, cw], l, bwd),
                                                    half(rel[j % 3][:], l, bwd), ALU.mult).then_inc(S["k_dec"], 1)
                        else:
                            if w >= 2:
                                pool.wait_ge(S["turned"], states(2 * w - 3))
                            nc.gpsimd.tensor_tensor(k_end[w % 2][:], qk[:, 4 + hd, cw], rel[j % 3][:],
                                                    ALU.mult).then_inc(S["k_dec"], 1)

            for i in range(layers):
                c = cols(i, "tail")
                if i == 2:
                    gla()
                if i == 3:
                    pool.wait_ge(s_bias_in, 16 * 13)
                    v = bias[:].rearrange("p h (r c) -> p (h r) c", c=GRID_W)
                    nc.gpsimd.tensor_tensor(v, v, window[:].unsqueeze(1).broadcast_to([P, 6 * D_HEADS, GRID_W]),
                                            ALU.add).then_inc(s_window, 1)
                residual(2 * i, c)
                n, fg = start["up", i]
                with pool.Fori(0, FT // 2) as it:
                    for u in range(2):
                        pool.wait_ge(s_silu, FT * i + u + 1 + 2 * it)
                        pool.wait_ge(s_free["dve"], freed[fg][1] + 2 * u + 1 + 4 * it)
                        nc.gpsimd.tensor_tensor(g32[u][:, c], conv[0][u][:, c], conv[1][u][:, c],
                                                ALU.mult).then_inc(s_gmul, 1)
                residual(2 * i + 1, c)

        @block.tensor
        def _(pe):
            mm = nc.tensor.matmul

            def three(out, w_hi, w_lo, x_hi, x_lo, first, last, moving_w=False):
                for n, (w, x) in enumerate(((w_hi, x_hi), (w_hi, x_lo), (w_lo, x_hi))):
                    l, r = (x, w) if moving_w else (w, x)
                    ins = mm(out, l, r, start=first and n == 0, stop=last and n == 2)
                return ins

            def split_ready(n, it=0, per=0):
                pe.wait_ge(s_hi, n + 1 + per * it)
                pe.wait_ge(s_lo, n + 1 + per * it)

            def project(n, out, x_hi, x_lo, c, k0=0, nk=8, first=True, last=True, ready=None, it=0, per=0):
                split_ready(n, it, per)
                slot = n % SLOTS
                for k in range(nk):
                    if ready:
                        pe.wait_ge(ready[0], ready[1] + k0 + k + 1)
                    wc = slice(k * P, (k + 1) * P)
                    ins = three(out[:, c], whi[slot][:, wc], wlo[slot][:, wc], x_hi[:, k0 + k, c], x_lo[:, k0 + k, c],
                                first and k == 0, last and k == nk - 1)
                ins.then_inc(s_used, 1)

            def group_free(fg):
                if fg >= 4:
                    who, count = freed[fg - 4]
                    pe.wait_ge(s_free[who], count)

            def mod_slab(n, group, q, it=0, per=0):
                split_ready(n, it, per)
                if q == 0 and group:
                    pe.wait_ge(s_mod_row, group + it)
                slot = n % SLOTS
                for k in range(2):
                    for part, w in enumerate((whi, wlo)):
                        ins = mm(MOD_ACC[0:4, :], cond4[:, 2 * q + k, :], w[slot][:, NB * k:NB * k + NB],
                                 start=q == 0 and k == 0 and part == 0, stop=q == 3 and k == 1 and part == 1)
                ins.then_inc(s_used, 1)

            def mod_turn(group, it=0):
                pe.wait_ge(s_mod_row, group + 1 + it)
                g = group % 12
                if group == 4:
                    pe.wait_ge(s_mod_in, 1)
                elif group >= 12 and g == 0:
                    pe.wait_ge(s_mod_in, group // 12 + 1)
                for b in range(4):
                    ins = mm(MOD_T[:, bass.ds(8 * g + 2 * b + 8 * it, 2)], mod_row[:, b * P:(b + 1) * P], sel,
                             start=True, stop=True)
                ins.then_inc(s_mod_t, 1)

            def stats(st, c):
                pe.wait_ge(s_sum, DT * (st + 1))
                mm(LN_SUM[:, c], ones, acc_s[:, c], start=True, stop=True)
                pe.wait_ge(s_qsum, 7 * (st + 1))
                mm(LN_SQ[:, c], ones, acc_q[:, c], start=True, stop=True).then_inc(s_stats, 1)

            def v_project(n, fg, groups):
                for g in range(groups):
                    split_ready(n + 1)
                    for tt in range(4):
                        if tt % 2 == 0:
                            group_free(fg + tt // 2)
                        out = bank[(fg + tt // 2) % 4][:, 256 * (tt % 2):256 * (tt % 2) + 256]
                        for k in range(DT):
                            slot, wc = (n + k // 4) % SLOTS, slice(256 * (k % 4), 256 * (k % 4) + 256)
                            tc = slice(tt * P, tt * P + P)
                            ins = three(out, whi[slot][:, wc], wlo[slot][:, wc], h_hi[:, k, tc], h_lo[:, k, tc],
                                        k == 0, k == DT - 1, moving_w=True)
                            if tt == 3 and k % 4 == 3:
                                ins.then_inc(s_used, 1)
                    n, fg = n + 2, fg + 2

            def swapped(S, ft, ps):
                mm(ps, swap, qk[:, ft, CTX:T], start=True, stop=True).then_inc(S["swapped"], 1)

            def qkv_norm_rope(n, fg):
                S = att[0]

                def squares(ft):
                    pe.wait_ge(S["squared_h"], ft + 1)
                    if ft:
                        pe.wait_ge(S["rs_ready"], ft)
                    mm(bank[4][:], heads, sqa[ft % 2][:], start=True, stop=True).then_inc(S["ss_full"], 1)

                def turn(ft):
                    pe.wait_ge(s_free["dve"], freed[fg + ft][1])
                    if ft:
                        pe.wait_ge(S["qk_ready"], ft)
                    swapped(S, ft, bank[5][:, 0:LAT])

                for ft in range(10):
                    group_free(fg + ft)
                    project(n, bank[(fg + ft) % 4], h_hi, h_lo, slice(0, T), ready=(s_hlo, 0) if ft == 0 else None)
                    n += 1
                    if ft:
                        squares(ft - 1)
                    if ft >= 2:
                        turn(ft - 2)
                    if ft < 8:
                        for q in range(4):
                            mod_slab(n, 4 + ft, q)
                            n += 1
                    if ft < 8:
                        mod_turn(4 + ft)
                squares(9)
                turn(8)
                turn(9)
                v_project(n, fg + 10, 1)

            def qkv_plain(i, n, fg):
                S = att[i]
                for ft in range(16):
                    c = slice(CTX, T) if i == 3 and ft < 8 else slice(0, T)
                    group_free(fg + ft)
                    project(n + ft, bank[(fg + ft) % 4], h_hi, h_lo, c,
                            ready=(s_hlo, 2 * i * DT) if ft == 0 else None)
                    if i == 1 and ft:
                        turn(S, ft - 1, fg)
                if i == 1:
                    turn(S, 15, fg)
                v_project(n + 16, fg + 16, 4)

            def turn(S, ft, fg):
                pe.wait_ge(s_free["act"], freed[fg + ft][1])
                if ft >= 2:
                    pe.wait_ge(S["qk_ready"], ft - 1)
                swapped(S, ft, bank[4 + ft % 2][:, 0:LAT])

            def attention(i):
                S, U = att[i], attention_units(i)
                maps = 2 if i == 1 else 1
                per_o = len(U) // DT
                c = slice(CTX, T) if i == 3 else slice(0, T)
                if i == 3:
                    n_last = freed[start["wo", i][1] - 9]
                    pe.wait_ge(s_free["act"], n_last[1])
                    pe.wait_ge(s_window, 1)
                else:
                    pe.wait_ge(S["qk_ready"], 10 if i == 0 else 16)
                if i == 0:
                    pe.wait_ge(s_kd, 1)
                pe.wait_ge(s_free["dve"], freed[start["wo", i][1] - 1][1])
                for u in range(len(U) + 6):
                    w = u - 6
                    if i == 1 and w >= 0 and w % per_o == per_o - 1:
                        o = w // per_o
                        pe.wait_ge(S["squared_h"], o + 1)
                        mm(bank[5][:], ones, sqb[:], start=True, stop=True).then_inc(S["ss_full"], 1)
                    if u < len(U):
                        hd, s, q0 = U[u]
                        nk = CTX if s == 0 else T
                        if maps == 1 and u >= 4:
                            pe.wait_ge(S["exped"], u - 3)
                        if maps == 2 and u >= 2:
                            pe.wait_ge(S["exped"], 2 * (u - 1))
                        for m in range(maps):
                            if i == 1:
                                r, qt, b = slice(HD * m, HD * m + HD), hd, bank[(2 * u + m) % 4]
                                keys = qk[r, 8 + hd, 0:nk]
                            else:
                                r, qt, b = slice(HD * (hd % 2), HD * (hd % 2) + HD), hd // 2, bank[u % 4]
                                keys = kd[r, hd // (A_HEADS // A_KV), 0:nk] if i == 0 else qk[r, 8 + qt, 0:nk]
                            mm(b[:, 0:nk], qk[r, qt, q0:q0 + P], keys, start=True, stop=True).then_inc(S["score_full"], 1)
                    w = u - 2
                    if 0 <= w < len(U):
                        ring = 1 if i == 1 else 2
                        pe.wait_ge(S["p_ready"], w + 1)
                        if w >= ring:
                            pe.wait_ge(S["pt_ready"], w + 1 - ring)
                        pb = bank[4] if i == 1 else bank[4 + w % 2]
                        for kt in range(2 if U[w][1] == 0 else 4):
                            ins = nc.tensor.transpose(pb[:, kt * P:kt * P + P], p1[w % 3][:, kt * P:kt * P + P], ident)
                        ins.then_inc(S["p_turned"], 1)
                    if u >= 4 and u % 2 == 0 and u - 4 < len(U):
                        p = (u - 4) // 2
                        hd, s, _ = U[2 * p]
                        o = 2 * p // per_o
                        pe.wait_ge(S["pt_ready"], 2 * p + 2)
                        if o >= 2:
                            pe.wait_ge(S["o_lo"], o - 1)
                        if i == 1:
                            out, vc = bank[6 + o % 2][:, CTX * s:CTX * s + 256], slice(2 * HD * hd, 2 * HD * hd + 2 * HD)
                        else:
                            r0 = HD * (hd % 2)
                            vh = hd // (A_HEADS // A_KV) if i == 0 else hd
                            out, vc = bank[6 + o % 2][r0:r0 + HD, CTX * s:CTX * s + 256], slice(HD * vh, HD * vh + HD)
                        kts = 2 if s == 0 else 4
                        for kt in range(kts):
                            ins = mm(out, v_tok[:, kt, vc], pt[p % 2][:, kt, :], start=kt == 0, stop=kt == kts - 1)
                        ins.then_inc(S["pv_full"], 1)

            def gate(S, u):
                if u:
                    pe.wait_ge(S["gate_soft"], u)
                    pe.wait_ge(S["gate_min"], u)
                if u >= 2:
                    pe.wait_ge(S["state"], 3 * (u - 1))
                rows_u = slice(32 * (u % 2), 32 * (u % 2) + C_RANK)
                mm(bank[7][:], w_gate[rows_u, CH * (u // 2):CH * (u // 2) + CH], zT[rows_u, :],
                   start=True, stop=True).then_inc(S["gate_full"], 1)

            def qkv_gla(n, fg):
                S = att[2]
                for ft in range(8):
                    group_free(fg + ft)
                    project(n + ft, bank[(fg + ft) % 4], h_hi, h_lo, slice(0, T),
                            ready=(s_hlo, 4 * DT) if ft == 0 else None)
                pe.wait_ge(S["z_lo"], 1)
                for k in range(DT):
                    ins = three(bank[4][0:64, :], z_hi[:, k, :], z_lo[:, k, :], h_hi[:, k, :], h_lo[:, k, :],
                                k == 0, k == DT - 1)
                ins.then_inc(S["z_full"], 1)
                pe.wait_ge(S["z_copied"], 1)
                gate(S, 0)
                v_project(n + 8, fg + 8, 4)
                for ft in range(8):
                    group_free(fg + 16 + ft)
                    project(n + 16 + ft, bank[(fg + 16 + ft) % 4], h_hi, h_lo, slice(0, T))

            def gla():
                S = att[2]

                def levels(c):
                    hd, bwd, p, ci, cs = chunk_of(c)
                    w = c // 2
                    pe.wait_ge(S["q_dec"], 8 * w + LEVELS)
                    pe.wait_ge(S["k_dec"], 8 * w + LEVELS)
                    if c >= 2:
                        pe.wait_ge(S["masked"], c - 1)
                    ks, qs = (right, left) if bwd else (left, right)
                    for l in range(8):
                        out = bank[2 * (c % 2) + l // 4][:, CH * (l % 4):CH * (l % 4) + CH]
                        if l < LEVELS:
                            ins = mm(out, ks[w % 2][:, l, ci], qs[w % 2][:, l, ci], start=True, stop=True)
                        else:
                            ins = mm(out, qk[:, 4 + hd, cs], qk[:, hd, cs], start=True, stop=True)
                    ins.then_inc(S["score_full"], 1)

                def chunk(c):
                    hd, bwd, p, ci, cs = chunk_of(c)
                    w = c // 2
                    vals = v_tok[:, cs.start // CH, C_HV * hd:C_HV * hd + C_HV]
                    pe.wait_ge(S["k_dec"], 8 * w + 8)
                    if c % 4 < 3:
                        if c:
                            pe.wait_ge(S["k_endT"], states(c) - 1)
                        if c % 8 == 0 and hd:
                            pe.wait_ge(S["rs_ready"], hd)
                        nc.tensor.transpose(bank[6][:, 0:CH], k_end[w % 2][:, ci], ident).then_inc(S["turned"], 1)
                    pe.wait_ge(S["scores"], c + 1)
                    pe.wait_ge(S["q_dec"], 8 * w + 8)
                    if c % 8 == 0 and hd:
                        pe.wait_ge(S["o_normed"], 2 * hd)
                    if c % 4:
                        pe.wait_ge(S["state"], states(c - 1))
                    for v in range(2):
                        vc = slice(CH * v, CH * v + CH)
                        ins = mm(bank[4 + v][:, cs], vals[:, vc], scores[:], start=c % 8 == 0,
                                 stop=c % 8 == 7 and c % 4 == 0, skip_group_check=True)
                        if c % 4:
                            ins = mm(bank[4 + v][:, cs], state[(c % 4 - 1) % 2][:, vc], q_dec[w % 2][:, ci], start=False,
                                     stop=c % 8 == 7, skip_group_check=True)
                    ins.then_inc(S["o_full"], 1)
                    if c % 4 < 3:
                        pe.wait_ge(S["k_endT"], states(c))
                        if c:
                            pe.wait_ge(S["state"], states(c) - 1)
                        g = min(c // 4 + 2, C_UNITS)
                        pe.wait_ge(S["gate_soft"], g)
                        pe.wait_ge(S["gate_min"], g)
                        mm(bank[7][:, 0:C_HV], k_endT[:], vals, start=True, stop=True).then_inc(S["update_full"], 1)

                n_chunks = 2 * C_ITEMS
                pe.wait_ge(s_free["act"], freed[start["wo", 2][1] - 1][1])
                pe.wait_ge(s_free["dve"], freed[start["wo", 2][1] - 9][1])
                levels(0)
                for c in range(n_chunks):
                    if c % 4 == 0 and c // 4 + 1 < C_UNITS:
                        gate(S, c // 4 + 1)
                    if c + 1 < n_chunks:
                        levels(c + 1)
                    chunk(c)
                    if c % 8 == 7:
                        hd = c // 8
                        pe.wait_ge(S["squared"], hd + 1)
                        pe.wait_ge(S["k_endT"], states(c))
                        for v in range(2):
                            ins = mm(bank[6][:], ones, o_head[v][:], start=v == 0, stop=v == 1)
                        ins.then_inc(S["ss_full"], 1)

            pe.wait_ge(s_cst, 16)
            pe.wait_ge(s_cond, 32)
            nc.tensor.transpose(bank[4][:, 0:16], cond_row[:], ident[0:16, 0:16]).then_inc(s_cond_t, 1)
            pe.wait_ge(s_small, 16)
            nc.tensor.transpose(bank[5][:, 0:32], small_row[:], ident[0:32, 0:32]).then_inc(s_cond_t, 1)
            pe.wait_ge(s_lam_p, 1)
            mm(bank[5][:, 0:2], ones[0:HD, :], small[0:HD, 9:11], start=True, stop=True).then_inc(s_lam_d, 1)
            pe.wait_ge(s_rows, 16)
            for b in range(2):
                for r in range(4):
                    ins = nc.tensor.transpose(bank[2 + b][:, r * P:r * P + P], rows[:, 4 * b + r, :], ident)
                ins.then_inc(s_rows_t, 1)
            pe.wait_ge(s_tok, 32)
            for k in range(DT):
                if k >= 2:
                    pe.wait_ge(s_xn, k - 1)
                for tt in range(4):
                    ins = nc.tensor.transpose(bank[k % 2][:, tt * P:tt * P + P], tok[:, tt, k * P:k * P + P], ident)
                ins.then_inc(s_tok_t, 1)
            pe.wait_ge(s_cond_v, 1)
            for g in range(4):
                for q in range(4):
                    mod_slab(4 * g + q, g, q)
                mod_turn(g)
            for i in range(layers):
                st = 2 * i
                n, fg = start["qkv", i]
                if i == 0:
                    qkv_norm_rope(n, fg)
                elif i == 2:
                    qkv_gla(n, fg)
                else:
                    qkv_plain(i, n, fg)
                gla() if i == 2 else attention(i)
                n, fg = start["wo", i]
                c = cols(i, "tail")
                for dt in range(DT):
                    group_free(fg + dt)
                    project(n + dt, bank[(fg + dt) % 4], h_hi, h_lo, c, ready=(att[i]["o_lo"], 0) if dt == 0 else None)
                stats(st, c)
                n, fg = start["premod", i]
                if i + 1 < layers:
                    for q in range(4):
                        mod_slab(n + q, 12 * (i + 1), q)
                n, fg = start["up", i]
                per = 8 if i + 1 < layers else 4
                group_free(fg + 3)
                with pe.Fori(0, FT // 2) as it:
                    for u in range(2):
                        for k in range(2):
                            at_slab = n + (4 * u + 2 * k if per == 8 else 2 * u + k)
                            pe.wait_ge(s_free["dve"], freed[fg][1] - 4 + 2 * u + k + 4 * it)
                            project(at_slab, bank[2 * u + k], h_hi, h_lo, c,
                                    ready=(s_hlo, (st + 1) * DT) if u == 0 and k == 0 else None, it=it, per=per)
                            if per == 8:
                                if u == 0 and k == 0:
                                    pe.wait_ge(s_mod_row, 12 * (i + 1) + 1 + it)
                                    for b in range(4):
                                        ins = mm(MOD_T[:, bass.ds(2 * b + 8 * it, 2)], mod_row[:, b * P:(b + 1) * P],
                                                 sel, start=True, stop=True)
                                    ins.then_inc(s_mod_t, 1)
                                q = 2 * u + k
                                mod_slab(at_slab + 1, 12 * (i + 1) + 1, q, it=it, per=per)
                if i + 1 < layers:
                    mod_turn(12 * (i + 1) + 11)
                n, fg = start["down", i]
                for dt in range(DT):
                    group_free(fg + dt)
                    for q, (k0, nk) in enumerate(((0, 8), (8, 8), (16, 6))):
                        project(n + 3 * dt + q, bank[(fg + dt) % 4], g_hi, g_lo, c, k0, nk, first=q == 0, last=q == 2,
                                ready=(s_glo, FT * i) if dt == 0 else None)
                stats(st + 1, c)
            for q in range(4):
                if q == 0:
                    pe.wait_ge(s_outf, DT)
                for k in range(4):
                    ins = nc.tensor.transpose(bank[q][:, k * P:k * P + P],
                                              out_f[:, 4 * (q % 2) + k, P * (q // 2):P * (q // 2) + P], ident)
                ins.then_inc(s_outt, 1)


def kernel(**inputs):
    import numpy as _np
    import concourse.bacc as _bacc
    from concourse import mybir as _mybir
    from concourse.bass_utils import run_bass_kernel_spmd as _run

    nc = _bacc.Bacc("TRN2", target_bir_lowering=False, num_devices=1, dynamic_dma_scratch_size=1024)
    data = {k: _np.ascontiguousarray(v) for k, v in inputs.items()}
    per_layer = []
    for i in range(DEPTH):
        per_layer += [data[n][i].reshape(-1, P) for n in ("mod_b", "ln1_g", "ln1_b", "ln2_g", "ln2_b",
                                                          "ffn_conv_b", "ffn_conv_w")]
    table = _np.concatenate(per_layer, 0)
    for n in ("mod_b", "ln1_g", "ln1_b", "ln2_g", "ln2_b", "ffn_conv_b", "ffn_conv_w"):
        del data[n]
    data["rows"] = table
    zeros = _np.zeros
    lam = [data.pop("b_lambda_" + n)[0] for n in ("q1", "k1", "q2", "k2")]
    small = zeros((32, P), _np.float32)
    small[0], small[1] = _np.tile(data.pop("a_q_norm")[0], 2), _np.tile(data.pop("a_k_norm")[0], 2)
    small[2], small[3:5] = data.pop("b_subln")[0], data.pop("c_norm")[0].reshape(2, P)
    for n in range(4):
        small[5 + n, 0:HD] = lam[n]
    small[16:20], small[20:24] = data.pop("c_b_gate_fwd")[0].reshape(4, P), data.pop("c_b_gate_bwd")[0].reshape(4, P)
    data["small"] = small
    data["k_const"], data["k_window"] = constants()
    data["k_blocks"] = block_masks()
    arrays, args = {}, {}
    for name, x in data.items():
        arrays[f"in_{name}"] = x
        args[name] = nc.dram_tensor(f"in_{name}", x.shape, _mybir.dt.from_np(x.dtype), kind="ExternalInput").ap()
    args["out"] = nc.dram_tensor("out_0", (1, LAT, D), _mybir.dt.float32, kind="ExternalOutput").ap()
    build_program(nc, args)
    r = _run(nc, [arrays], core_ids=[0])
    return r.results[0]["out_0"]
```

```python
import math
from contextlib import ExitStack

import numpy as np

import concourse.bass as bass
import concourse.mybir as mybir

f32, f32r = mybir.dt.float32, mybir.dt.float32r
ACT, ALU = mybir.ActivationFunctionType, mybir.AluOpType
AX = mybir.AxisListType.X

P = 128
D, DEPTH = 1024, 4
CTX, LAT = 256, 256
T = CTX + LAT
DT = D // P
FF = 2816
FT = FF // P
GRID_W = 64
N_MOD = 6
A_HEADS, A_KV, B_HEADS, C_HEADS, D_HEADS, HD = 16, 4, 8, 4, 16, 64
C_KEY, C_VAL, C_RANK, C_NORMALIZER = 512, 1024, 16, 16.0
WIN_C, N_DR, N_DC = 16, 15, 31
NORM_EPS, LN_EPS = 1e-6, 1e-5
ALPHA = (2 * DEPTH) ** 0.25
SCALE = HD ** -0.5
LAM_INIT = 0.8 - 0.6 * math.exp(-0.3 * 1)

R_MODB, R_LN1G, R_LN1B, R_LN2G, R_LN2B, R_CB, R_CW = 0, 48, 56, 64, 72, 80, 124
R_LAYER = 256

K_ID, K_SWAP, K_ONES, K_HEAD, K_COS, K_SIN, K_EPS = 0, 128, 256, 384, 512, 768, 1024
K_N = 1032

SLOTS = 4
AHEAD = SLOTS - 1
PREMOD = 2
SLAB = 1024
NB = 512

CH = 128
LEVELS = 7
PLANES = 6
C_UNITS = 2 * C_HEADS
C_ITEMS = 2 * C_UNITS
C_HV = C_VAL // C_HEADS


def constants():
    k = np.zeros((P, K_N), np.float32)
    i = np.arange(P)
    k[:, K_ID:K_ID + P] = np.eye(P)
    k[i ^ 32, K_SWAP + i] = 1.0
    k[:, K_ONES:K_ONES + P] = 1.0
    k[:, K_HEAD:K_HEAD + P] = (i[:, None] // HD == i[None, :] // HD)
    t = np.arange(LAT)
    nf = HD // 4
    inv = (np.float32(1.0) / np.float32(10000.0) ** (np.arange(nf, dtype=np.float32) / np.float32(nf))).astype(np.float32)
    ang = np.concatenate([(t // GRID_W).astype(np.float32)[:, None] * inv,
                          (t % GRID_W).astype(np.float32)[:, None] * inv], -1).astype(np.float32)
    pair = i % 32
    k[:, K_COS:K_COS + LAT] = np.cos(ang).T[pair]
    k[:, K_SIN:K_SIN + LAT] = np.sin(ang).T[pair] * np.where(i % HD < 32, -1.0, 1.0)[:, None]
    k[:, K_EPS], k[:, K_EPS + 1], k[:, K_EPS + 2] = NORM_EPS, LN_EPS, 1.0
    k[0:2, K_EPS + 3], k[2:4, K_EPS + 4] = 1.0, 1.0
    cq = np.arange(GRID_W)
    c0 = np.clip(cq - WIN_C // 2, 0, GRID_W - WIN_C)
    col_in = (cq[None, :] >= c0[:, None]) & (cq[None, :] < c0[:, None] + WIN_C)
    window = np.tile(np.where(col_in, 0.0, -1e30).astype(np.float32)[::-1], (2, 1))
    return k, window


def block_masks():
    j, i = np.arange(P)[:, None], np.arange(P)[None, :]
    return np.stack([(i >> s) == (j >> s) for s in (7, 4, 3, 2, 1, 0)], 1).astype(np.float32)


class Count:

    def __init__(self, sem):
        self.sem, self.n = sem, 0

    def up(self, ins, by=1):
        ins.then_inc(self.sem, by)
        self.n += by
        return self.n


def mods_after(phase, tile):
    if phase == "qkv":
        return range(2 * tile, 2 * tile + 2)
    return range(20 + (3 * tile + 1) // 2, 20 + (3 * tile + 4) // 2)


def mod_events(i, part):
    return part + 1 if i == 0 else i + 3


def make_plan(layers):
    slabs, owner, start = [], [], {}

    def mod_group(layer, g):
        slabs.extend(("mod", layer, g, q) for q in range(4))

    start["mod"] = (0, 0)
    for g in range(4):
        mod_group(0, g)
    for i in range(layers):
        start["qkv", i] = (len(slabs), len(owner))
        if i == 0:
            for ft in range(10):
                slabs.append(("f", "a_w_qkv", ft * P, 0, 8))
                owner.append("dve")
                slabs.extend(("mod", 0, 4 + m // 4, m % 4) for m in mods_after("qkv", ft))
            slabs.extend(("v", "a_w_qkv", 1280, q) for q in range(2))
            owner += ["dve"] * 2
        elif i == 1 or i == 3:
            name = "b_w_qkv" if i == 1 else "d_w_qkv"
            for ft in range(16):
                slabs.append(("f", name, ft * P, 0, 8))
                owner.append("act")
            for g in range(4):
                slabs.extend(("v", name, 2048 + 256 * g, q) for q in range(2))
                owner += ["dve"] * 2
        else:
            for ft in range(8):
                slabs.append(("f", "c_w_in", ft * P, 0, 8))
                owner.append("act")
            for g in range(4):
                slabs.extend(("v", "c_w_in", 1024 + 256 * g, q) for q in range(2))
                owner += ["dve"] * 2
            for ft in range(8):
                slabs.append(("f", "c_w_in", 2048 + ft * P, 0, 8))
                owner.append("act")
        start["wo", i] = (len(slabs), len(owner))
        for dt in range(DT):
            slabs.append(("f", "abcd"[i] + "_w_o", dt * P, 0, 8))
            owner.append("act")
            if i == 0:
                slabs.extend(("mod", 0, 4 + m // 4, m % 4) for m in mods_after("wo", dt))
        mods = [("mod", i + 1, m // 4, m % 4) for m in range(48)] if i + 1 < layers else []
        start["premod", i] = (len(slabs), len(owner))
        slabs.extend(mods[:PREMOD])
        start["up", i] = (len(slabs), len(owner))
        for j in range(FT):
            slabs.extend(("up", i, col) for col in (j * P, FF + j * P))
            owner += ["dve"] * 2
            slabs.extend(mods[PREMOD + 2 * j:PREMOD + 2 * j + 2])
        start["postmod", i] = (len(slabs), len(owner))
        slabs.extend(mods[PREMOD + 2 * FT:])
        start["down", i] = (len(slabs), len(owner))
        for dt in range(DT):
            for k0, nk in ((0, 8), (8, 8), (16, 6)):
                slabs.append(("down", i, dt * P, k0, nk))
            owner.append("act")
    freed, seen = [], {"act": 0, "dve": 0}
    for e in owner:
        seen[e] += 1
        freed.append((e, seen[e]))
    return slabs, freed, start


def build_program(nc, a, layers=DEPTH, probe=None):
    slabs, freed, start = make_plan(layers)
    n_slabs = len(slabs)
    ctx = ExitStack()
    with ctx:
        top = [(nc.sbuf_base + 63) // 64 * 64]

        def place(name, shape, dt=f32, at=None):
            size = int(np.prod(shape[1:])) * mybir.dt.size(dt)
            offset = top[0] if at is None else at[0]
            (top if at is None else at)[0] += (size + 63) // 64 * 64
            return nc.alloc_sbuf_tensor_at(name, list(shape), dt, offset=offset)

        xn = place("xn", [P, DT, T])
        h_hi, h_lo = place("h_hi", [P, DT, T], f32r), place("h_lo", [P, DT, T], f32r)
        raw = [place(f"slab_raw{s}", [P, SLAB]) for s in range(SLOTS)]
        whi = [place(f"slab_hi{s}", [P, SLAB], f32r) for s in range(SLOTS)]
        wlo = [place(f"slab_lo{s}", [P, SLAB], f32r) for s in range(SLOTS)]
        rotary_at = [top[0] + 4 * K_COS]
        cst = place("cst", [P, K_N])
        k_end = [place(f"k_end{s}", [P, 2 * CH], at=rotary_at) for s in range(2)]
        prm = place("prm", [P, DEPTH * R_LAYER])
        modT = [place(f"modT{s}", [P, N_MOD * DT, 2]) for s in range(2)]
        coef = [place(f"coef{s}", [P, 6, DT]) for s in range(2)]
        unit_gb = place("unit_gb", [P, 2, DT])
        mod_row_at = [top[0]]
        mod_row = place("mod_row", [4, NB])
        w_gate = place("w_gate", [48, C_KEY], at=mod_row_at)
        small_row = place("small_row", [32, P])
        cond_row = place("cond_row", [16, P])
        cond = place("cond", [P, 2, DT])
        cond4 = place("cond4", [P, DT, 4], f32r)
        small = place("small", [P, 32])
        mean, rstd = place("mean", [P, T]), place("rstd", [P, T])
        work = [top[0]]
        res_t = [place(f"res_t{s}", [P, T], at=work) for s in range(2)]
        acc_s, acc_q = place("acc_s", [P, T], at=work), place("acc_q", [P, T], at=work)
        sq = place("sq", [P, T], at=work)
        conv_at = [top[0]]
        conv = [[place(f"conv{c}{u}", [P, T], at=conv_at) for u in range(2)] for c in range(2)]
        g32 = [place(f"g32_{u}", [P, T], at=conv_at) for u in range(2)]
        gla_at = [top[0]]
        masked = [place(f"masked{s}", [P, PLANES, CH], at=gla_at) for s in range(2)]
        o_head = [place(f"o_head{v}", [P, T], at=gla_at) for v in range(2)]
        sq_head = [rstd, place("sq_head", [P, T], at=gla_at)]
        top[0] = max(work[0], conv_at[0])
        arena = top[0]
        at = [arena]
        tok = place("tok", [P, 4, D], at=at)
        rows = place("rows", [P, 8, P], at=at)
        at = [arena]
        g_hi, g_lo = place("g_hi", [P, FT, T], f32r, at=at), place("g_lo", [P, FT, T], f32r, at=at)
        at = [arena]
        qk = place("qk", [P, 16, T], at=at)
        v_tok = place("v_tok", [P, 4, D], at=at)
        p1 = [place(f"p1_{s}", [P, T], at=at) for s in range(3)]
        pt = [place(f"pt{s}", [P, 4, 256], at=at) for s in range(2)]
        stat = place("stat", [P, 6, 128], at=at)
        own = at[0]
        at = [own]
        kd = place("kd", [P, A_KV, T], at=at)
        sqa = [place(f"sqa{s}", [P, T], at=at) for s in range(2)]
        rsa = [place(f"rsa{s}", [P, T], at=at) for s in range(2)]
        rope_t = place("rope_t", [P, LAT], at=at)
        at = [own]
        rope_b = place("rope_b", [P, LAT], at=at)
        p2 = [place(f"p2_{s}", [P, T], at=at) for s in range(3)]
        sqb, rsb, o32 = place("sqb", [P, T], at=at), place("rsb", [P, T], at=at), place("o32", [P, T], at=at)
        at = [own]
        bias = place("bias", [P, D_HEADS, 6 * GRID_W], at=at)
        window = place("window", [P, GRID_W], at=at)
        at = [arena + 4 * (16 * T + 4 * D)]
        right = [place(f"right{s}", [P, LEVELS, 2 * CH], at=at) for s in range(2)]
        left = [place(f"left{s}", [P, LEVELS, 2 * CH], at=at) for s in range(2)]
        same_block = place("same_block", [P, PLANES, CH], at=at)
        z_at = [at[0]]
        soft = place("soft", [P, T], at=at)
        cum = [place(f"cum{s}", [P, T], at=at) for s in range(2)]
        rel = [place(f"rel{s}", [P, 2 * CH], at=at) for s in range(3)]
        q_dec = [place(f"q_dec{s}", [P, 2 * CH], at=at) for s in range(2)]
        start_dec = [place(f"start_dec{s}", [P, 2 * CH], at=at) for s in range(2)]
        k_endT, scores = place("k_endT", [P, CH], at=at), place("scores", [P, CH], at=at)
        state = [place(f"state{s}", [P, C_HV], at=at) for s in range(2)]
        zT = place("zT", [64, T], at=at)
        z_raw = place("z_raw", [P, DT, 64], at=z_at)
        z_hi, z_lo = place("z_hi", [P, DT, 64], f32r, at=z_at), place("z_lo", [P, DT, 64], f32r, at=z_at)
        gate_min = mean
        assert at[0] <= nc.sbuf_usable_end
        at = [arena]
        out_f = place("out_f", [P, DT, LAT], at=at)
        out_tok = place("out_tok", [P, 2, D], at=at)
        assert at[0] <= nc.sbuf_usable_end

        bank = [nc.alloc_psum_tensor(f"bank{b}", [P, NB], f32) for b in range(8)]
        LN_SUM, LN_SQ, MOD_ACC, MOD_T = bank[4], bank[5], bank[6], bank[7]

        def sem(name):
            return ctx.enter_context(nc.semaphore(name))

        loaded = [sem(f"slab_loaded{s}") for s in range(SLOTS)]
        s_hi, s_lo, s_used = sem("slab_hi_ready"), sem("slab_lo_ready"), sem("slab_used")
        s_free = {"act": sem("group_freed_act"), "dve": sem("group_freed_dve")}
        s_cst, s_cond, s_tok, s_rows, s_small, s_bias_in = (sem(n) for n in (
            "consts_in", "cond_in", "tokens_in", "rows_in", "small_in", "bias_in"))
        s_cond_t, s_cond_a, s_cond_v, s_rows_t, s_rows_v, s_tok_t = (sem(n) for n in (
            "cond_transposed", "cond_act", "cond_split", "rows_transposed", "rows_copied", "tokens_transposed"))
        s_mod_row, s_mod_t, s_mod_in, s_coef = (sem(n) for n in (
            "mod_row_copied", "mod_transposed", "mod_evacuated", "coefficients_ready"))
        s_y, s_sum, s_sqd, s_qsum, s_stats, s_mean, s_var, s_rstd, s_cen, s_xn = (sem(n) for n in (
            "residual_added", "sum_added", "squared", "squares_added", "stats_full",
            "mean_ready", "var_ready", "rstd_ready", "centred", "xn_ready"))
        s_hf, s_hhi, s_hlo = sem("h_modulated"), sem("h_hi_ready"), sem("h_lo_ready")
        s_tap1, s_tap2, s_silu, s_gmul, s_ghi, s_glo = (sem(n) for n in (
            "conv_centre_tap", "conv_left_tap", "silu_done", "gated", "g_hi_ready", "g_lo_ready"))
        s_dve, s_act = sem("dve_step"), sem("act_step")
        s_kd, s_window = sem("keys_doubled"), sem("bias_masked")
        s_lam_p, s_lam_d, s_lam_e, s_gains = (sem(n) for n in (
            "lambda_products", "lambda_dots", "lambda_exps", "gains_ready"))
        s_outf, s_outt, s_outv, s_out = sem("out_scaled"), sem("out_transposed"), sem("out_copied"), sem("out_stored")

        att = {}
        for i in (0, 1, 3):
            att[i] = {n: sem(f"{n}_{i}") for n in (
                "qk_ready", "swapped", "score_full", "biased", "context_copied", "negmax", "exped", "p_ready", "p_turned",
                "pt_ready", "pv_full", "o_hi", "o_lo")}
            if i < 2:
                att[i].update({n: sem(f"{n}_{i}") for n in ("squared_h", "ss_full", "rs_ready", "o_normed")})
        att[2] = {n: sem(f"gla_{n}") for n in (
            "zeroed", "tables_in", "z_hi", "z_lo", "z_full", "z_copied", "gate_full", "gate_soft", "gate_min", "cum",
            "rel", "decay", "q_dec", "k_dec", "score_full", "masked", "scores", "turned", "k_endT", "o_full",
            "update_full", "state", "o_copied_act", "o_copied_dve", "squared", "ss_full", "rs_ready", "o_normed", "o_gated", "o_hi", "o_lo")}

        block = ctx.enter_context(nc.Block())

        ident, swap, ones, heads = (cst[:, c:c + P] for c in (K_ID, K_SWAP, K_ONES, K_HEAD))
        cos, sin = cst[:, K_COS:K_COS + LAT], cst[:, K_SIN:K_SIN + LAT]
        eps_norm, eps_ln, one = (cst[:, K_EPS + c:K_EPS + c + 1] for c in range(3))
        sel = cst[0:4, K_EPS + 3:K_EPS + 5]

        def cols(i, part):
            return slice(CTX, T) if i == DEPTH - 1 and part == "tail" else slice(0, T)

        def segs(c):
            return [s for s in ((0, slice(0, CTX)), (1, slice(CTX, T))) if s[1].start >= c.start]

        def gain(st):
            if st == 0:
                return unit_gb[:, 0, :], unit_gb[:, 1, :]
            i, second = (st - 1) // 2, (st - 1) % 2
            r = R_LAYER * i + (R_LN2G if second else R_LN1G)
            return prm[:, r:r + DT], prm[:, r + DT:r + 2 * DT]

        def mod(st, which):
            return (3 * (st % 2) + which) * DT

        def src(s):
            kind = s[0]
            if kind == "mod":
                _, i, g, q = s
                return a["mod_w"][i, 2 * q * P:(2 * q + 2) * P, g * NB:(g + 1) * NB].rearrange("(k p) c -> p k c", p=P), 2
            if kind == "f":
                _, name, c, k0, nk = s
                return a[name][0, k0 * P:(k0 + nk) * P, c:c + P].rearrange("(k p) c -> p k c", p=P), nk
            if kind == "v":
                _, name, c, q = s
                return a[name][0, 4 * q * P:(4 * q + 4) * P, c:c + 256].rearrange("(k p) c -> p k c", p=P), 4
            if kind == "up":
                _, i, c = s
                return a["ffn_w_up"][i, :, c:c + P].rearrange("(k p) c -> p k c", p=P), 8
            _, i, c, k0, nk = s
            return a["ffn_w_down"][i, k0 * P:(k0 + nk) * P, c:c + P].rearrange("(k p) c -> p k c", p=P), nk

        def width(s):
            return {"mod": SLAB, "v": SLAB, "up": SLAB}.get(s[0]) or s[4] * P

        def mirrored(ap):
            return ap.rearrange("p (r c) -> p r c", c=GRID_W)[:, :, ::-1]

        def attention_units(i):
            n = (A_HEADS, B_HEADS, 0, D_HEADS)[i]
            return [(hd, s, CTX * s + P * b) for hd in range(n) for s in ((1,) if i == 3 else (0, 1)) for b in (0, 1)]

        def rpb_block(dr):
            t = a["d_rpb"]
            return bass.AP(tensor=t.tensor, offset=dr * N_DC + WIN_C - GRID_W,
                           ap=[[1, GRID_W], [N_DR * N_DC, D_HEADS], [1, GRID_W]])

        def gates_at(w):
            return (w + 3) // 2 if w % 2 and (w + 3) // 2 < C_UNITS else None

        def item_of(w):
            return w // 4, w // 2 % 2, slice(CTX * (w % 2), CTX * (w % 2) + 2 * CH)

        def chunk_of(c):
            hd, bwd, cols_w = item_of(c // 2)
            p = c % 2 ^ bwd
            return hd, bwd, p, slice(CH * p, CH * p + CH), slice(cols_w.start + CH * p, cols_w.start + CH * p + CH)

        def states(c):
            return 3 * (c // 4) + min(c % 4 + 1, 3)

        def half(ap, l, right_half):
            v = ap.rearrange("p (n h s) -> p n h s", h=2, s=64 >> l)
            return v[:, :, 1 if right_half else 0, :]

        @block.sync
        def _(sp):
            sp.dma_start(cst[:], a["k_const"]).then_inc(s_cst, 16)
            sp.dma_start(cond_row[0:DT, :], a["c_ctx"].rearrange("(k p) -> k p", p=P)).then_inc(s_cond, 16)
            sp.dma_start(cond_row[DT:2 * DT, :], a["c"][0].rearrange("(k p) -> k p", p=P)).then_inc(s_cond, 16)

            def load(n):
                source, nk = src(slabs[n])
                if n >= SLOTS:
                    sp.wait_ge(s_hi, n - SLOTS + 1)
                    sp.wait_ge(s_lo, n - SLOTS + 1)
                dst = raw[n % SLOTS][:, 0:width(slabs[n])].rearrange("p (k c) -> p k c", k=nk)
                sp.dma_start(dst, source).then_inc(loaded[n % SLOTS], 16)

            n = 0
            while n < n_slabs:
                rolled = [i for i in range(layers) if start["up", i][0] == n]
                if not rolled:
                    load(n)
                    n += 1
                    continue
                i = rolled[0]
                per = 8 if i + 1 < layers else 4
                with sp.Fori(0, FT // 2) as it:
                    for c in range(per):
                        s = slabs[n + c]
                        sp.wait_ge(s_hi, n + c - SLOTS + 1 + per * it)
                        sp.wait_ge(s_lo, n + c - SLOTS + 1 + per * it)
                        if s[0] == "up":
                            source = a["ffn_w_up"][i, :, bass.ds(s[2] + 2 * P * it, P)]
                        else:
                            source = a["mod_w"][i + 1, 2 * s[3] * P:(2 * s[3] + 2) * P, bass.ds(NB * s[2] + NB * it, NB)]
                        nk = 8 if s[0] == "up" else 2
                        sp.dma_start(raw[(n + c) % SLOTS][:].rearrange("p (k c) -> p k c", k=nk),
                                     source.rearrange("(k p) c -> p k c", p=P)).then_inc(loaded[(n + c) % SLOTS], 16)
                n += per * (FT // 2)
            sp.wait_ge(s_outv, 4)
            sp.dma_start(a["out"][0].rearrange("(t p) d -> p t d", p=P), out_tok[:]).then_inc(s_out, 16)
            sp.wait_ge(s_out, 16)

        @block.scalar
        def _(act):
            step = Count(s_act)
            act.dma_start(small_row[:], a["small"]).then_inc(s_small, 16)
            act.dma_start(rows[:], a["rows"].rearrange("(r p) d -> p r d", p=P)).then_inc(s_rows, 16)
            act.dma_start(tok[:, 0:2, :], a["ctx"][0].rearrange("(t p) d -> p t d", p=P)).then_inc(s_tok, 16)
            act.dma_start(tok[:, 2:4, :], a["x"][0].rearrange("(t p) d -> p t d", p=P)).then_inc(s_tok, 16)

            def split(n, it=0, per=0):
                if n >= n_slabs:
                    return
                slot = n % SLOTS
                act.wait_ge(loaded[slot], 16 * (n // SLOTS + 1) + 16 * (per // SLOTS) * it)
                if n >= SLOTS:
                    act.wait_ge(s_used, n - SLOTS + 1 + per * it)
                w = SLAB if per else width(slabs[n])
                nc.scalar.activation(whi[slot][:, 0:w], raw[slot][:, 0:w], ACT.Copy).then_inc(s_hi, 1)

            def make_h(st, c):
                cf = coef[st % 2]
                for k in range(DT):
                    act.wait_ge(s_xn, DT * st + k + 1)
                    if k == 0:
                        act.wait_ge(s_coef, st + 1)
                    if k >= 2:
                        act.wait_ge(s_hlo, DT * st + k - 1)
                    for s, cc in segs(c):
                        ins = nc.scalar.activation(res_t[k % 2][:, cc], xn[:, k, cc], ACT.Identity,
                                                   bias=cf[:, 2 + s, k:k + 1], scale=cf[:, s, k:k + 1])
                    ins.then_inc(s_hf, 1)
                    act.wait_ge(s_hf, DT * st + k + 1)
                    nc.scalar.activation(h_hi[:, k, c], res_t[k % 2][:, c], ACT.Copy).then_inc(s_hhi, 1)

            def residual(st, n, fg, per, c):
                i = st // 2

                def square(dt):
                    act.wait_ge(s_y, DT * st + dt + 1)
                    if dt >= 2:
                        act.wait_ge(s_qsum, 7 * st + dt - 1)
                    nc.scalar.activation((sq if dt else acc_q)[:, c], xn[:, dt, c], ACT.Square).then_inc(s_sqd, 1)

                if st % 2:
                    nc.scalar.preload_act_table_set("natural_log_exp_and_others")
                for dt in range(DT):
                    for q in range(per):
                        split(n + q + AHEAD)
                    n += per
                    if dt:
                        square(dt - 1)
                    act.wait_ge(s_used, n)
                    if dt == 0:
                        act.wait_ge(s_mod_in, mod_events(i, 1))
                    for s, cc in segs(c):
                        ins = nc.scalar.activation(
                            res_t[dt % 2][:, cc], bank[(fg + dt) % 4][:, cc], ACT.Identity,
                            bias=coef[st % 2][:, 5, dt:dt + 1],
                            scale=modT[i % 2][:, mod(st, 2) + dt, s:s + 1])
                    ins.then_inc(s_free["act"], 1)
                    for m in mods_after("wo", dt) if st == 0 else ():
                        split(n + AHEAD)
                        n += 1
                square(DT - 1)
                if st % 2 == 0 and i + 1 < layers:
                    for q in range(PREMOD):
                        split(n + q + AHEAD)
                act.wait_ge(s_var, st + 1)
                step.up(nc.scalar.activation(rstd[:, c], acc_q[:, c], ACT.Ln))
                act.wait_ge(s_act, step.n)
                nc.scalar.activation(rstd[:, c], rstd[:, c], ACT.Exp, scale=-0.5).then_inc(s_rstd, 1)

            def root(dst, of, scale):
                step.up(nc.scalar.activation(dst, of, ACT.Ln, scale=scale, bias=eps_norm))
                act.wait_ge(s_act, step.n)
                return nc.scalar.activation(dst, dst, ACT.Exp, scale=-0.5)

            def qkv_norm_rope(n, fg):
                S = att[0]

                def roots(ft):
                    act.wait_ge(S["ss_full"], ft + 1)
                    if ft >= 2:
                        act.wait_ge(s_free["dve"], ft - 1)
                    root(rsa[ft % 2][:], bank[4][:], 1.0 / HD).then_inc(S["rs_ready"], 1)

                for ft in range(10):
                    split(n + AHEAD)
                    n += 1
                    act.wait_ge(s_used, n)
                    if ft >= 2:
                        act.wait_ge(S["ss_full"], ft - 1)
                    nc.scalar.activation(sqa[ft % 2][:], bank[(fg + ft) % 4][:], ACT.Square).then_inc(S["squared_h"], 1)
                    if ft:
                        roots(ft - 1)
                    for m in mods_after("qkv", ft):
                        split(n + AHEAD)
                        n += 1
                roots(9)
                for q in range(2):
                    split(n + AHEAD)
                    n += 1
                act.wait_ge(S["qk_ready"], 10)
                for kt in range(2):
                    for j in range(2):
                        for half in range(2):
                            ins = nc.scalar.activation(kd[HD * half:HD * half + HD, 2 * kt + j, :],
                                                       qk[HD * j:HD * j + HD, 8 + kt, :], ACT.Copy)
                ins.then_inc(s_kd, 1)

            def qkv_plain(i, n, fg):
                S = att[i]
                for ft in range(16):
                    split(n + ft + AHEAD)
                    act.wait_ge(s_used, n + ft + 1)
                    dst, ps = qk[:, ft, :], bank[(fg + ft) % 4]
                    if i == 3 and ft < 8:
                        dst, source = mirrored(dst[:, CTX:T]), ps[:, CTX:T].rearrange("p (r c) -> p r c", c=GRID_W)
                    else:
                        source = ps[:]
                    nc.scalar.activation(dst, source, ACT.Identity,
                                         scale=SCALE if ft < 8 else 1.0).then_inc(s_free["act"], 1)
                for q in range(8):
                    split(n + 16 + q + AHEAD)

            def attention(i):
                S, U = att[i], attention_units(i)
                maps = 2 if i == 1 else 1
                per_o = len(U) // DT

                def copy_context(u):
                    if u < len(U):
                        act.wait_ge(S["biased"], u + 1)
                        nc.scalar.activation(p1[u % 3][:, 0:CTX], bank[u % 4][:, 0:CTX],
                                             ACT.Copy).then_inc(S["context_copied"], 1)

                if i == 3:
                    copy_context(0)
                for u in range(len(U) + 6):
                    if u < len(U):
                        hd, s, q0 = U[u]
                        nk = CTX if s == 0 else T
                        if u >= 3:
                            act.wait_ge(S["p_turned"], u - 2)
                        if i == 3:
                            copy_context(u + 1)
                        for m in range(maps):
                            act.wait_ge(S["negmax"], maps * u + m + 1)
                            b = bank[(2 * u + m) % 4] if maps == 2 else bank[u % 4]
                            dst = (p1, p2)[m][u % 3]
                            source = p1[u % 3] if i == 3 else b
                            nc.scalar.activation(dst[:, 0:nk], source[:, 0:nk], ACT.Exp,
                                                 bias=stat[:, m, u:u + 1],
                                                 accum_out=stat[:, 2 + m, u:u + 1]).then_inc(S["exped"], 1)
                    if 0 <= u - 2 < len(U):
                        w = u - 2
                        hd, s, q0 = U[w]
                        act.wait_ge(S["p_turned"], w + 1)
                        if w >= 4:
                            act.wait_ge(S["pv_full"], w // 2 - 1)
                        kt = 2 if s == 0 else 4
                        pb = bank[4] if i == 1 else bank[4 + w % 2]
                        nc.scalar.activation(pt[w // 2 % 2][:, 0:kt, P * (w % 2):P * (w % 2) + P],
                                             pb[:, 0:kt * P].rearrange("p (k q) -> p k q", k=kt),
                                             ACT.Copy).then_inc(S["pt_ready"], 1)
                    w = u - 5
                    if w >= 0 and w % per_o == per_o - 1:
                        o = w // per_o
                        c = slice(CTX, T) if i == 3 else slice(0, T)
                        act.wait_ge(S["pv_full"], (w + 1) // 2)
                        if i == 1:
                            nc.scalar.activation(sqb[:], bank[6 + o % 2][:], ACT.Square).then_inc(S["squared_h"], 1)
                            act.wait_ge(S["ss_full"], o + 1)
                            root(rsb[:], bank[5][:], 1.0 / (2 * HD)).then_inc(S["rs_ready"], 1)
                            act.wait_ge(S["o_normed"], o + 1)
                            nc.scalar.activation(h_hi[:, o, :], o32[:], ACT.Copy).then_inc(S["o_hi"], 1)
                        elif i == 0:
                            nc.scalar.activation(h_hi[:, o, :], bank[6 + o % 2][:], ACT.Copy).then_inc(S["o_hi"], 1)
                        else:
                            nc.scalar.activation(h_hi[:, o, c].rearrange("p (r c) -> p r c", c=GRID_W),
                                                 mirrored(bank[6 + o % 2][:, c]), ACT.Copy).then_inc(S["o_hi"], 1)

            def gate(S, u):
                b = 16 + C_HEADS * (u % 2) + u // 2
                act.wait_ge(S["gate_full"], u + 1)
                if u:
                    act.wait_ge(S["cum"], u)
                step.up(nc.scalar.activation(soft[:], bank[7][:], ACT.Abs, bias=small[:, b:b + 1]))
                act.wait_ge(s_act, step.n)
                step.up(nc.scalar.activation(soft[:], soft[:], ACT.Exp, scale=-1.0))
                act.wait_ge(s_act, step.n)
                nc.scalar.activation(soft[:], soft[:], ACT.Ln, bias=one).then_inc(S["gate_soft"], 1)

            def gla_tables():
                S = att[2]
                act.wait_ge(S["zeroed"], 1)
                act.dma_start(z_raw[:, :, 0:C_RANK], a["c_w_in"][0, :, 3072:3088].rearrange("(k p) c -> p k c", p=P)
                              ).then_inc(S["tables_in"], 16)
                act.dma_start(z_raw[:, :, 32:32 + C_RANK], a["c_w_in"][0, :, 3088:3104].rearrange("(k p) c -> p k c", p=P)
                              ).then_inc(S["tables_in"], 16)
                act.dma_start(w_gate[0:C_RANK, :], a["c_w_gate_fwd"][0]).then_inc(S["tables_in"], 16)
                act.dma_start(w_gate[32:32 + C_RANK, :], a["c_w_gate_bwd"][0]).then_inc(S["tables_in"], 16)
                act.dma_start(same_block[:], a["k_blocks"]).then_inc(S["tables_in"], 16)

            def qkv_gla(n, fg):
                S = att[2]
                for ft in range(8):
                    split(n + ft + AHEAD)
                    act.wait_ge(s_used, n + ft + 1)
                    nc.scalar.activation(qk[:, ft, :], bank[(fg + ft) % 4][:], ACT.Identity,
                                         scale=CH ** -0.5 if ft < 4 else 1.0).then_inc(s_free["act"], 1)
                    if ft == 3:
                        act.wait_ge(S["tables_in"], 80)
                        nc.scalar.activation(z_hi[:], z_raw[:], ACT.Copy).then_inc(S["z_hi"], 1)
                gate(S, 0)
                gate(S, 1)
                nc.scalar.preload_act_table_set("silu_and_others")
                for q in range(8):
                    split(n + 8 + q + AHEAD)
                for ft in range(8):
                    split(n + 16 + ft + AHEAD)
                    act.wait_ge(s_used, n + 16 + ft + 1)
                    nc.scalar.activation(qk[:, 8 + ft, :], bank[(fg + 16 + ft) % 4][:],
                                         ACT.Silu).then_inc(s_free["act"], 1)
                nc.scalar.preload_act_table_set("natural_log_exp_and_others")

            def gla():
                S = att[2]

                def decays(w, l0, l1):
                    hd, bwd, cw = item_of(w)
                    for l in range(l0, l1):
                        act.wait_ge(S["rel"], 8 * w + l + 1)
                        r = rel[(8 * w + l) % 3]
                        if l < LEVELS:
                            for is_q in (1, 0):
                                v = half(r[:], l, is_q ^ bwd)
                                ins = nc.scalar.activation(v, v, ACT.Exp, scale=(1 if is_q else -1) / C_NORMALIZER)
                        else:
                            if w >= 2:
                                act.wait_ge(S["state"], states(2 * w - 3))
                            nc.scalar.activation(r[:], r[:], ACT.Exp, scale=-1 / C_NORMALIZER)
                            ins = nc.scalar.activation(start_dec[w % 2][:], cum[w // 2 % 2][:, cw], ACT.Exp,
                                                       scale=1 / C_NORMALIZER)
                        ins.then_inc(S["decay"], 1)

                def key_end(c):
                    if c % 4 < 3:
                        act.wait_ge(S["turned"], states(c))
                        if c:
                            act.wait_ge(S["update_full"], states(c) - 1)
                        nc.scalar.activation(k_endT[:], bank[6][:, 0:CH], ACT.Copy).then_inc(S["k_endT"], 1)

                def head_squares(hd):
                    act.wait_ge(S["o_full"], 8 * hd + 8)
                    if hd:
                        act.wait_ge(S["o_lo"], 2 * hd)
                    nc.scalar.activation(o_head[0][:], bank[4][:], ACT.Copy).then_inc(S["o_copied_act"], 1)
                    act.wait_ge(S["o_copied_act"], hd + 1)
                    nc.scalar.activation(sq_head[0][:], o_head[0][:], ACT.Square)
                    act.wait_ge(S["o_copied_dve"], hd + 1)
                    nc.scalar.activation(sq_head[1][:], o_head[1][:], ACT.Square).then_inc(S["squared"], 1)

                def head_root(hd):
                    act.wait_ge(S["ss_full"], hd + 1)
                    root(rstd[:], bank[6][:], 1.0 / C_HV).then_inc(S["rs_ready"], 1)

                def head_hi(hd):
                    for v in range(2):
                        act.wait_ge(S["o_gated"], 2 * hd + v + 1)
                        nc.scalar.activation(h_hi[:, 2 * hd + v, :], o_head[v][:], ACT.Copy).then_inc(S["o_hi"], 1)

                decays(0, 0, 8)
                decays(1, 0, 4)
                for w in range(C_ITEMS):
                    if gates_at(w):
                        gate(S, gates_at(w))
                    key_end(2 * w)
                    if w + 1 < C_ITEMS:
                        decays(w + 1, 4, 8)
                    if w % 4 == 0 and w:
                        head_root(w // 4 - 1)
                    key_end(2 * w + 1)
                    if w + 2 < C_ITEMS:
                        decays(w + 2, 0, 4)
                    if w % 4 == 0 and w:
                        head_hi(w // 4 - 1)
                    if w % 4 == 3:
                        head_squares(w // 4)
                head_root(C_HEADS - 1)
                head_hi(C_HEADS - 1)

            for n in range(AHEAD):
                split(n)
            act.wait_ge(s_lam_d, 1)
            nc.scalar.activation(small[:, 11:13], bank[5][:, 0:2], ACT.Exp).then_inc(s_lam_e, 1)
            act.wait_ge(s_cond_t, 1)
            nc.scalar.activation(cond[:].rearrange("p s k -> p (s k)"), bank[4][:, 0:16], ACT.Silu).then_inc(s_cond_a, 1)
            act.wait_ge(s_cond_a, 1)
            for s in range(2):
                ins = nc.scalar.activation(cond4[:, :, 2 * s], cond[:, s, :], ACT.Copy)
            ins.then_inc(s_cond_a, 1)
            for n in range(16):
                split(n + AHEAD)
            for i in range(layers):
                st = 2 * i
                nc.scalar.preload_act_table_set("natural_log_exp_and_others")
                make_h(st, cols(i, "head"))
                n, fg = start["qkv", i]
                if i == 0:
                    qkv_norm_rope(n, fg)
                elif i == 2:
                    gla_tables()
                    qkv_gla(n, fg)
                else:
                    if i == 3:
                        for par in range(2):
                            for r in range(6):
                                act.dma_start(bias[64 * par:64 * par + 64, :, GRID_W * r:GRID_W * r + GRID_W],
                                              rpb_block((5, 4)[par] + r)).then_inc(s_bias_in, 16)
                        act.dma_start(window[:], a["k_window"]).then_inc(s_bias_in, 16)
                    qkv_plain(i, n, fg)
                gla() if i == 2 else attention(i)
                n, fg = start["wo", i]
                residual(st, n, fg, 1, cols(i, "tail"))
                make_h(st + 1, cols(i, "tail"))
                nc.scalar.preload_act_table_set("silu_and_others")
                c = cols(i, "tail")
                n, fg = start["up", i]
                per = 8 if i + 1 < layers else 4

                def round_product(j, u):
                    act.wait_ge(s_gmul, FT * i + 1 + j)
                    nc.scalar.activation(g_hi[:, bass.ds(j, 1), c], g32[u][:, c].unsqueeze(1),
                                         ACT.Copy).then_inc(s_ghi, 1)

                def two_tiles(it, first=False):
                    for u in range(2):
                        for k in range(2):
                            at_slab = n + per // 2 * u + k
                            split(at_slab + AHEAD, it, per)
                            act.wait_ge(s_used, at_slab + 1 + per * it)
                            tile = FT * k + u + 2 * it
                            nc.scalar.activation(
                                conv[k][u][:, c], bank[2 * u + k][:, c], ACT.Identity,
                                bias=prm[:, bass.ds(R_LAYER * i + R_CB + tile, 1)],
                                scale=prm[:, bass.ds(R_LAYER * i + R_CW + 2 * FT + tile, 1)]).then_inc(s_tap1, 1)
                            if k == 0:
                                act.wait_ge(s_free["dve"], freed[fg][1] + 2 * u + 4 * it)
                                nc.scalar.activation(conv[0][u][:, c], conv[0][u][:, c], ACT.Silu).then_inc(s_silu, 1)
                            if k == 0 and not (first and u == 0):
                                round_product(2 * it - 1 + u, 1 - u)
                        for q in range(2 if per == 8 else 0):
                            split(n + 4 * u + 2 + q + AHEAD, it, per)

                two_tiles(0, first=True)
                with act.Fori(1, FT // 2) as it:
                    two_tiles(it)
                round_product(FT - 1, 1)
                for q in range(PREMOD if per == 8 else 0):
                    split(start["postmod", i][0] + q + AHEAD)
                n, fg = start["down", i]
                residual(st + 1, n, fg, 3, c)
            for k in range(DT):
                act.wait_ge(s_xn, DT * 2 * layers + k + 1)
                g, b = gain(2 * layers)
                nc.scalar.activation(out_f[:, k, :], xn[:, k, CTX:T], ACT.Identity, bias=b[:, k:k + 1],
                                     scale=g[:, k:k + 1]).then_inc(s_outf, 1)

        @block.vector
        def _(dve):
            step = Count(s_dve)

            def link(ins):
                step.up(ins)
                dve.wait_ge(s_dve, step.n)

            def split(n, it=0, per=0):
                if n >= n_slabs:
                    return
                slot = n % SLOTS
                dve.wait_ge(s_hi, n + 1 + per * it)
                w = SLAB if per else width(slabs[n])
                nc.vector.tensor_tensor(wlo[slot][:, 0:w], raw[slot][:, 0:w], whi[slot][:, 0:w].bitcast(f32),
                                        ALU.subtract).then_inc(s_lo, 1)

            def mod_row_copy(group, n):
                dve.wait_ge(s_used, n + 1)
                if group:
                    dve.wait_ge(s_mod_t, group)
                nc.vector.tensor_copy(mod_row[:], MOD_ACC[0:4, :]).then_inc(s_mod_row, 1)

            def mod_evacuate(i, c0, c1, turned):
                dve.wait_ge(s_mod_t, turned)
                v = MOD_T[:, 0:N_MOD * DT * 2].rearrange("p (c s) -> p c s", s=2)
                for s in range(2):
                    ins = nc.vector.tensor_tensor(modT[i % 2][:, c0:c1, s], v[:, c0:c1, s],
                                                  prm[:, R_LAYER * i + c0:R_LAYER * i + c1], ALU.add)
                ins.then_inc(s_mod_in, 1)

            def coefficients(st, events):
                dve.wait_ge(s_mod_in, events)
                cf, m = coef[st % 2], modT[st // 2 % 2]
                g, b = gain(st)
                sh, sc = mod(st, 0), mod(st, 1)
                for s in range(2):
                    nc.vector.scalar_tensor_tensor(cf[:, s, :], m[:, sc:sc + DT, s], 1.0, g, ALU.add, ALU.mult)
                    ins = nc.vector.scalar_tensor_tensor(cf[:, 2 + s, :], m[:, sc:sc + DT, s], 1.0, b, ALU.add, ALU.mult)
                link(ins)
                nc.vector.tensor_scalar(cf[:, 4, :], g, ALPHA, None, ALU.mult)
                nc.vector.tensor_scalar(cf[:, 5, :], b, ALPHA, None, ALU.mult)
                for s in range(2):
                    ins = nc.vector.tensor_tensor(cf[:, 2 + s, :], cf[:, 2 + s, :], m[:, sh:sh + DT, s], ALU.add)
                ins.then_inc(s_coef, 1)

            def scale_xn(st, k, c):
                dve.wait_ge(s_cen, DT * (st - 1) + k + 1)
                if k == 0:
                    dve.wait_ge(s_rstd, st)
                nc.vector.tensor_tensor(xn[:, k, c], xn[:, k, c], rstd[:, c], ALU.mult).then_inc(s_xn, 1)

            def make_h(st, c):
                if st:
                    scale_xn(st, 0, c)
                for k in range(DT):
                    if st and k + 1 < DT:
                        scale_xn(st, k + 1, c)
                    dve.wait_ge(s_hhi, DT * st + k + 1)
                    nc.vector.tensor_tensor(h_lo[:, k, c], res_t[k % 2][:, c], h_hi[:, k, c].bitcast(f32),
                                            ALU.subtract).then_inc(s_hlo, 1)

            def residual(st, n, fg, per, c):

                def add_square(dt):
                    dve.wait_ge(s_sqd, DT * st + dt + 1)
                    if dt >= 2:
                        dve.wait_ge(s_qsum, 7 * st + dt - 1)
                    nc.vector.tensor_tensor(acc_q[:, c], acc_q[:, c], sq[:, c], ALU.add).then_inc(s_qsum, 1)

                for dt in range(DT):
                    for q in range(per):
                        split(n + q + AHEAD)
                    n += per
                    dve.wait_ge(s_free["act"], freed[fg + dt][1])
                    nc.vector.scalar_tensor_tensor(xn[:, dt, c], xn[:, dt, c], coef[st % 2][:, 4, dt:dt + 1],
                                                   res_t[dt % 2][:, c], ALU.mult, ALU.add).then_inc(s_y, 1)
                    if dt >= 2:
                        add_square(dt - 1)
                    for m in mods_after("wo", dt) if st == 0 else ():
                        split(n + AHEAD)
                        n += 1
                        if m % 4 == 3:
                            mod_row_copy(4 + m // 4, n - 1)
                if st == 0:
                    mod_evacuate(0, 36, 48, 12)
                add_square(DT - 1)
                if st % 2 == 0 and st // 2 + 1 < layers:
                    for q in range(PREMOD):
                        split(n + q + AHEAD)
                dve.wait_ge(s_stats, st + 1)
                nc.vector.tensor_scalar(mean[:, c], LN_SUM[:, c], 1.0 / D, None, ALU.mult).then_inc(s_mean, 1)
                dve.wait_ge(s_mean, st + 1)
                link(nc.vector.scalar_tensor_tensor(acc_s[:, c], mean[:, c], -1.0, mean[:, c], ALU.mult, ALU.mult))
                link(nc.vector.scalar_tensor_tensor(acc_q[:, c], LN_SQ[:, c], 1.0 / D, acc_s[:, c], ALU.mult, ALU.add))
                nc.vector.tensor_scalar(acc_q[:, c], acc_q[:, c], 0.0, LN_EPS, ALU.max, ALU.add).then_inc(s_var, 1)

            def v_out(n, fg, groups):
                for g in range(groups):
                    for q in range(2):
                        split(n + 2 * g + q + AHEAD)
                    dve.wait_ge(s_used, n + 2 * g + 2)
                    for half in range(2):
                        nc.vector.tensor_copy(v_tok[:, 2 * half:2 * half + 2, 256 * g:256 * g + 256],
                                              bank[(fg + 2 * g + half) % 4][:].rearrange("p (t c) -> p t c", t=2)
                                              ).then_inc(s_free["dve"], 1)

            def rope(S, ft, ps, tmp):
                dve.wait_ge(S["swapped"], ft + 1)
                if ft:
                    dve.wait_ge(S["qk_ready"], ft)
                nc.vector.tensor_tensor(tmp[:], ps, sin, ALU.mult)
                link(nc.vector.tensor_tensor(qk[:, ft, CTX:T], qk[:, ft, CTX:T], cos, ALU.mult))
                nc.vector.tensor_tensor(qk[:, ft, CTX:T], qk[:, ft, CTX:T], tmp[:], ALU.add).then_inc(S["qk_ready"], 1)

            def qkv_norm_rope(n, fg):
                S = att[0]

                def norm(ft):
                    dve.wait_ge(S["rs_ready"], ft + 1)
                    nc.vector.scalar_tensor_tensor(qk[:, ft, :], bank[(fg + ft) % 4][:],
                                                   small[:, 14:15] if ft < 8 else small[:, 1:2],
                                                   rsa[ft % 2][:], ALU.mult, ALU.mult).then_inc(s_free["dve"], 1)

                for ft in range(10):
                    split(n + AHEAD)
                    n += 1
                    if ft >= 1:
                        norm(ft - 1)
                    if ft >= 2:
                        rope(S, ft - 2, bank[5][:, 0:LAT], rope_t)
                    for m in mods_after("qkv", ft):
                        split(n + AHEAD)
                        n += 1
                        if m % 4 == 3:
                            mod_row_copy(4 + m // 4, n - 1)
                norm(9)
                mod_evacuate(0, 16, 36, 9)
                rope(S, 8, bank[5][:, 0:LAT], rope_t)
                rope(S, 9, bank[5][:, 0:LAT], rope_t)
                v_out(n, fg + 10, 1)

            def qkv_plain(i, n, fg):
                S = att[i]
                for ft in range(16):
                    split(n + ft + AHEAD)
                    if i == 1 and ft >= 1:
                        rope(S, ft - 1, bank[4 + (ft - 1) % 2][:, 0:LAT], rope_b)
                if i == 1:
                    rope(S, 15, bank[5][:, 0:LAT], rope_b)
                v_out(n + 16, fg + 16, 4)

            def attention(i):
                S, U = att[i], attention_units(i)
                maps = 2 if i == 1 else 1
                per_o = len(U) // DT

                def add_bias(u):
                    if u < len(U):
                        hd, s, q0 = U[u]
                        dve.wait_ge(S["score_full"], u + 1)
                        if u >= 3:
                            dve.wait_ge(S["p_turned"], u - 2)
                        r = 2 * GRID_W if q0 == CTX else 0
                        nc.vector.tensor_tensor(p1[u % 3][:, CTX:T], bank[u % 4][:, CTX:T],
                                                bias[:, hd, r:r + LAT], ALU.add).then_inc(S["biased"], 1)

                if i == 3:
                    add_bias(0)
                for u in range(len(U) + 6):
                    if u < len(U):
                        hd, s, q0 = U[u]
                        nk = CTX if s == 0 else T
                        if i == 3:
                            add_bias(u + 1)
                            dve.wait_ge(S["biased"], u + 1)
                            dve.wait_ge(S["context_copied"], u + 1)
                            nc.vector.tensor_reduce(stat[:, 0, u:u + 1], p1[u % 3][:], AX, ALU.max,
                                                    negate=True).then_inc(S["negmax"], 1)
                        else:
                            for m in range(maps):
                                dve.wait_ge(S["score_full"], maps * u + m + 1)
                                b = bank[(2 * u + m) % 4] if maps == 2 else bank[u % 4]
                                nc.vector.tensor_reduce(stat[:, m, u:u + 1], b[:, 0:nk], AX, ALU.max,
                                                        negate=True).then_inc(S["negmax"], 1)
                    w = u - 1
                    if 0 <= w < len(U):
                        nk = CTX if U[w][1] == 0 else T
                        dve.wait_ge(S["exped"], maps * (w + 1))
                        for m in range(maps):
                            ins = nc.vector.reciprocal(stat[:, 4 + m, w:w + 1], stat[:, 2 + m, w:w + 1])
                        link(ins)
                        r1 = stat[:, 4, w:w + 1]
                        if maps == 1:
                            nc.vector.tensor_scalar(p1[w % 3][:, 0:nk], p1[w % 3][:, 0:nk], r1, None,
                                                    ALU.mult).then_inc(S["p_ready"], 1)
                        else:
                            nc.vector.tensor_scalar(p1[w % 3][:, 0:nk], p1[w % 3][:, 0:nk], r1, None, ALU.mult)
                            link(nc.vector.tensor_tensor(stat[:, 5, w:w + 1], stat[:, 5, w:w + 1], small[:, 13:14],
                                                         ALU.mult))
                            nc.vector.scalar_tensor_tensor(p1[w % 3][:, 0:nk], p2[w % 3][:, 0:nk],
                                                           stat[:, 5, w:w + 1], p1[w % 3][:, 0:nk],
                                                           ALU.mult, ALU.add).then_inc(S["p_ready"], 1)
                    w = u - 5
                    if w >= 0 and w % per_o == per_o - 1:
                        o = w // per_o
                        c = slice(CTX, T) if i == 3 else slice(0, T)
                        if i == 1:
                            dve.wait_ge(S["rs_ready"], o + 1)
                            if o:
                                dve.wait_ge(S["o_lo"], o)
                            nc.vector.scalar_tensor_tensor(o32[:], bank[6 + o % 2][:], small[:, 15:16], rsb[:],
                                                           ALU.mult, ALU.mult).then_inc(S["o_normed"], 1)
                        dve.wait_ge(S["o_hi"], o + 1)
                        lo, source, hi = h_lo[:, o, c], (o32 if i == 1 else bank[6 + o % 2])[:, c], h_hi[:, o, c].bitcast(f32)
                        if i == 3:
                            rows_of = "p (r c) -> p r c"
                            lo, source, hi = lo.rearrange(rows_of, c=GRID_W), mirrored(source), hi.rearrange(rows_of, c=GRID_W)
                        nc.vector.tensor_tensor(lo, source, hi, ALU.subtract).then_inc(S["o_lo"], 1)

            def gate(S, u):
                b = 16 + C_HEADS * (u % 2) + u // 2
                dve.wait_ge(S["gate_soft"], u + 1)
                if u:
                    dve.wait_ge(S["cum"], u)
                nc.vector.tensor_scalar(gate_min[:], bank[7][:], small[:, b:b + 1], 0.0, ALU.add,
                                        ALU.min).then_inc(S["gate_min"], 1)

            def gate_sums(S, u):
                bwd = u % 2
                if u >= 2:
                    dve.wait_ge(S["decay"], 16 * (u - 1))
                dve.wait_ge(S["gate_min"], u + 1)
                link(nc.vector.tensor_tensor(gate_min[:], gate_min[:], soft[:], ALU.subtract))
                for c in range(4):
                    v = slice(CH * c, CH * c + CH)
                    src_c, dst_c = gate_min[:, v], cum[u % 2][:, v]
                    if bwd:
                        src_c, dst_c = src_c[:, ::-1], dst_c[:, ::-1]
                    ins = nc.vector.tensor_tensor_scan(dst_c, ones, src_c, 0.0, ALU.mult, ALU.add)
                ins.then_inc(S["cum"], 1)

            def qkv_gla(n, fg):
                S = att[2]
                for ft in range(8):
                    split(n + ft + AHEAD)
                    if ft == 3:
                        dve.wait_ge(S["z_hi"], 1)
                        nc.vector.tensor_tensor(z_lo[:], z_raw[:], z_hi[:].bitcast(f32), ALU.subtract).then_inc(S["z_lo"], 1)
                dve.wait_ge(S["z_full"], 1)
                nc.vector.tensor_copy(zT[:], bank[4][0:64, :]).then_inc(S["z_copied"], 1)
                for u in range(2):
                    gate(S, u)
                    gate_sums(S, u)
                v_out(n + 8, fg + 8, 4)
                for ft in range(8):
                    split(n + 16 + ft + AHEAD)

            def gla():
                S = att[2]

                def query(w, l):
                    hd, bwd, cw = item_of(w)
                    j = 8 * w + l
                    dve.wait_ge(S["decay"], j + 1)
                    if l < LEVELS:
                        if l == 0 and w >= 2:
                            dve.wait_ge(S["score_full"], 2 * w - 2)
                        dst = (left if bwd else right)[w % 2][:, l, :]
                        nc.vector.tensor_tensor(half(dst, l, not bwd), half(qk[:, hd, cw], l, not bwd),
                                                half(rel[j % 3][:], l, not bwd), ALU.mult).then_inc(S["q_dec"], 1)
                    else:
                        if w >= 2:
                            dve.wait_ge(S["o_full"], 2 * w - 2)
                        nc.vector.tensor_tensor(q_dec[w % 2][:], qk[:, hd, cw], start_dec[w % 2][:],
                                                ALU.mult).then_inc(S["q_dec"], 1)

                def build(w, l0, l1):
                    for l in range(l0, l1):
                        query(w, l)

                def add_levels(c):
                    dve.wait_ge(S["score_full"], c + 1)
                    if c >= 2:
                        dve.wait_ge(S["scores"], c - 1)
                    for h, v in enumerate((slice(0, 4), slice(4, PLANES))):
                        ps = bank[2 * (c % 2) + h][:].rearrange("p (l i) -> p l i", l=4)
                        ins = nc.vector.tensor_tensor(masked[c % 2][:, v, :], ps[:, 0:v.stop - v.start, :],
                                                      same_block[:, v, :], ALU.mult)
                    ins.then_inc(S["masked"], 1)
                    dve.wait_ge(S["masked"], c + 1)
                    if c:
                        dve.wait_ge(S["o_full"], c)
                    nc.vector.tensor_reduce(scores[:], masked[c % 2][:].rearrange("p l i -> p i l"), AX,
                                            ALU.add).then_inc(S["scores"], 1)

                def next_state(c):
                    if c % 4 == 3:
                        return
                    hd, bwd, p, ci, cs = chunk_of(c)
                    dve.wait_ge(S["update_full"], states(c))
                    if c % 4 == 0:
                        nc.vector.tensor_copy(state[0][:], bank[7][:, 0:C_HV]).then_inc(S["state"], 1)
                    else:
                        dve.wait_ge(S["state"], states(c) - 1)
                        end = ci.start if bwd else ci.stop - 1
                        nc.vector.scalar_tensor_tensor(state[c % 4 % 2][:], state[(c % 4 - 1) % 2][:],
                                                       start_dec[c // 2 % 2][:, end:end + 1], bank[7][:, 0:C_HV],
                                                       ALU.mult, ALU.add).then_inc(S["state"], 1)

                def head_copy(hd):
                    dve.wait_ge(S["o_full"], 8 * hd + 8)
                    if hd:
                        dve.wait_ge(S["o_lo"], 2 * hd)
                    nc.vector.tensor_copy(o_head[1][:], bank[5][:]).then_inc(S["o_copied_dve"], 1)

                def head_gated(hd):
                    dve.wait_ge(S["rs_ready"], hd + 1)
                    for v in range(2):
                        nc.vector.scalar_tensor_tensor(o_head[v][:], o_head[v][:], small[:, 3 + v:4 + v], rstd[:],
                                                       ALU.mult, ALU.mult).then_inc(S["o_normed"], 1)
                    for v in range(2):
                        dve.wait_ge(S["o_normed"], 2 * hd + v + 1)
                        nc.vector.tensor_tensor(o_head[v][:], o_head[v][:], qk[:, 8 + 2 * hd + v, :],
                                                ALU.mult).then_inc(S["o_gated"], 1)

                def head_lo(hd):
                    for v in range(2):
                        dve.wait_ge(S["o_hi"], 2 * hd + v + 1)
                        nc.vector.tensor_tensor(h_lo[:, 2 * hd + v, :], o_head[v][:],
                                                h_hi[:, 2 * hd + v, :].bitcast(f32), ALU.subtract).then_inc(S["o_lo"], 1)

                dve.wait_ge(s_free["act"], freed[start["qkv", 2][1] + 7][1])
                dve.wait_ge(S["zeroed"], 2)
                build(0, 0, 8)
                build(1, 0, 4)
                for w in range(C_ITEMS):
                    add_levels(2 * w)
                    if gates_at(w):
                        gate(S, gates_at(w))
                    if w + 1 < C_ITEMS:
                        build(w + 1, 4, 8)
                    if gates_at(w):
                        gate_sums(S, gates_at(w))
                    next_state(2 * w)
                    add_levels(2 * w + 1)
                    if w + 2 < C_ITEMS:
                        build(w + 2, 0, 4)
                    next_state(2 * w + 1)
                    if w % 4 == 0 and w:
                        head_gated(w // 4 - 1)
                    if w % 4 == 1 and w > 1:
                        head_lo(w // 4 - 1)
                    if w % 4 == 3:
                        head_copy(w // 4)
                head_gated(C_HEADS - 1)
                head_lo(C_HEADS - 1)

            nc.vector.memset(unit_gb[:, 0, :], 1.0)
            link(nc.vector.memset(unit_gb[:, 1, :], 0.0))
            dve.wait_ge(s_cond_t, 2)
            link(nc.vector.tensor_copy(small[:], bank[5][:, 0:32]))
            nc.vector.tensor_tensor(small[0:HD, 9:10], small[0:HD, 5:6], small[0:HD, 6:7], ALU.mult)
            nc.vector.tensor_tensor(small[0:HD, 10:11], small[0:HD, 7:8], small[0:HD, 8:9], ALU.mult).then_inc(s_lam_p, 1)
            nc.vector.tensor_scalar(small[:, 14:15], small[:, 0:1], SCALE, None, ALU.mult)
            link(nc.vector.tensor_scalar(small[:, 15:16], small[:, 2:3], 1.0 - LAM_INIT, None, ALU.mult))
            dve.wait_ge(s_lam_e, 1)
            link(nc.vector.tensor_tensor(small[:, 13:14], small[:, 12:13], small[:, 11:12], ALU.subtract))
            link(nc.vector.tensor_scalar(small[:, 13:14], small[:, 13:14], LAM_INIT, None, ALU.subtract))
            for n in range(AHEAD):
                split(n)
            dve.wait_ge(s_cond_a, 2)
            for s in range(2):
                ins = nc.vector.tensor_tensor(cond4[:, :, 2 * s + 1], cond[:, s, :],
                                              cond4[:, :, 2 * s].bitcast(f32), ALU.subtract)
            ins.then_inc(s_cond_v, 1)
            for b in range(2):
                dve.wait_ge(s_rows_t, b + 1)
                nc.vector.tensor_copy(prm[:, NB * b:NB * b + NB], bank[2 + b][:]).then_inc(s_rows_v, 1)
            dve.wait_ge(s_rows_v, 2)
            for k in range(DT):
                dve.wait_ge(s_tok_t, k + 1)
                nc.vector.tensor_copy(xn[:, k, :], bank[k % 2][:]).then_inc(s_xn, 1)
            for g in range(4):
                for q in range(4):
                    split(4 * g + q + AHEAD)
                mod_row_copy(g, 4 * g + 3)
            mod_evacuate(0, 0, 16, 4)
            for i in range(layers):
                st = 2 * i
                coefficients(st, mod_events(i, 0))
                make_h(st, cols(i, "head"))
                n, fg = start["qkv", i]
                if i == 0:
                    qkv_norm_rope(n, fg)
                elif i == 2:
                    qkv_gla(n, fg)
                else:
                    qkv_plain(i, n, fg)
                gla() if i == 2 else attention(i)
                n, fg = start["wo", i]
                c = cols(i, "tail")
                residual(st, n, fg, 1, c)
                coefficients(st + 1, mod_events(i, 2))
                make_h(st + 1, c)
                n, fg = start["up", i]
                per = 8 if i + 1 < layers else 4
                base = freed[fg][1] - 1

                def round_rest(j, u):
                    dve.wait_ge(s_ghi, FT * i + 1 + j)
                    nc.vector.tensor_tensor(g_lo[:, bass.ds(j, 1), c], g32[u][:, c].unsqueeze(1),
                                            g_hi[:, bass.ds(j, 1), c].bitcast(f32), ALU.subtract).then_inc(s_glo, 1)

                def two_tiles(it, first=False):
                    for u in range(2):
                        for k in range(2):
                            at_slab = n + per // 2 * u + k
                            split(at_slab + AHEAD, it, per)
                            if per == 8 and u == 1 and k == 0:
                                dve.wait_ge(s_used, n + 4 + per * it)
                                dve.wait_ge(s_mod_t, 12 * (i + 1) + it)
                                nc.vector.tensor_copy(mod_row[:], MOD_ACC[0:4, :]).then_inc(s_mod_row, 1)
                            group = 2 * u + k
                            dve.wait_ge(s_tap1, 2 * FT * i + group + 1 + 4 * it)
                            w = R_LAYER * i + R_CW + FT * k + u + 2 * it
                            runs = "p (s t) -> p s t"
                            ps = bank[group][:, c].rearrange(runs, t=LAT)
                            dst = conv[k][u][:, c].rearrange(runs, t=LAT)
                            nc.vector.scalar_tensor_tensor(dst[:, :, 1:LAT], ps[:, :, 0:LAT - 1], prm[:, bass.ds(w, 1)],
                                                           dst[:, :, 1:LAT], ALU.mult, ALU.add).then_inc(s_tap2, 1)
                            dve.wait_ge(s_tap2, 2 * FT * i + group + 1 + 4 * it)
                            nc.vector.scalar_tensor_tensor(dst[:, :, 0:LAT - 1], ps[:, :, 1:LAT],
                                                           prm[:, bass.ds(4 * FT + w, 1)],
                                                           dst[:, :, 0:LAT - 1], ALU.mult, ALU.add).then_inc(s_free["dve"], 1)
                            if k == 0 and not (first and u == 0):
                                round_rest(2 * it - 1 + u, 1 - u)
                        if per == 8:
                            for q in range(2):
                                split(n + 4 * u + 2 + q + AHEAD, it, per)

                two_tiles(0, first=True)
                with dve.Fori(1, FT // 2) as it:
                    two_tiles(it)
                round_rest(FT - 1, 1)
                if i + 1 < layers:
                    n, fg = start["postmod", i]
                    for q in range(PREMOD):
                        split(n + q + AHEAD)
                    mod_row_copy(12 * (i + 1) + 11, n + 1)
                    mod_evacuate(i + 1, 0, N_MOD * DT, 12 * (i + 2))
                n, fg = start["down", i]
                residual(st + 1, n, fg, 3, c)
            for k in range(DT):
                scale_xn(2 * layers, k, slice(CTX, T))
            for q in range(4):
                dve.wait_ge(s_outt, q + 1)
                nc.vector.tensor_copy(out_tok[:, q // 2, NB * (q % 2):NB * (q % 2) + NB], bank[q][:]).then_inc(s_outv, 1)

        @block.gpsimd
        def _(pool):
            def residual(st, c):
                for dt in range(DT):
                    pool.wait_ge(s_y, DT * st + dt + 1)
                    if dt == 0:
                        nc.gpsimd.tensor_copy(acc_s[:, c], xn[:, 0, c]).then_inc(s_sum, 1)
                    else:
                        pool.wait_ge(s_sum, DT * st + dt)
                        nc.gpsimd.tensor_tensor(acc_s[:, c], acc_s[:, c], xn[:, dt, c], ALU.add).then_inc(s_sum, 1)
                pool.wait_ge(s_mean, st + 1)
                for k in range(DT):
                    nc.gpsimd.tensor_tensor(xn[:, k, c], xn[:, k, c], mean[:, c], ALU.subtract).then_inc(s_cen, 1)

            def gla():
                S = att[2]
                nc.gpsimd.memset(z_raw[:], 0.0).then_inc(S["zeroed"], 1)
                for s in range(2):
                    nc.gpsimd.memset(right[s][:], 0.0)
                    ins = nc.gpsimd.memset(left[s][:], 0.0)
                ins.then_inc(S["zeroed"], 1)
                pool.wait_ge(S["zeroed"], 2)
                pool.wait_ge(s_free["act"], freed[start["qkv", 2][1] + 7][1])

                def relative(w, l):
                    hd, bwd, cw = item_of(w)
                    j = 8 * w + l
                    if j >= 3:
                        pool.wait_ge(S["k_dec"], j - 2)
                        pool.wait_ge(S["q_dec"], j - 2)
                    if w % 2 == 0 and l == 0:
                        pool.wait_ge(S["cum"], w // 2 + 1)
                    s = 64 >> min(l, 6)
                    n2 = 2 * s if l < LEVELS else CH
                    ref = (s if bwd else s - 1) if l < LEVELS else (0 if bwd else CH - 1)
                    v = cum[w // 2 % 2][:, cw].rearrange("p (n s) -> p n s", s=n2)
                    nc.gpsimd.tensor_tensor(rel[j % 3][:].rearrange("p (n s) -> p n s", s=n2), v,
                                            v[:, :, ref:ref + 1].broadcast_to([P, 2 * CH // n2, n2]),
                                            ALU.subtract).then_inc(S["rel"], 1)

                relative(0, 0)
                relative(0, 1)
                for w in range(C_ITEMS):
                    hd, bwd, cw = item_of(w)
                    for l in range(8):
                        j = 8 * w + l
                        if j + 2 < 8 * C_ITEMS:
                            relative((j + 2) // 8, (j + 2) % 8)
                        pool.wait_ge(S["decay"], j + 1)
                        if l < LEVELS:
                            if l == 0 and w >= 2:
                                pool.wait_ge(S["score_full"], 2 * w - 2)
                            dst = (right if bwd else left)[w % 2][:, l, :]
                            nc.gpsimd.tensor_tensor(half(dst, l, bwd), half(qk[:, 4 + hd, cw], l, bwd),
                                                    half(rel[j % 3][:], l, bwd), ALU.mult).then_inc(S["k_dec"], 1)
                        else:
                            if w >= 2:
                                pool.wait_ge(S["turned"], states(2 * w - 3))
                            nc.gpsimd.tensor_tensor(k_end[w % 2][:], qk[:, 4 + hd, cw], rel[j % 3][:],
                                                    ALU.mult).then_inc(S["k_dec"], 1)

            for i in range(layers):
                c = cols(i, "tail")
                if i == 2:
                    gla()
                if i == 3:
                    pool.wait_ge(s_bias_in, 16 * 13)
                    v = bias[:].rearrange("p h (r c) -> p (h r) c", c=GRID_W)
                    nc.gpsimd.tensor_tensor(v, v, window[:].unsqueeze(1).broadcast_to([P, 6 * D_HEADS, GRID_W]),
                                            ALU.add).then_inc(s_window, 1)
                residual(2 * i, c)
                n, fg = start["up", i]
                with pool.Fori(0, FT // 2) as it:
                    for u in range(2):
                        pool.wait_ge(s_silu, FT * i + u + 1 + 2 * it)
                        pool.wait_ge(s_free["dve"], freed[fg][1] + 2 * u + 1 + 4 * it)
                        nc.gpsimd.tensor_tensor(g32[u][:, c], conv[0][u][:, c], conv[1][u][:, c],
                                                ALU.mult).then_inc(s_gmul, 1)
                residual(2 * i + 1, c)

        @block.tensor
        def _(pe):
            mm = nc.tensor.matmul

            def three(out, w_hi, w_lo, x_hi, x_lo, first, last, moving_w=False):
                for n, (w, x) in enumerate(((w_hi, x_hi), (w_hi, x_lo), (w_lo, x_hi))):
                    l, r = (x, w) if moving_w else (w, x)
                    ins = mm(out, l, r, start=first and n == 0, stop=last and n == 2)
                return ins

            def split_ready(n, it=0, per=0):
                pe.wait_ge(s_hi, n + 1 + per * it)
                pe.wait_ge(s_lo, n + 1 + per * it)

            def project_pair(n, outs, x_hi, x_lo, c, ready):
                split_ready(n + 1)
                for k in range(DT):
                    pe.wait_ge(ready[0], ready[1] + k + 1)
                    for j in range(2):
                        slot, wc = (n + j) % SLOTS, slice(k * P, (k + 1) * P)
                        ins = three(outs[j][:, c], whi[slot][:, wc], wlo[slot][:, wc], x_hi[:, k, c], x_lo[:, k, c],
                                    k == 0, k == DT - 1)
                        if k == DT - 1:
                            ins.then_inc(s_used, 1)

            def project(n, out, x_hi, x_lo, c, k0=0, nk=8, first=True, last=True, ready=None, it=0, per=0):
                split_ready(n, it, per)
                slot = n % SLOTS
                for k in range(nk):
                    if ready:
                        pe.wait_ge(ready[0], ready[1] + k0 + k + 1)
                    wc = slice(k * P, (k + 1) * P)
                    ins = three(out[:, c], whi[slot][:, wc], wlo[slot][:, wc], x_hi[:, k0 + k, c], x_lo[:, k0 + k, c],
                                first and k == 0, last and k == nk - 1)
                ins.then_inc(s_used, 1)

            def group_free(fg):
                if fg >= 4:
                    who, count = freed[fg - 4]
                    pe.wait_ge(s_free[who], count)

            def mod_slab(n, group, q, it=0, per=0):
                split_ready(n, it, per)
                if q == 0 and group:
                    pe.wait_ge(s_mod_row, group + it)
                slot = n % SLOTS
                for k in range(2):
                    for part, w in enumerate((whi, wlo)):
                        ins = mm(MOD_ACC[0:4, :], cond4[:, 2 * q + k, :], w[slot][:, NB * k:NB * k + NB],
                                 start=q == 0 and k == 0 and part == 0, stop=q == 3 and k == 1 and part == 1)
                ins.then_inc(s_used, 1)

            def mod_turn(group, it=0):
                pe.wait_ge(s_mod_row, group + 1 + it)
                g = group % 12
                if group in (4, 9):
                    pe.wait_ge(s_mod_in, 1 if group == 4 else 2)
                elif group >= 12 and g == 0 and isinstance(it, int):
                    pe.wait_ge(s_mod_in, group // 12 + 2)
                for b in range(4):
                    ins = mm(MOD_T[:, bass.ds(8 * g + 2 * b + 8 * it, 2)], mod_row[:, b * P:(b + 1) * P], sel,
                             start=True, stop=True)
                ins.then_inc(s_mod_t, 1)

            def stats(st, c):
                pe.wait_ge(s_sum, DT * (st + 1))
                mm(LN_SUM[:, c], ones, acc_s[:, c], start=True, stop=True)
                pe.wait_ge(s_qsum, 7 * (st + 1))
                mm(LN_SQ[:, c], ones, acc_q[:, c], start=True, stop=True).then_inc(s_stats, 1)

            def v_project(n, fg, groups, between=None):
                for g in range(groups):
                    split_ready(n + 1)
                    for tt in range(4):
                        if between and g == 0 and tt == 2:
                            between()
                        if tt % 2 == 0:
                            group_free(fg + tt // 2)
                        out = bank[(fg + tt // 2) % 4][:, 256 * (tt % 2):256 * (tt % 2) + 256]
                        for k in range(DT):
                            slot, wc = (n + k // 4) % SLOTS, slice(256 * (k % 4), 256 * (k % 4) + 256)
                            tc = slice(tt * P, tt * P + P)
                            ins = three(out, whi[slot][:, wc], wlo[slot][:, wc], h_hi[:, k, tc], h_lo[:, k, tc],
                                        k == 0, k == DT - 1, moving_w=True)
                            if tt == 3 and k % 4 == 3:
                                ins.then_inc(s_used, 1)
                    n, fg = n + 2, fg + 2

            def swapped(S, ft, ps):
                mm(ps, swap, qk[:, ft, CTX:T], start=True, stop=True).then_inc(S["swapped"], 1)

            def qkv_norm_rope(n, fg):
                S = att[0]

                def squares(ft):
                    pe.wait_ge(S["squared_h"], ft + 1)
                    if ft:
                        pe.wait_ge(S["rs_ready"], ft)
                    mm(bank[4][:], heads, sqa[ft % 2][:], start=True, stop=True).then_inc(S["ss_full"], 1)

                def turn(ft):
                    pe.wait_ge(s_free["dve"], freed[fg + ft][1])
                    if ft:
                        pe.wait_ge(S["qk_ready"], ft)
                    swapped(S, ft, bank[5][:, 0:LAT])

                for ft in range(10):
                    group_free(fg + ft)
                    project(n, bank[(fg + ft) % 4], h_hi, h_lo, slice(0, T), ready=(s_hlo, 0) if ft == 0 else None)
                    n += 1
                    if ft:
                        squares(ft - 1)
                    if ft >= 2:
                        turn(ft - 2)
                    for m in mods_after("qkv", ft):
                        if m % 4 == 0 and m:
                            mod_turn(3 + m // 4)
                        mod_slab(n, 4 + m // 4, m % 4)
                        n += 1
                squares(9)
                mod_turn(8)
                turn(8)
                v_project(n, fg + 10, 1, between=lambda: turn(9))

            def qkv_plain(i, n, fg):
                S = att[i]
                for ft in range(16):
                    c = slice(CTX, T) if i == 3 and ft < 8 else slice(0, T)
                    group_free(fg + ft)
                    if ft == 1:
                        project_pair(n, (bank[fg % 4], bank[(fg + 1) % 4]), h_hi, h_lo, c, (s_hlo, 2 * i * DT))
                    elif ft:
                        project(n + ft, bank[(fg + ft) % 4], h_hi, h_lo, c)
                    if i == 1 and ft:
                        turn(S, ft - 1, fg)
                if i == 1:
                    turn(S, 15, fg)
                v_project(n + 16, fg + 16, 4)

            def turn(S, ft, fg):
                pe.wait_ge(s_free["act"], freed[fg + ft][1])
                if ft >= 2:
                    pe.wait_ge(S["qk_ready"], ft - 1)
                swapped(S, ft, bank[4 + ft % 2][:, 0:LAT])

            def attention(i):
                S, U = att[i], attention_units(i)
                maps = 2 if i == 1 else 1
                per_o = len(U) // DT
                c = slice(CTX, T) if i == 3 else slice(0, T)
                if i == 3:
                    n_last = freed[start["wo", i][1] - 9]
                    pe.wait_ge(s_free["act"], n_last[1])
                    pe.wait_ge(s_window, 1)
                else:
                    pe.wait_ge(S["qk_ready"], 10 if i == 0 else 16)
                if i == 0:
                    pe.wait_ge(s_kd, 1)
                pe.wait_ge(s_free["dve"], freed[start["wo", i][1] - 1][1])

                def score(u):
                    if not 0 <= u < len(U):
                        return
                    hd, s, q0 = U[u]
                    nk = CTX if s == 0 else T
                    if maps == 1 and u >= 4:
                        pe.wait_ge(S["context_copied" if i == 3 else "exped"], u - 3)
                    if maps == 2 and u >= 2:
                        pe.wait_ge(S["exped"], 2 * (u - 1))
                    for m in range(maps):
                        if i == 1:
                            r, qt, b = slice(HD * m, HD * m + HD), hd, bank[(2 * u + m) % 4]
                            keys = qk[r, 8 + hd, 0:nk]
                        else:
                            r, qt, b = slice(HD * (hd % 2), HD * (hd % 2) + HD), hd // 2, bank[u % 4]
                            keys = kd[r, hd // (A_HEADS // A_KV), 0:nk] if i == 0 else qk[r, 8 + qt, 0:nk]
                        mm(b[:, 0:nk], qk[r, qt, q0:q0 + P], keys, start=True, stop=True).then_inc(S["score_full"], 1)

                for u in range(-1, len(U) + 6):
                    w = u - 6
                    if i == 1 and w >= 0 and w % per_o == per_o - 1:
                        o = w // per_o
                        pe.wait_ge(S["squared_h"], o + 1)
                        mm(bank[5][:], ones, sqb[:], start=True, stop=True).then_inc(S["ss_full"], 1)
                    if maps == 1:
                        score(u + 1)
                    w = u - 2
                    if 0 <= w < len(U):
                        ring = 1 if i == 1 else 2
                        pe.wait_ge(S["p_ready"], w + 1)
                        if w >= ring:
                            pe.wait_ge(S["pt_ready"], w + 1 - ring)
                        pb = bank[4] if i == 1 else bank[4 + w % 2]
                        for kt in range(2 if U[w][1] == 0 else 4):
                            ins = nc.tensor.transpose(pb[:, kt * P:kt * P + P], p1[w % 3][:, kt * P:kt * P + P], ident)
                        ins.then_inc(S["p_turned"], 1)
                    if maps == 2:
                        score(u + 1)
                    if u >= 4 and u % 2 == 0 and u - 4 < len(U):
                        p = (u - 4) // 2
                        hd, s, _ = U[2 * p]
                        o = 2 * p // per_o
                        pe.wait_ge(S["pt_ready"], 2 * p + 2)
                        if o >= 2:
                            pe.wait_ge(S["o_lo"], o - 1)
                        if i == 1:
                            out, vc = bank[6 + o % 2][:, CTX * s:CTX * s + 256], slice(2 * HD * hd, 2 * HD * hd + 2 * HD)
                        else:
                            r0 = HD * (hd % 2)
                            vh = hd // (A_HEADS // A_KV) if i == 0 else hd
                            out, vc = bank[6 + o % 2][r0:r0 + HD, CTX * s:CTX * s + 256], slice(HD * vh, HD * vh + HD)
                        kts = 2 if s == 0 else 4
                        for kt in range(kts):
                            ins = mm(out, v_tok[:, kt, vc], pt[p % 2][:, kt, :], start=kt == 0, stop=kt == kts - 1)
                        ins.then_inc(S["pv_full"], 1)

            def gate(S, u):
                if u:
                    pe.wait_ge(S["gate_soft"], u)
                    pe.wait_ge(S["gate_min"], u)
                if u >= 2:
                    pe.wait_ge(S["state"], states(4 * u - 7))
                rows_u = slice(32 * (u % 2), 32 * (u % 2) + C_RANK)
                mm(bank[7][:], w_gate[rows_u, CH * (u // 2):CH * (u // 2) + CH], zT[rows_u, :],
                   start=True, stop=True).then_inc(S["gate_full"], 1)

            def qkv_gla(n, fg):
                S = att[2]
                for ft in range(8):
                    group_free(fg + ft)
                    if ft == 1:
                        project_pair(n, (bank[fg % 4], bank[(fg + 1) % 4]), h_hi, h_lo, slice(0, T), (s_hlo, 4 * DT))
                    elif ft:
                        project(n + ft, bank[(fg + ft) % 4], h_hi, h_lo, slice(0, T))
                pe.wait_ge(S["z_lo"], 1)
                for k in range(DT):
                    ins = three(bank[4][0:64, :], z_hi[:, k, :], z_lo[:, k, :], h_hi[:, k, :], h_lo[:, k, :],
                                k == 0, k == DT - 1)
                ins.then_inc(S["z_full"], 1)
                pe.wait_ge(S["z_copied"], 1)
                gate(S, 0)
                gate(S, 1)
                v_project(n + 8, fg + 8, 4)
                for ft in range(8):
                    group_free(fg + 16 + ft)
                    project(n + 16 + ft, bank[(fg + 16 + ft) % 4], h_hi, h_lo, slice(0, T))

            def gla():
                S = att[2]

                def levels(c):
                    hd, bwd, p, ci, cs = chunk_of(c)
                    w = c // 2
                    pe.wait_ge(S["q_dec"], 8 * w + LEVELS)
                    pe.wait_ge(S["k_dec"], 8 * w + LEVELS)
                    if c >= 2:
                        pe.wait_ge(S["masked"], c - 1)
                    ks, qs = (right, left) if bwd else (left, right)
                    out = bank[2 * (c % 2)]
                    for l in range(3):
                        n = CH >> l
                        for b in range(0, CH, n):
                            v = slice(ci.start + b, ci.start + b + n)
                            mm(out[b:b + n, b:b + n], ks[w % 2][:, l, v], qs[w % 2][:, l, v], start=l == 0, stop=l == 2,
                               skip_group_check=True)
                    for l in range(3, 8):
                        plane = l - 2
                        out = bank[2 * (c % 2) + plane // 4][:, CH * (plane % 4):CH * (plane % 4) + CH]
                        if l < LEVELS:
                            ins = mm(out, ks[w % 2][:, l, ci], qs[w % 2][:, l, ci], start=True, stop=True)
                        else:
                            ins = mm(out, qk[:, 4 + hd, cs], qk[:, hd, cs], start=True, stop=True)
                    ins.then_inc(S["score_full"], 1)

                def turn_keys(c):
                    hd, bwd, p, ci, cs = chunk_of(c)
                    w = c // 2
                    if c % 4 < 3:
                        pe.wait_ge(S["k_dec"], 8 * w + 8)
                        if c:
                            pe.wait_ge(S["k_endT"], states(c) - 1)
                        if c % 8 == 1 and hd:
                            pe.wait_ge(S["rs_ready"], hd)
                        nc.tensor.transpose(bank[6][:, 0:CH], k_end[w % 2][:, ci], ident).then_inc(S["turned"], 1)

                def chunk(c):
                    hd, bwd, p, ci, cs = chunk_of(c)
                    w = c // 2
                    vals = v_tok[:, cs.start // CH, C_HV * hd:C_HV * hd + C_HV]
                    pe.wait_ge(S["scores"], c + 1)
                    pe.wait_ge(S["q_dec"], 8 * w + 8)
                    if c % 8 == 0 and hd:
                        pe.wait_ge(S["o_copied_act"], hd)
                        pe.wait_ge(S["o_copied_dve"], hd)
                    if c % 4:
                        pe.wait_ge(S["state"], states(c - 1))
                    for v in range(2):
                        vc = slice(CH * v, CH * v + CH)
                        ins = mm(bank[4 + v][:, cs], vals[:, vc], scores[:], start=c % 8 == 0,
                                 stop=c % 8 == 7 and c % 4 == 0, skip_group_check=True)
                        if c % 4:
                            ins = mm(bank[4 + v][:, cs], state[(c % 4 - 1) % 2][:, vc], q_dec[w % 2][:, ci], start=False,
                                     stop=c % 8 == 7, skip_group_check=True)
                    ins.then_inc(S["o_full"], 1)
                    if c % 4 < 3:
                        pe.wait_ge(S["k_endT"], states(c))
                        if c:
                            pe.wait_ge(S["state"], states(c) - 1)
                        g = min(c // 4 + 2 + (c % 4 >= 2), C_UNITS)
                        pe.wait_ge(S["gate_soft"], g)
                        pe.wait_ge(S["gate_min"], g)
                        mm(bank[7][:, 0:C_HV], k_endT[:], vals, start=True, stop=True).then_inc(S["update_full"], 1)

                def squares_sum(hd, c):
                    pe.wait_ge(S["squared"], hd + 1)
                    pe.wait_ge(S["k_endT"], states(c))
                    for v in range(2):
                        ins = mm(bank[6][:], ones, sq_head[v][:], start=v == 0, stop=v == 1)
                    ins.then_inc(S["ss_full"], 1)

                n_chunks = 2 * C_ITEMS
                pe.wait_ge(s_free["act"], freed[start["wo", 2][1] - 1][1])
                pe.wait_ge(s_free["dve"], freed[start["wo", 2][1] - 9][1])
                levels(0)
                for c in range(n_chunks):
                    if c % 2 == 0 and gates_at(c // 2):
                        gate(S, gates_at(c // 2))
                    turn_keys(c)
                    if c + 1 < n_chunks:
                        levels(c + 1)
                    chunk(c)
                    if c % 8 == 0 and c:
                        squares_sum(c // 8 - 1, c)
                squares_sum(C_HEADS - 1, n_chunks - 1)

            pe.wait_ge(s_cst, 16)
            pe.wait_ge(s_cond, 32)
            nc.tensor.transpose(bank[4][:, 0:16], cond_row[:], ident[0:16, 0:16]).then_inc(s_cond_t, 1)
            pe.wait_ge(s_small, 16)
            nc.tensor.transpose(bank[5][:, 0:32], small_row[:], ident[0:32, 0:32]).then_inc(s_cond_t, 1)
            pe.wait_ge(s_lam_p, 1)
            mm(bank[5][:, 0:2], ones[0:HD, :], small[0:HD, 9:11], start=True, stop=True).then_inc(s_lam_d, 1)
            pe.wait_ge(s_rows, 16)
            for b in range(2):
                for r in range(4):
                    ins = nc.tensor.transpose(bank[2 + b][:, r * P:r * P + P], rows[:, 4 * b + r, :], ident)
                ins.then_inc(s_rows_t, 1)
            pe.wait_ge(s_tok, 32)
            for k in range(DT):
                if k >= 2:
                    pe.wait_ge(s_xn, k - 1)
                for tt in range(4):
                    ins = nc.tensor.transpose(bank[k % 2][:, tt * P:tt * P + P], tok[:, tt, k * P:k * P + P], ident)
                ins.then_inc(s_tok_t, 1)
            pe.wait_ge(s_cond_v, 1)
            for g in range(4):
                for q in range(4):
                    mod_slab(4 * g + q, g, q)
                mod_turn(g)
            for i in range(layers):
                st = 2 * i
                n, fg = start["qkv", i]
                if i == 0:
                    qkv_norm_rope(n, fg)
                elif i == 2:
                    qkv_gla(n, fg)
                else:
                    qkv_plain(i, n, fg)
                gla() if i == 2 else attention(i)
                n, fg = start["wo", i]
                c = cols(i, "tail")
                for dt in range(DT):
                    group_free(fg + dt)
                    project(n, bank[(fg + dt) % 4], h_hi, h_lo, c, ready=(att[i]["o_lo"], 0) if dt == 0 else None)
                    n += 1
                    for m in mods_after("wo", dt) if i == 0 else ():
                        if m in (24, 28):
                            mod_turn(3 + m // 4)
                        mod_slab(n, 4 + m // 4, m % 4)
                        n += 1
                if i == 0:
                    mod_turn(11)
                n, fg = start["premod", i]
                nxt = 12 * (i + 1)
                for q in range(PREMOD if i + 1 < layers else 0):
                    mod_slab(n + q, nxt, q)
                stats(st, c)
                n, fg = start["up", i]
                per = 8 if i + 1 < layers else 4
                group_free(fg + 3)

                def two_tiles(it, first=False):
                    for u in range(2):
                        at_slab = n + per // 2 * u
                        for k in range(2):
                            pe.wait_ge(s_free["dve"], freed[fg][1] - 4 + 2 * u + k + 4 * it)
                            if not (first and u == 0):
                                project(at_slab + k, bank[2 * u + k], h_hi, h_lo, c, it=it, per=per)
                            elif k == 1:
                                project_pair(at_slab, bank, h_hi, h_lo, c, (s_hlo, (st + 1) * DT))
                        if per == 8:
                            if u == 1:
                                mod_turn(nxt, it)
                            for q in range(2):
                                mod_slab(at_slab + 2 + q, nxt + u, (2 - 2 * u) + q, it=it, per=per)

                two_tiles(0, first=True)
                with pe.Fori(1, FT // 2) as it:
                    two_tiles(it)
                if i + 1 < layers:
                    n, fg = start["postmod", i]
                    for q in range(2):
                        mod_slab(n + q, nxt + 11, 2 + q)
                    mod_turn(nxt + 11)
                n, fg = start["down", i]
                for dt in range(DT):
                    group_free(fg + dt)
                    for q, (k0, nk) in enumerate(((0, 8), (8, 8), (16, 6))):
                        project(n + 3 * dt + q, bank[(fg + dt) % 4], g_hi, g_lo, c, k0, nk, first=q == 0, last=q == 2,
                                ready=(s_glo, FT * i) if dt == 0 else None)
                stats(st + 1, c)
            for q in range(4):
                if q == 0:
                    pe.wait_ge(s_outf, DT)
                for k in range(4):
                    ins = nc.tensor.transpose(bank[q][:, k * P:k * P + P],
                                              out_f[:, 4 * (q % 2) + k, P * (q // 2):P * (q // 2) + P], ident)
                ins.then_inc(s_outt, 1)


def kernel(**inputs):
    import numpy as _np
    import concourse.bacc as _bacc
    from concourse import mybir as _mybir
    from concourse.bass_utils import run_bass_kernel_spmd as _run

    nc = _bacc.Bacc("TRN2", target_bir_lowering=False, num_devices=1, dynamic_dma_scratch_size=1024)
    data = {k: _np.ascontiguousarray(v) for k, v in inputs.items()}
    per_layer = []
    for i in range(DEPTH):
        per_layer += [data[n][i].reshape(-1, P) for n in ("mod_b", "ln1_g", "ln1_b", "ln2_g", "ln2_b",
                                                          "ffn_conv_b", "ffn_conv_w")]
    table = _np.concatenate(per_layer, 0)
    for n in ("mod_b", "ln1_g", "ln1_b", "ln2_g", "ln2_b", "ffn_conv_b", "ffn_conv_w"):
        del data[n]
    data["rows"] = table
    zeros = _np.zeros
    lam = [data.pop("b_lambda_" + n)[0] for n in ("q1", "k1", "q2", "k2")]
    small = zeros((32, P), _np.float32)
    small[0], small[1] = _np.tile(data.pop("a_q_norm")[0], 2), _np.tile(data.pop("a_k_norm")[0], 2)
    small[2], small[3:5] = data.pop("b_subln")[0], data.pop("c_norm")[0].reshape(2, P)
    for n in range(4):
        small[5 + n, 0:HD] = lam[n]
    small[16:20], small[20:24] = data.pop("c_b_gate_fwd")[0].reshape(4, P), data.pop("c_b_gate_bwd")[0].reshape(4, P)
    data["small"] = small
    data["k_const"], data["k_window"] = constants()
    data["k_blocks"] = block_masks()
    arrays, args = {}, {}
    for name, x in data.items():
        arrays[f"in_{name}"] = x
        args[name] = nc.dram_tensor(f"in_{name}", x.shape, _mybir.dt.from_np(x.dtype), kind="ExternalInput").ap()
    args["out"] = nc.dram_tensor("out_0", (1, LAT, D), _mybir.dt.float32, kind="ExternalOutput").ap()
    build_program(nc, args)
    r = _run(nc, [arrays], core_ids=[0])
    return r.results[0]["out_0"]
```

```python
import math
from contextlib import ExitStack

import numpy as np

import concourse.bass as bass
import concourse.mybir as mybir

f32, f32r = mybir.dt.float32, mybir.dt.float32r
ACT, ALU = mybir.ActivationFunctionType, mybir.AluOpType
AX = mybir.AxisListType.X

P = 128
D, DEPTH = 1024, 4
CTX, LAT = 256, 256
T = CTX + LAT
DT = D // P
FF = 2816
FT = FF // P
GRID_W = 64
N_MOD = 6
A_HEADS, A_KV, B_HEADS, C_HEADS, D_HEADS, HD = 16, 4, 8, 4, 16, 64
C_KEY, C_VAL, C_RANK, C_NORMALIZER = 512, 1024, 16, 16.0
WIN_C, N_DR, N_DC = 16, 15, 31
NORM_EPS, LN_EPS = 1e-6, 1e-5
ALPHA = (2 * DEPTH) ** 0.25
SCALE = HD ** -0.5
LAM_INIT = 0.8 - 0.6 * math.exp(-0.3 * 1)

R_MODB, R_LN1G, R_LN1B, R_LN2G, R_LN2B, R_CB, R_CW = 0, 48, 56, 64, 72, 80, 124
R_LAYER = 256

K_ID, K_SWAP, K_ONES, K_HEAD, K_COS, K_SIN, K_EPS = 0, 128, 256, 384, 512, 768, 1024
K_N = 1032

SLOTS = 4
AHEAD = SLOTS - 1
PREMOD = 2
MAPS, TURN = 5, 3
SLAB = 1024
NB = 512

CH = 128
LEVELS = 7
REL, REL_AHEAD = 4, 2
PLANES = 6
C_UNITS = 2 * C_HEADS
C_ITEMS = 2 * C_UNITS
C_HV = C_VAL // C_HEADS


def constants():
    k = np.zeros((P, K_N), np.float32)
    i = np.arange(P)
    k[:, K_ID:K_ID + P] = np.eye(P)
    k[i ^ 32, K_SWAP + i] = 1.0
    k[:, K_ONES:K_ONES + P] = 1.0
    k[:, K_HEAD:K_HEAD + P] = (i[:, None] // HD == i[None, :] // HD)
    t = np.arange(LAT)
    nf = HD // 4
    inv = (np.float32(1.0) / np.float32(10000.0) ** (np.arange(nf, dtype=np.float32) / np.float32(nf))).astype(np.float32)
    ang = np.concatenate([(t // GRID_W).astype(np.float32)[:, None] * inv,
                          (t % GRID_W).astype(np.float32)[:, None] * inv], -1).astype(np.float32)
    pair = i % 32
    k[:, K_COS:K_COS + LAT] = np.cos(ang).T[pair]
    k[:, K_SIN:K_SIN + LAT] = np.sin(ang).T[pair] * np.where(i % HD < 32, -1.0, 1.0)[:, None]
    k[:, K_EPS], k[:, K_EPS + 1], k[:, K_EPS + 2] = NORM_EPS, LN_EPS, 1.0
    k[0:2, K_EPS + 3], k[2:4, K_EPS + 4] = 1.0, 1.0
    cq = np.arange(GRID_W)
    c0 = np.clip(cq - WIN_C // 2, 0, GRID_W - WIN_C)
    col_in = (cq[None, :] >= c0[:, None]) & (cq[None, :] < c0[:, None] + WIN_C)
    window = np.tile(np.where(col_in, 0.0, -1e30).astype(np.float32)[::-1], (2, 1))
    return k, window


def block_masks():
    j, i = np.arange(P)[:, None], np.arange(P)[None, :]
    return np.stack([(i >> s) == (j >> s) for s in (7, 4, 3, 2, 1, 0)], 1).astype(np.float32)


class Count:

    def __init__(self, sem):
        self.sem, self.n = sem, 0

    def up(self, ins, by=1):
        ins.then_inc(self.sem, by)
        self.n += by
        return self.n


def mods_after(phase, tile):
    if phase == "qkv":
        return range(2 * tile, 2 * tile + 2)
    return range(20 + (3 * tile + 1) // 2, 20 + (3 * tile + 4) // 2)


def mod_events(i, part):
    return part + 1 if i == 0 else i + 3


def make_plan(layers):
    slabs, owner, start = [], [], {}

    def mod_group(layer, g):
        slabs.extend(("mod", layer, g, q) for q in range(4))

    start["mod"] = (0, 0)
    for g in range(4):
        mod_group(0, g)
    for i in range(layers):
        start["qkv", i] = (len(slabs), len(owner))
        if i == 0:
            for ft in range(10):
                slabs.append(("f", "a_w_qkv", ft * P, 0, 8))
                owner.append("dve")
                slabs.extend(("mod", 0, 4 + m // 4, m % 4) for m in mods_after("qkv", ft))
            slabs.extend(("v", "a_w_qkv", 1280, q) for q in range(2))
            owner += ["dve"] * 2
        elif i == 1 or i == 3:
            name = "b_w_qkv" if i == 1 else "d_w_qkv"
            for ft in range(16):
                slabs.append(("f", name, ft * P, 0, 8))
                owner.append("act")
            for g in range(4):
                slabs.extend(("v", name, 2048 + 256 * g, q) for q in range(2))
                owner += ["dve"] * 2
        else:
            for ft in range(16):
                slabs.append(("f", "c_w_in", (2048 + ft * P) if ft < 8 else (ft - 8) * P, 0, 8))
                owner.append("act")
            for g in range(4):
                slabs.extend(("v", "c_w_in", 1024 + 256 * g, q) for q in range(2))
                owner += ["dve"] * 2
        start["wo", i] = (len(slabs), len(owner))
        for dt in range(DT):
            slabs.append(("f", "abcd"[i] + "_w_o", dt * P, 0, 8))
            owner.append("act")
            if i == 0:
                slabs.extend(("mod", 0, 4 + m // 4, m % 4) for m in mods_after("wo", dt))
        mods = [("mod", i + 1, m // 4, m % 4) for m in range(48)] if i + 1 < layers else []
        start["premod", i] = (len(slabs), len(owner))
        slabs.extend(mods[:PREMOD])
        start["up", i] = (len(slabs), len(owner))
        for j in range(FT):
            slabs.extend(("up", i, col) for col in (j * P, FF + j * P))
            owner += ["dve"] * 2
            slabs.extend(mods[PREMOD + 2 * j:PREMOD + 2 * j + 2])
        start["postmod", i] = (len(slabs), len(owner))
        slabs.extend(mods[PREMOD + 2 * FT:])
        start["down", i] = (len(slabs), len(owner))
        for dt in range(DT):
            for k0, nk in ((0, 8), (8, 8), (16, 6)):
                slabs.append(("down", i, dt * P, k0, nk))
            owner.append("act")
    freed, seen = [], {"act": 0, "dve": 0}
    for e in owner:
        seen[e] += 1
        freed.append((e, seen[e]))
    return slabs, freed, start


def build_program(nc, a, layers=DEPTH):
    slabs, freed, start = make_plan(layers)
    n_slabs = len(slabs)
    ctx = ExitStack()
    with ctx:
        top = [(nc.sbuf_base + 63) // 64 * 64]

        def place(name, shape, dt=f32, at=None):
            size = int(np.prod(shape[1:])) * mybir.dt.size(dt)
            offset = top[0] if at is None else at[0]
            (top if at is None else at)[0] += (size + 63) // 64 * 64
            return nc.alloc_sbuf_tensor_at(name, list(shape), dt, offset=offset)

        xn = place("xn", [P, DT, T])
        h_hi, h_lo = place("h_hi", [P, DT, T], f32r), place("h_lo", [P, DT, T], f32r)
        raw = [place(f"slab_raw{s}", [P, SLAB]) for s in range(SLOTS)]
        whi = [place(f"slab_hi{s}", [P, SLAB], f32r) for s in range(SLOTS)]
        wlo = [place(f"slab_lo{s}", [P, SLAB], f32r) for s in range(SLOTS)]
        rotary_at = [top[0] + 4 * K_COS]
        cst = place("cst", [P, K_N])
        k_end = [place(f"k_end{s}", [P, 2 * CH], at=rotary_at) for s in range(2)]
        prm = place("prm", [P, DEPTH * R_LAYER])
        modT = [place(f"modT{s}", [P, N_MOD * DT, 2]) for s in range(2)]
        coef = [place(f"coef{s}", [P, 6, DT]) for s in range(2)]
        unit_gb = place("unit_gb", [P, 2, DT])
        mod_row_at = [top[0]]
        mod_row = place("mod_row", [4, NB])
        w_gate = place("w_gate", [48, C_KEY], at=mod_row_at)
        small_row = place("small_row", [32, P])
        cond_row = place("cond_row", [16, P])
        cond = place("cond", [P, 2, DT])
        cond4 = place("cond4", [P, DT, 4], f32r)
        small = place("small", [P, 32])
        mean, rstd = place("mean", [P, T]), place("rstd", [P, T])
        work = [top[0]]
        res_t = [place(f"res_t{s}", [P, T], at=work) for s in range(2)]
        acc_s, acc_q = place("acc_s", [P, T], at=work), place("acc_q", [P, T], at=work)
        sq = place("sq", [P, T], at=work)
        conv_at = [top[0]]
        conv = [[place(f"conv{c}{u}", [P, T], at=conv_at) for u in range(2)] for c in range(2)]
        g32 = [place(f"g32_{u}", [P, T], at=conv_at) for u in range(2)]
        gla_at = [top[0]]
        masked = [place(f"masked{s}", [P, PLANES, CH], at=gla_at) for s in range(2)]
        o_head = [place(f"o_head{v}", [P, T], at=gla_at) for v in range(2)]
        sq_head = [rstd, place("sq_head", [P, T], at=gla_at)]
        top[0] = max(work[0], conv_at[0])
        arena = top[0]
        at = [arena]
        tok = place("tok", [P, 4, D], at=at)
        rows = place("rows", [P, 8, P], at=at)
        at = [arena]
        g_hi, g_lo = place("g_hi", [P, FT, T], f32r, at=at), place("g_lo", [P, FT, T], f32r, at=at)
        at = [arena]
        qk = place("qk", [P, 16, T], at=at)
        v_tok = place("v_tok", [P, 4, D], at=at)
        p1 = [place(f"p1_{s}", [P, T], at=at) for s in range(MAPS)]
        pt = [place(f"pt{s}", [P, 4, 256], at=at) for s in range(2)]
        stat = place("stat", [P, 6, 128], at=at)
        own = at[0]
        at = [own]
        kd = place("kd", [P, A_KV, T], at=at)
        sqa = [place(f"sqa{s}", [P, T], at=at) for s in range(2)]
        rsa = [place(f"rsa{s}", [P, T], at=at) for s in range(2)]
        rope_t = place("rope_t", [P, LAT], at=at)
        at = [own]
        rope_b = place("rope_b", [P, LAT], at=at)
        p2 = [place(f"p2_{s}", [P, T], at=at) for s in range(MAPS)]
        sqb, rsb, o32 = place("sqb", [P, T], at=at), place("rsb", [P, T], at=at), place("o32", [P, T], at=at)
        at = [own]
        bias = place("bias", [P, D_HEADS, 6 * GRID_W], at=at)
        window = place("window", [P, GRID_W], at=at)
        at = [arena + 4 * (16 * T + 4 * D)]
        right = [place(f"right{s}", [P, LEVELS, 2 * CH], at=at) for s in range(2)]
        left = [place(f"left{s}", [P, LEVELS, 2 * CH], at=at) for s in range(2)]
        same_block = place("same_block", [P, PLANES, CH], at=at)
        z_at = [at[0]]
        soft = place("soft", [P, T], at=at)
        cum = [place(f"cum{s}", [P, T], at=at) for s in range(2)]
        rel = [place(f"rel{s}", [P, 2 * CH], at=at) for s in range(REL)]
        q_dec = [place(f"q_dec{s}", [P, 2 * CH], at=at) for s in range(2)]
        start_dec = [place(f"start_dec{s}", [P, 2 * CH], at=at) for s in range(2)]
        k_endT, scores = place("k_endT", [P, CH], at=at), place("scores", [P, CH], at=at)
        state = [place(f"state{s}", [P, C_HV], at=at) for s in range(2)]
        zT = place("zT", [64, T], at=at)
        edge = [place(f"edge{s}", [P, 3, T // CH], at=at) for s in range(2)]
        z_raw = place("z_raw", [P, DT, 64], at=z_at)
        z_hi, z_lo = place("z_hi", [P, DT, 64], f32r, at=z_at), place("z_lo", [P, DT, 64], f32r, at=z_at)
        gate_min = mean
        assert at[0] <= nc.sbuf_usable_end
        at = [arena]
        out_f = place("out_f", [P, DT, LAT], at=at)
        out_tok = place("out_tok", [P, 2, D], at=at)
        assert at[0] <= nc.sbuf_usable_end

        bank = [nc.alloc_psum_tensor(f"bank{b}", [P, NB], f32) for b in range(8)]
        LN_SUM, LN_SQ, MOD_ACC, MOD_T = bank[4], bank[5], bank[6], bank[7]

        def sem(name):
            return ctx.enter_context(nc.semaphore(name))

        loaded = [sem(f"slab_loaded{s}") for s in range(SLOTS)]
        s_hi, s_lo, s_used = sem("slab_hi_ready"), sem("slab_lo_ready"), sem("slab_used")
        s_free = {"act": sem("group_freed_act"), "dve": sem("group_freed_dve")}
        s_cst, s_cond, s_tok, s_rows, s_small, s_bias_in = (sem(n) for n in (
            "consts_in", "cond_in", "tokens_in", "rows_in", "small_in", "bias_in"))
        s_cond_t, s_cond_a, s_cond_v, s_rows_t, s_rows_v, s_tok_t = (sem(n) for n in (
            "cond_transposed", "cond_act", "cond_split", "rows_transposed", "rows_copied", "tokens_transposed"))
        s_mod_row, s_mod_t, s_mod_in, s_coef = (sem(n) for n in (
            "mod_row_copied", "mod_transposed", "mod_evacuated", "coefficients_ready"))
        s_y, s_sum, s_sqd, s_qsum, s_stats, s_mean, s_var, s_rstd, s_cen, s_xn = (sem(n) for n in (
            "residual_added", "sum_added", "squared", "squares_added", "stats_full",
            "mean_ready", "var_ready", "rstd_ready", "centred", "xn_ready"))
        s_hf, s_hf_lat = sem("h_modulated"), sem("h_latents_modulated")
        s_hhi, s_hlo = sem("h_hi_ready"), sem("h_lo_ready")
        s_tap1, s_tap2, s_silu, s_gmul, s_ghi, s_glo = (sem(n) for n in (
            "conv_centre_tap", "conv_left_tap", "silu_done", "gated", "g_hi_ready", "g_lo_ready"))
        s_dve, s_act = sem("dve_step"), sem("act_step")
        s_kd, s_window = sem("keys_doubled"), sem("bias_masked")
        s_lam_p, s_lam_d, s_lam_e = (sem(n) for n in (
            "lambda_products", "lambda_dots", "lambda_exps"))
        s_outf, s_outt, s_outv, s_out = sem("out_scaled"), sem("out_transposed"), sem("out_copied"), sem("out_stored")

        att = {}
        for i in (0, 1, 3):
            att[i] = {n: sem(f"{n}_{i}") for n in (
                "qk_ready", "swapped", "score_full", "biased", "context_copied", "negmax", "exped", "p_ready", "p_turned",
                "pt_ready", "pv_full", "o_hi", "o_lo")}
            if i < 2:
                att[i].update({n: sem(f"{n}_{i}") for n in ("squared_h", "ss_full", "rs_ready", "o_normed")})
        att[2] = {n: sem(f"gla_{n}") for n in (
            "zeroed", "tables_in", "z_hi", "z_lo", "z_full", "z_copied", "gate_full", "gate_soft", "gate_min", "cum",
            "rel", "decay", "q_dec", "k_dec", "score_full", "masked", "scores", "turned", "k_endT", "o_full",
            "update_full", "state", "o_copied_act", "o_copied_dve", "squared", "ss_full", "rs_ready", "o_normed", "o_gated", "o_hi", "o_lo")}

        block = ctx.enter_context(nc.Block())

        ident, swap, ones, heads = (cst[:, c:c + P] for c in (K_ID, K_SWAP, K_ONES, K_HEAD))
        cos, sin = cst[:, K_COS:K_COS + LAT], cst[:, K_SIN:K_SIN + LAT]
        eps_norm, one = (cst[:, K_EPS + c:K_EPS + c + 1] for c in (0, 2))
        sel = cst[0:4, K_EPS + 3:K_EPS + 5]

        def cols(i, part):
            return slice(CTX, T) if i == DEPTH - 1 and part == "tail" else slice(0, T)

        def segs(c):
            return [s for s in ((0, slice(0, CTX)), (1, slice(CTX, T))) if s[1].start >= c.start]

        def gain(st):
            if st == 0:
                return unit_gb[:, 0, :], unit_gb[:, 1, :]
            i, second = (st - 1) // 2, (st - 1) % 2
            r = R_LAYER * i + (R_LN2G if second else R_LN1G)
            return prm[:, r:r + DT], prm[:, r + DT:r + 2 * DT]

        def mod(st, which):
            return (3 * (st % 2) + which) * DT

        def src(s):
            kind = s[0]
            if kind == "mod":
                _, i, g, q = s
                return a["mod_w"][i, 2 * q * P:(2 * q + 2) * P, g * NB:(g + 1) * NB].rearrange("(k p) c -> p k c", p=P), 2
            if kind == "f":
                _, name, c, k0, nk = s
                return a[name][0, k0 * P:(k0 + nk) * P, c:c + P].rearrange("(k p) c -> p k c", p=P), nk
            if kind == "v":
                _, name, c, q = s
                return a[name][0, 4 * q * P:(4 * q + 4) * P, c:c + 256].rearrange("(k p) c -> p k c", p=P), 4
            if kind == "up":
                _, i, c = s
                return a["ffn_w_up"][i, :, c:c + P].rearrange("(k p) c -> p k c", p=P), 8
            _, i, c, k0, nk = s
            return a["ffn_w_down"][i, k0 * P:(k0 + nk) * P, c:c + P].rearrange("(k p) c -> p k c", p=P), nk

        def width(s):
            return {"mod": SLAB, "v": SLAB, "up": SLAB}.get(s[0]) or s[4] * P

        def mirrored(ap):
            return ap.rearrange("p (r c) -> p r c", c=GRID_W)[:, :, ::-1]

        def attention_units(i):
            n = (A_HEADS, B_HEADS, 0, D_HEADS)[i]
            return [(hd, s, CTX * s + P * b) for hd in range(n) for s in ((1,) if i == 3 else (0, 1)) for b in (0, 1)]

        def rpb_block(dr):
            t = a["d_rpb"]
            return bass.AP(tensor=t.tensor, offset=dr * N_DC + WIN_C - GRID_W,
                           ap=[[1, GRID_W], [N_DR * N_DC, D_HEADS], [1, GRID_W]])

        def gates_at(w):
            return (w + 3) // 2 if w % 2 and (w + 3) // 2 < C_UNITS else None

        def item_of(w):
            return w // 4, w // 2 % 2, slice(CTX * (w % 2), CTX * (w % 2) + 2 * CH)

        def chunk_of(c):
            hd, bwd, cols_w = item_of(c // 2)
            p = c % 2 ^ bwd
            return hd, bwd, p, slice(CH * p, CH * p + CH), slice(cols_w.start + CH * p, cols_w.start + CH * p + CH)

        def states(c):
            return 3 * (c // 4) + min(c % 4 + 1, 3)

        def half(ap, l, right_half):
            v = ap.rearrange("p (n h s) -> p n h s", h=2, s=64 >> l)
            return v[:, :, 1 if right_half else 0, :]

        @block.sync
        def _(sp):
            sp.dma_start(cst[:], a["k_const"]).then_inc(s_cst, 16)
            sp.dma_start(cond_row[0:DT, :], a["c_ctx"].rearrange("(k p) -> k p", p=P)).then_inc(s_cond, 16)
            sp.dma_start(cond_row[DT:2 * DT, :], a["c"][0].rearrange("(k p) -> k p", p=P)).then_inc(s_cond, 16)

            def load(n):
                source, nk = src(slabs[n])
                if n >= SLOTS:
                    sp.wait_ge(s_hi, n - SLOTS + 1)
                    sp.wait_ge(s_lo, n - SLOTS + 1)
                dst = raw[n % SLOTS][:, 0:width(slabs[n])].rearrange("p (k c) -> p k c", k=nk)
                sp.dma_start(dst, source).then_inc(loaded[n % SLOTS], 16)

            n = 0
            while n < n_slabs:
                if n == 4:
                    sp.dma_start(rows[:], a["rows"].rearrange("(r p) d -> p r d", p=P)).then_inc(s_rows, 16)
                if n == 6:
                    sp.dma_start(tok[:, 0:2, :], a["ctx"][0].rearrange("(t p) d -> p t d", p=P)).then_inc(s_tok, 16)
                if n == 8:
                    sp.dma_start(tok[:, 2:4, :], a["x"][0].rearrange("(t p) d -> p t d", p=P)).then_inc(s_tok, 16)
                rolled = [i for i in range(layers) if start["up", i][0] == n]
                if not rolled:
                    load(n)
                    n += 1
                    continue
                i = rolled[0]
                per = 8 if i + 1 < layers else 4
                with sp.Fori(0, FT // 2) as it:
                    for c in range(per):
                        s = slabs[n + c]
                        sp.wait_ge(s_hi, n + c - SLOTS + 1 + per * it)
                        sp.wait_ge(s_lo, n + c - SLOTS + 1 + per * it)
                        if s[0] == "up":
                            source = a["ffn_w_up"][i, :, bass.ds(s[2] + 2 * P * it, P)]
                        else:
                            source = a["mod_w"][i + 1, 2 * s[3] * P:(2 * s[3] + 2) * P, bass.ds(NB * s[2] + NB * it, NB)]
                        nk = 8 if s[0] == "up" else 2
                        sp.dma_start(raw[(n + c) % SLOTS][:].rearrange("p (k c) -> p k c", k=nk),
                                     source.rearrange("(k p) c -> p k c", p=P)).then_inc(loaded[(n + c) % SLOTS], 16)
                n += per * (FT // 2)
            sp.wait_ge(s_outv, 4)
            sp.dma_start(a["out"][0].rearrange("(t p) d -> p t d", p=P), out_tok[:]).then_inc(s_out, 16)
            sp.wait_ge(s_out, 16)

        @block.scalar
        def _(act):
            step = Count(s_act)
            act.dma_start(small_row[:], a["small"]).then_inc(s_small, 16)

            def split(n, it=0, per=0):
                if n >= n_slabs:
                    return
                slot = n % SLOTS
                act.wait_ge(loaded[slot], 16 * (n // SLOTS + 1) + 16 * (per // SLOTS) * it)
                if n >= SLOTS:
                    act.wait_ge(s_used, n - SLOTS + 1 + per * it)
                w = SLAB if per else width(slabs[n])
                nc.scalar.activation(whi[slot][:, 0:w], raw[slot][:, 0:w], ACT.Copy).then_inc(s_hi, 1)

            def make_h(st, c, following=None):
                cf, both = coef[st % 2], c.start == 0
                for k in range(DT):
                    act.wait_ge(s_xn, DT * st + k + 1)
                    if k == 0:
                        act.wait_ge(s_coef, st + 1)
                    if k >= 2:
                        act.wait_ge(s_hlo, DT * st + k - 1)
                    s, cc = segs(c)[0]
                    nc.scalar.activation(res_t[k % 2][:, cc], xn[:, k, cc], ACT.Identity,
                                         bias=cf[:, 2 + s, k:k + 1], scale=cf[:, s, k:k + 1]).then_inc(s_hf, 1)
                    act.wait_ge(s_hf, DT * st + k + 1)
                    if both:
                        act.wait_ge(s_hf_lat, DT * st + k + 1)
                    nc.scalar.activation(h_hi[:, k, c], res_t[k % 2][:, c], ACT.Copy).then_inc(s_hhi, 1)
                    if k == 5 and following is not None:
                        split(following)

            def residual(st, n, fg, per, c):
                i = st // 2

                def square(dt):
                    act.wait_ge(s_y, DT * st + dt + 1)
                    if dt >= 2:
                        act.wait_ge(s_qsum, 6 * st + dt - 1)
                    nc.scalar.activation((sq if dt else acc_q)[:, c], xn[:, dt, c], ACT.Square).then_inc(s_sqd, 1)

                if st % 2:
                    nc.scalar.preload_act_table_set("natural_log_exp_and_others")
                for dt in range(DT):
                    for q in range(per):
                        split(n + q + AHEAD)
                    n += per
                    if dt:
                        square(dt - 1)
                    act.wait_ge(s_used, n)
                    if dt == 0:
                        act.wait_ge(s_mod_in, mod_events(i, 1))
                    for s, cc in segs(c):
                        ins = nc.scalar.activation(
                            res_t[dt % 2][:, cc], bank[(fg + dt) % 4][:, cc], ACT.Identity,
                            bias=coef[st % 2][:, 5, dt:dt + 1],
                            scale=modT[i % 2][:, mod(st, 2) + dt, s:s + 1])
                    ins.then_inc(s_free["act"], 1)
                    for m in mods_after("wo", dt) if st == 0 else ():
                        split(n + AHEAD)
                        n += 1
                square(DT - 1)
                if st % 2 == 0 and i + 1 < layers:
                    for q in range(PREMOD):
                        split(n + q + AHEAD)
                act.wait_ge(s_var, st + 1)
                step.up(nc.scalar.activation(rstd[:, c], acc_q[:, c], ACT.Ln))
                act.wait_ge(s_act, step.n)
                nc.scalar.activation(rstd[:, c], rstd[:, c], ACT.Exp, scale=-0.5).then_inc(s_rstd, 1)

            def root(dst, of, scale):
                step.up(nc.scalar.activation(dst, of, ACT.Ln, scale=scale, bias=eps_norm))
                act.wait_ge(s_act, step.n)
                return nc.scalar.activation(dst, dst, ACT.Exp, scale=-0.5)

            def qkv_norm_rope(n, fg):
                S = att[0]

                def roots(ft):
                    act.wait_ge(S["ss_full"], ft + 1)
                    if ft >= 2:
                        act.wait_ge(s_free["dve"], ft - 1)
                    root(rsa[ft % 2][:], bank[4][:], 1.0 / HD).then_inc(S["rs_ready"], 1)

                for ft in range(10):
                    if ft:
                        split(n + AHEAD)
                    n += 1
                    act.wait_ge(s_used, n)
                    if ft >= 2:
                        act.wait_ge(S["ss_full"], ft - 1)
                    nc.scalar.activation(sqa[ft % 2][:], bank[(fg + ft) % 4][:], ACT.Square).then_inc(S["squared_h"], 1)
                    if ft:
                        roots(ft - 1)
                    for m in mods_after("qkv", ft):
                        split(n + AHEAD)
                        n += 1
                roots(9)
                for q in range(2):
                    split(n + AHEAD)
                    n += 1
                act.wait_ge(S["qk_ready"], 10)
                for kt in range(2):
                    for j in range(2):
                        for half in range(2):
                            ins = nc.scalar.activation(kd[HD * half:HD * half + HD, 2 * kt + j, :],
                                                       qk[HD * j:HD * j + HD, 8 + kt, :], ACT.Copy)
                ins.then_inc(s_kd, 1)

            def qkv_plain(i, n, fg):
                S = att[i]
                for ft in range(16):
                    if ft:
                        split(n + ft + AHEAD)
                    act.wait_ge(s_used, n + ft + 1)
                    dst, ps = qk[:, ft, :], bank[(fg + ft) % 4]
                    if i == 3 and ft < 8:
                        dst, source = mirrored(dst[:, CTX:T]), ps[:, CTX:T].rearrange("p (r c) -> p r c", c=GRID_W)
                    else:
                        source = ps[:]
                    nc.scalar.activation(dst, source, ACT.Identity,
                                         scale=SCALE if ft < 8 else 1.0).then_inc(s_free["act"], 1)
                for q in range(8):
                    split(n + 16 + q + AHEAD)

            def attention(i):
                S, U = att[i], attention_units(i)
                maps = 2 if i == 1 else 1
                per_o = len(U) // DT

                def copy_context(u):
                    if u < len(U):
                        act.wait_ge(S["biased"], u + 1)
                        nc.scalar.activation(p1[u % MAPS][:, 0:CTX], bank[u % 4][:, 0:CTX],
                                             ACT.Copy).then_inc(S["context_copied"], 1)

                if i == 3:
                    copy_context(0)
                for u in range(len(U) + TURN + 7):
                    if u < len(U):
                        hd, s, q0 = U[u]
                        nk = CTX if s == 0 else T
                        if u >= MAPS:
                            act.wait_ge(S["p_turned"], u - MAPS + 1)
                        if i == 3:
                            copy_context(u + 1)
                        for m in range(maps):
                            act.wait_ge(S["negmax"], maps * u + m + 1)
                            b = bank[(2 * u + m) % 4] if maps == 2 else bank[u % 4]
                            dst = (p1, p2)[m][u % MAPS]
                            source = p1[u % MAPS] if i == 3 else b
                            nc.scalar.activation(dst[:, 0:nk], source[:, 0:nk], ACT.Exp,
                                                 bias=stat[:, m, u:u + 1],
                                                 accum_out=stat[:, 2 + m, u:u + 1]).then_inc(S["exped"], 1)
                    if 0 <= u - TURN < len(U):
                        w = u - TURN
                        hd, s, q0 = U[w]
                        act.wait_ge(S["p_turned"], w + 1)
                        if w >= 4:
                            act.wait_ge(S["pv_full"], w // 2 - 1)
                        kt = 2 if s == 0 else 4
                        pb = bank[4] if i == 1 else bank[4 + w % 2]
                        nc.scalar.activation(pt[w // 2 % 2][:, 0:kt, P * (w % 2):P * (w % 2) + P],
                                             pb[:, 0:kt * P].rearrange("p (k q) -> p k q", k=kt),
                                             ACT.Copy).then_inc(S["pt_ready"], 1)
                    if i == 1:
                        for stage, lag in enumerate((TURN + 3, TURN + 5, TURN + 6)):
                            w = u - lag
                            if not 0 <= w < len(U) or w % per_o != per_o - 1:
                                continue
                            o = w // per_o
                            if stage == 0:
                                act.wait_ge(S["pv_full"], (w + 1) // 2)
                                nc.scalar.activation(sqb[:], bank[6 + o % 2][:], ACT.Square).then_inc(S["squared_h"], 1)
                            elif stage == 1:
                                act.wait_ge(S["ss_full"], o + 1)
                                root(rsb[:], bank[5][:], 1.0 / (2 * HD)).then_inc(S["rs_ready"], 1)
                            else:
                                act.wait_ge(S["o_normed"], o + 1)
                                nc.scalar.activation(h_hi[:, o, :], o32[:], ACT.Copy).then_inc(S["o_hi"], 1)
                        continue
                    w = u - TURN - 3
                    if 0 <= w < len(U) and w % per_o == per_o - 1:
                        o = w // per_o
                        c = slice(CTX, T) if i == 3 else slice(0, T)
                        act.wait_ge(S["pv_full"], (w + 1) // 2)
                        if i == 0:
                            nc.scalar.activation(h_hi[:, o, :], bank[6 + o % 2][:], ACT.Copy).then_inc(S["o_hi"], 1)
                        else:
                            nc.scalar.activation(h_hi[:, o, c].rearrange("p (r c) -> p r c", c=GRID_W),
                                                 mirrored(bank[6 + o % 2][:, c]), ACT.Copy).then_inc(S["o_hi"], 1)

            def gate(S, u):
                b = 16 + C_HEADS * (u % 2) + u // 2
                act.wait_ge(S["gate_full"], u + 1)
                if u:
                    act.wait_ge(S["cum"], u)
                step.up(nc.scalar.activation(soft[:], bank[7][:], ACT.Abs, bias=small[:, b:b + 1]))
                act.wait_ge(s_act, step.n)
                step.up(nc.scalar.activation(soft[:], soft[:], ACT.Exp, scale=-1.0))
                act.wait_ge(s_act, step.n)
                nc.scalar.activation(soft[:], soft[:], ACT.Ln, bias=one).then_inc(S["gate_soft"], 1)

            def gla_tables():
                S = att[2]
                act.wait_ge(S["zeroed"], 1)
                act.dma_start(z_raw[:, :, 0:C_RANK], a["c_w_in"][0, :, 3072:3088].rearrange("(k p) c -> p k c", p=P)
                              ).then_inc(S["tables_in"], 16)
                act.dma_start(z_raw[:, :, 32:32 + C_RANK], a["c_w_in"][0, :, 3088:3104].rearrange("(k p) c -> p k c", p=P)
                              ).then_inc(S["tables_in"], 16)
                act.dma_start(w_gate[0:C_RANK, :], a["c_w_gate_fwd"][0]).then_inc(S["tables_in"], 16)
                act.dma_start(w_gate[32:32 + C_RANK, :], a["c_w_gate_bwd"][0]).then_inc(S["tables_in"], 16)
                act.dma_start(same_block[:], a["k_blocks"]).then_inc(S["tables_in"], 16)

            def decays(w, l0, l1):
                S = att[2]
                hd, bwd, cw = item_of(w)
                sums, e, inv = cum[w // 2 % 2], edge[w // 2 % 2], 1 / C_NORMALIZER
                for l in range(l0, l1):
                    j = 8 * w + l
                    r = rel[j % REL]
                    if l == 0 and w % 2 == 0:
                        act.wait_ge(S["cum"], w // 2 + 1)
                        chunks = sums[:].rearrange("p (c t) -> p c t", t=CH)
                        mid, end = (CH // 2, 0) if bwd else (CH // 2 - 1, CH - 1)
                        for n, (token, sign) in enumerate(((mid, inv), (mid, -inv), (end, inv))):
                            ins = nc.scalar.activation(e[:, n, :], chunks[:, :, token], ACT.Copy, scale=sign)
                        step.up(ins)
                        act.wait_ge(s_act, step.n)
                    if l in (0, LEVELS):
                        if j >= REL:
                            act.wait_ge(S["k_dec"], j - REL + 1)
                            act.wait_ge(S["q_dec"], j - REL + 1)
                        if l and w >= 2:
                            act.wait_ge(S["state"], states(2 * w - 3))
                        for c in range(2):
                            chunk = 2 * (w % 2) + c
                            if l:
                                nc.scalar.activation(r[:, CH * c:CH * c + CH], sums[:, CH * chunk:CH * chunk + CH], ACT.Exp,
                                                     scale=-inv, bias=e[:, 2, chunk:chunk + 1])
                                continue
                            for is_q in (1, 0):
                                t0 = CH // 2 * (is_q ^ bwd)
                                ins = nc.scalar.activation(
                                    r[:, CH * c + t0:CH * c + t0 + CH // 2],
                                    sums[:, CH * chunk + t0:CH * chunk + t0 + CH // 2], ACT.Exp,
                                    scale=inv if is_q else -inv, bias=e[:, is_q, chunk:chunk + 1])
                        if l:
                            ins = nc.scalar.activation(start_dec[w % 2][:], sums[:, cw], ACT.Exp, scale=inv)
                    else:
                        act.wait_ge(S["rel"], 6 * w + l)
                        for is_q in (1, 0):
                            v = half(r[:], l, is_q ^ bwd)
                            ins = nc.scalar.activation(v, v, ACT.Exp, scale=inv if is_q else -inv)
                    ins.then_inc(S["decay"], 1)

            def qkv_gla(n, fg):
                S = att[2]
                nc.scalar.preload_act_table_set("silu_and_others")
                for ft in range(16):
                    if ft:
                        split(n + ft + AHEAD)
                    act.wait_ge(s_used, n + ft + 1)
                    if ft < 8:
                        nc.scalar.activation(qk[:, 8 + ft, :], bank[(fg + ft) % 4][:], ACT.Silu).then_inc(s_free["act"], 1)
                    else:
                        nc.scalar.activation(qk[:, ft - 8, :], bank[(fg + ft) % 4][:], ACT.Identity,
                                             scale=CH ** -0.5 if ft < 12 else 1.0).then_inc(s_free["act"], 1)
                    if ft == 4:
                        act.wait_ge(S["tables_in"], 80)
                        nc.scalar.activation(z_hi[:], z_raw[:], ACT.Copy).then_inc(S["z_hi"], 1)
                    if ft == 8:
                        nc.scalar.preload_act_table_set("natural_log_exp_and_others")
                for g in range(4):
                    split(n + 16 + 2 * g + AHEAD)
                    if g == 0:
                        gate(S, 0)
                        gate(S, 1)
                    elif g < 3:
                        decays(g - 1, 0, (8, 4)[g - 1])
                    split(n + 16 + 2 * g + 1 + AHEAD)

            def gla():
                S = att[2]

                def key_end(c):
                    if c % 4 < 3:
                        act.wait_ge(S["turned"], states(c))
                        if c:
                            act.wait_ge(S["update_full"], states(c) - 1)
                        nc.scalar.activation(k_endT[:], bank[6][:, 0:CH], ACT.Copy).then_inc(S["k_endT"], 1)

                def head_squares(hd):
                    act.wait_ge(S["o_full"], 8 * hd + 8)
                    if hd:
                        act.wait_ge(S["o_lo"], 2 * hd)
                    nc.scalar.activation(o_head[0][:], bank[4][:], ACT.Copy).then_inc(S["o_copied_act"], 1)
                    act.wait_ge(S["o_copied_act"], hd + 1)
                    nc.scalar.activation(sq_head[0][:], o_head[0][:], ACT.Square)
                    act.wait_ge(S["o_copied_dve"], hd + 1)
                    nc.scalar.activation(sq_head[1][:], o_head[1][:], ACT.Square).then_inc(S["squared"], 1)

                def head_root(hd):
                    act.wait_ge(S["ss_full"], hd + 1)
                    root(rstd[:], bank[6][:], 1.0 / C_HV).then_inc(S["rs_ready"], 1)

                def head_hi(hd):
                    for v in range(2):
                        act.wait_ge(S["o_gated"], 2 * hd + v + 1)
                        nc.scalar.activation(h_hi[:, 2 * hd + v, :], o_head[v][:], ACT.Copy).then_inc(S["o_hi"], 1)

                for w in range(C_ITEMS):
                    if gates_at(w):
                        gate(S, gates_at(w))
                    key_end(2 * w)
                    if w + 1 < C_ITEMS:
                        decays(w + 1, 4, 8)
                    if w % 4 == 0 and w:
                        head_root(w // 4 - 1)
                    key_end(2 * w + 1)
                    if w + 2 < C_ITEMS:
                        decays(w + 2, 0, 4)
                    if w % 4 == 0 and w:
                        head_hi(w // 4 - 1)
                    if w % 4 == 3:
                        head_squares(w // 4)
                head_root(C_HEADS - 1)
                head_hi(C_HEADS - 1)

            for n in range(AHEAD):
                split(n)
            act.wait_ge(s_cond_t, 1)
            nc.scalar.activation(cond[:].rearrange("p s k -> p (s k)"), bank[4][:, 0:16], ACT.Silu).then_inc(s_cond_a, 1)
            act.wait_ge(s_cond_a, 1)
            for s in range(2):
                ins = nc.scalar.activation(cond4[:, :, 2 * s], cond[:, s, :], ACT.Copy)
            ins.then_inc(s_cond_a, 1)
            for n in range(16):
                split(n + AHEAD)
            act.wait_ge(s_lam_d, 1)
            nc.scalar.activation(small[:, 11:13], bank[5][:, 0:2], ACT.Exp).then_inc(s_lam_e, 1)
            for i in range(layers):
                st = 2 * i
                nc.scalar.preload_act_table_set("natural_log_exp_and_others")
                n, fg = start["qkv", i]
                make_h(st, cols(i, "head"), n + AHEAD)
                if i == 0:
                    qkv_norm_rope(n, fg)
                elif i == 2:
                    gla_tables()
                    qkv_gla(n, fg)
                else:
                    if i == 3:
                        for par in range(2):
                            for r in range(6):
                                act.dma_start(bias[64 * par:64 * par + 64, :, GRID_W * r:GRID_W * r + GRID_W],
                                              rpb_block((5, 4)[par] + r)).then_inc(s_bias_in, 16)
                        act.dma_start(window[:], a["k_window"]).then_inc(s_bias_in, 16)
                    qkv_plain(i, n, fg)
                gla() if i == 2 else attention(i)
                n, fg = start["wo", i]
                residual(st, n, fg, 1, cols(i, "tail"))
                make_h(st + 1, cols(i, "tail"), start["up", i][0] + AHEAD)
                nc.scalar.preload_act_table_set("silu_and_others")
                c = cols(i, "tail")
                n, fg = start["up", i]
                per = 8 if i + 1 < layers else 4

                def round_product(j, u):
                    act.wait_ge(s_gmul, FT * i + 1 + j)
                    nc.scalar.activation(g_hi[:, bass.ds(j, 1), c], g32[u][:, c].unsqueeze(1),
                                         ACT.Copy).then_inc(s_ghi, 1)

                def two_tiles(it, first=False):
                    for u in range(2):
                        for k in range(2):
                            at_slab = n + per // 2 * u + k
                            if not (first and u == k == 0):
                                split(at_slab + AHEAD, it, per)
                            act.wait_ge(s_used, at_slab + 1 + per * it)
                            tile = FT * k + u + 2 * it
                            nc.scalar.activation(
                                conv[k][u][:, c], bank[2 * u + k][:, c], ACT.Identity,
                                bias=prm[:, bass.ds(R_LAYER * i + R_CB + tile, 1)],
                                scale=prm[:, bass.ds(R_LAYER * i + R_CW + 2 * FT + tile, 1)]).then_inc(s_tap1, 1)
                        act.wait_ge(s_free["dve"], freed[fg][1] + 2 * u + 4 * it)
                        nc.scalar.activation(conv[0][u][:, c], conv[0][u][:, c], ACT.Silu).then_inc(s_silu, 1)
                        if not (first and u == 0):
                            round_product(2 * it - 1 + u, 1 - u)
                        for q in range(2 if per == 8 else 0):
                            split(n + 4 * u + 2 + q + AHEAD, it, per)

                two_tiles(0, first=True)
                with act.Fori(1, FT // 2) as it:
                    two_tiles(it)
                for q in range(PREMOD if per == 8 else 0):
                    split(start["postmod", i][0] + q + AHEAD)
                round_product(FT - 1, 1)
                n, fg = start["down", i]
                residual(st + 1, n, fg, 3, c)
            for k in range(DT):
                act.wait_ge(s_xn, DT * 2 * layers + k + 1)
                g, b = gain(2 * layers)
                nc.scalar.activation(out_f[:, k, :], xn[:, k, CTX:T], ACT.Identity, bias=b[:, k:k + 1],
                                     scale=g[:, k:k + 1]).then_inc(s_outf, 1)

        @block.vector
        def _(dve):
            step = Count(s_dve)

            def link(ins):
                step.up(ins)
                dve.wait_ge(s_dve, step.n)

            def split(n, it=0, per=0):
                if n >= n_slabs:
                    return
                slot = n % SLOTS
                dve.wait_ge(s_hi, n + 1 + per * it)
                w = SLAB if per else width(slabs[n])
                nc.vector.tensor_tensor(wlo[slot][:, 0:w], raw[slot][:, 0:w], whi[slot][:, 0:w].bitcast(f32),
                                        ALU.subtract).then_inc(s_lo, 1)

            def mod_row_copy(group, n):
                dve.wait_ge(s_used, n + 1)
                if group:
                    dve.wait_ge(s_mod_t, group)
                nc.vector.tensor_copy(mod_row[:], MOD_ACC[0:4, :]).then_inc(s_mod_row, 1)

            def mod_evacuate(i, c0, c1, turned):
                dve.wait_ge(s_mod_t, turned)
                v = MOD_T[:, 0:N_MOD * DT * 2].rearrange("p (c s) -> p c s", s=2)
                for s in range(2):
                    ins = nc.vector.tensor_tensor(modT[i % 2][:, c0:c1, s], v[:, c0:c1, s],
                                                  prm[:, R_LAYER * i + R_MODB + c0:R_LAYER * i + R_MODB + c1], ALU.add)
                ins.then_inc(s_mod_in, 1)

            def coefficients(st, events):
                dve.wait_ge(s_mod_in, events)
                cf, m = coef[st % 2], modT[st // 2 % 2]
                g, b = gain(st)
                sh, sc = mod(st, 0), mod(st, 1)
                for s in range(2):
                    nc.vector.scalar_tensor_tensor(cf[:, s, :], m[:, sc:sc + DT, s], 1.0, g, ALU.add, ALU.mult)
                    ins = nc.vector.scalar_tensor_tensor(cf[:, 2 + s, :], m[:, sc:sc + DT, s], 1.0, b, ALU.add, ALU.mult)
                link(ins)
                nc.vector.tensor_scalar(cf[:, 4, :], g, ALPHA, None, ALU.mult)
                nc.vector.tensor_scalar(cf[:, 5, :], b, ALPHA, None, ALU.mult)
                for s in range(2):
                    ins = nc.vector.tensor_tensor(cf[:, 2 + s, :], cf[:, 2 + s, :], m[:, sh:sh + DT, s], ALU.add)
                ins.then_inc(s_coef, 1)

            def scale_xn(st, k, c):
                dve.wait_ge(s_cen, DT * (st - 1) + k + 1)
                if k == 0:
                    dve.wait_ge(s_rstd, st)
                nc.vector.tensor_tensor(xn[:, k, c], xn[:, k, c], rstd[:, c], ALU.mult).then_inc(s_xn, 1)

            def modulate(st, k, c):
                if st:
                    scale_xn(st, k, c)
                if c.start == 0:
                    cf = coef[st % 2]
                    dve.wait_ge(s_xn, DT * st + k + 1)
                    if k == 0:
                        dve.wait_ge(s_coef, st + 1)
                    if k >= 2:
                        dve.wait_ge(s_hlo, DT * st + k - 1)
                    nc.vector.tensor_scalar(res_t[k % 2][:, CTX:T], xn[:, k, CTX:T], cf[:, 1, k:k + 1], cf[:, 3, k:k + 1],
                                            ALU.mult, ALU.add).then_inc(s_hf_lat, 1)

            def make_h(st, c, following=None):
                modulate(st, 0, c)
                for k in range(DT):
                    if k + 1 < DT:
                        modulate(st, k + 1, c)
                    dve.wait_ge(s_hhi, DT * st + k + 1)
                    nc.vector.tensor_tensor(h_lo[:, k, c], res_t[k % 2][:, c], h_hi[:, k, c].bitcast(f32),
                                            ALU.subtract).then_inc(s_hlo, 1)
                    if k == 5 and following is not None:
                        split(following)

            def residual(st, n, fg, per, c):

                def add_square(dt):
                    dve.wait_ge(s_sqd, DT * st + dt + 1)
                    if dt >= 2:
                        dve.wait_ge(s_qsum, 6 * st + dt - 1)
                    nc.vector.tensor_tensor(acc_q[:, c], acc_q[:, c], sq[:, c], ALU.add).then_inc(s_qsum, 1)

                for dt in range(DT):
                    for q in range(per):
                        split(n + q + AHEAD)
                    n += per
                    dve.wait_ge(s_free["act"], freed[fg + dt][1])
                    nc.vector.scalar_tensor_tensor(xn[:, dt, c], xn[:, dt, c], coef[st % 2][:, 4, dt:dt + 1],
                                                   res_t[dt % 2][:, c], ALU.mult, ALU.add).then_inc(s_y, 1)
                    if dt >= 2:
                        add_square(dt - 1)
                    if dt == 1 and st % 2 and st // 2 + 1 < layers:
                        mod_evacuate(st // 2 + 1, 0, N_MOD * DT, 12 * (st // 2 + 2))
                    for m in mods_after("wo", dt) if st == 0 else ():
                        split(n + AHEAD)
                        n += 1
                        if m % 4 == 3:
                            mod_row_copy(4 + m // 4, n - 1)
                if st == 0:
                    mod_evacuate(0, 36, 48, 12)
                premod = st % 2 == 0 and st // 2 + 1 < layers
                if premod:
                    split(n + AHEAD)
                dve.wait_ge(s_stats, st + 1)
                nc.vector.tensor_scalar(mean[:, c], LN_SUM[:, c], 1.0 / D, None, ALU.mult).then_inc(s_mean, 1)
                dve.wait_ge(s_mean, st + 1)
                link(nc.vector.scalar_tensor_tensor(acc_s[:, c], mean[:, c], -1.0, mean[:, c], ALU.mult, ALU.mult))
                link(nc.vector.scalar_tensor_tensor(acc_q[:, c], LN_SQ[:, c], 1.0 / D, acc_s[:, c], ALU.mult, ALU.add))
                nc.vector.tensor_scalar(acc_q[:, c], acc_q[:, c], 0.0, LN_EPS, ALU.max, ALU.add).then_inc(s_var, 1)
                if premod:
                    split(n + 1 + AHEAD)

            def v_out(n, fg, groups):
                for g in range(groups):
                    for q in range(2):
                        split(n + 2 * g + q + AHEAD)
                    values(n, fg, g)

            def values(n, fg, g):
                dve.wait_ge(s_used, n + 2 * g + 2)
                for half in range(2):
                    nc.vector.tensor_copy(v_tok[:, 2 * half:2 * half + 2, 256 * g:256 * g + 256],
                                          bank[(fg + 2 * g + half) % 4][:].rearrange("p (t c) -> p t c", t=2)
                                          ).then_inc(s_free["dve"], 1)

            def rope(S, ft, ps, tmp):
                dve.wait_ge(S["swapped"], ft + 1)
                if ft:
                    dve.wait_ge(S["qk_ready"], ft)
                nc.vector.tensor_tensor(tmp[:], ps, sin, ALU.mult)
                link(nc.vector.tensor_tensor(qk[:, ft, CTX:T], qk[:, ft, CTX:T], cos, ALU.mult))
                nc.vector.tensor_tensor(qk[:, ft, CTX:T], qk[:, ft, CTX:T], tmp[:], ALU.add).then_inc(S["qk_ready"], 1)

            def qkv_norm_rope(n, fg):
                S = att[0]

                def norm(ft):
                    dve.wait_ge(S["rs_ready"], ft + 1)
                    nc.vector.scalar_tensor_tensor(qk[:, ft, :], bank[(fg + ft) % 4][:],
                                                   small[:, 14:15] if ft < 8 else small[:, 1:2],
                                                   rsa[ft % 2][:], ALU.mult, ALU.mult).then_inc(s_free["dve"], 1)

                for ft in range(10):
                    if ft:
                        split(n + AHEAD)
                    n += 1
                    if ft >= 1:
                        norm(ft - 1)
                    if ft >= 2:
                        rope(S, ft - 2, bank[5][:, 0:LAT], rope_t)
                    for m in mods_after("qkv", ft):
                        split(n + AHEAD)
                        n += 1
                        if m % 4 == 3:
                            mod_row_copy(4 + m // 4, n - 1)
                norm(9)
                rope(S, 8, bank[5][:, 0:LAT], rope_t)
                rope(S, 9, bank[5][:, 0:LAT], rope_t)
                v_out(n, fg + 10, 1)
                mod_evacuate(0, 16, 36, 9)

            def qkv_plain(i, n, fg):
                S = att[i]
                for ft in range(16):
                    if ft:
                        split(n + ft + AHEAD)
                    if i == 1 and ft >= 1:
                        rope(S, ft - 1, bank[4 + (ft - 1) % 2][:, 0:LAT], rope_b)
                if i == 1:
                    rope(S, 15, bank[5][:, 0:LAT], rope_b)
                v_out(n + 16, fg + 16, 4)

            def attention(i):
                S, U = att[i], attention_units(i)
                maps = 2 if i == 1 else 1
                per_o = len(U) // DT

                def add_bias(u):
                    if u < len(U):
                        hd, s, q0 = U[u]
                        dve.wait_ge(S["score_full"], u + 1)
                        if u >= MAPS:
                            dve.wait_ge(S["p_turned"], u - MAPS + 1)
                        r = 2 * GRID_W if q0 == CTX else 0
                        nc.vector.tensor_tensor(p1[u % MAPS][:, CTX:T], bank[u % 4][:, CTX:T],
                                                bias[:, hd, r:r + LAT], ALU.add).then_inc(S["biased"], 1)

                if i == 3:
                    add_bias(0)
                for u in range(len(U) + TURN + 7):
                    if u < len(U):
                        hd, s, q0 = U[u]
                        nk = CTX if s == 0 else T
                        if i == 3:
                            add_bias(u + 1)
                            dve.wait_ge(S["biased"], u + 1)
                            dve.wait_ge(S["context_copied"], u + 1)
                            nc.vector.tensor_reduce(stat[:, 0, u:u + 1], p1[u % MAPS][:], AX, ALU.max,
                                                    negate=True).then_inc(S["negmax"], 1)
                        else:
                            for m in range(maps):
                                dve.wait_ge(S["score_full"], maps * u + m + 1)
                                b = bank[(2 * u + m) % 4] if maps == 2 else bank[u % 4]
                                nc.vector.tensor_reduce(stat[:, m, u:u + 1], b[:, 0:nk], AX, ALU.max,
                                                        negate=True).then_inc(S["negmax"], 1)
                    w = u - 1
                    if 0 <= w < len(U):
                        nk = CTX if U[w][1] == 0 else T
                        dve.wait_ge(S["exped"], maps * (w + 1))
                        for m in range(maps):
                            ins = nc.vector.reciprocal(stat[:, 4 + m, w:w + 1], stat[:, 2 + m, w:w + 1])
                        link(ins)
                        r1 = stat[:, 4, w:w + 1]
                        if maps == 1:
                            nc.vector.tensor_scalar(p1[w % MAPS][:, 0:nk], p1[w % MAPS][:, 0:nk], r1, None,
                                                    ALU.mult).then_inc(S["p_ready"], 1)
                        else:
                            nc.vector.tensor_scalar(p1[w % MAPS][:, 0:nk], p1[w % MAPS][:, 0:nk], r1, None, ALU.mult)
                            link(nc.vector.tensor_tensor(stat[:, 5, w:w + 1], stat[:, 5, w:w + 1], small[:, 13:14],
                                                         ALU.mult))
                            nc.vector.scalar_tensor_tensor(p1[w % MAPS][:, 0:nk], p2[w % MAPS][:, 0:nk],
                                                           stat[:, 5, w:w + 1], p1[w % MAPS][:, 0:nk],
                                                           ALU.mult, ALU.add).then_inc(S["p_ready"], 1)
                    w = u - TURN - 5
                    if i == 1 and 0 <= w < len(U) and w % per_o == per_o - 1:
                        o = w // per_o
                        dve.wait_ge(S["rs_ready"], o + 1)
                        if o:
                            dve.wait_ge(S["o_lo"], o)
                        nc.vector.scalar_tensor_tensor(o32[:], bank[6 + o % 2][:], small[:, 15:16], rsb[:],
                                                       ALU.mult, ALU.mult).then_inc(S["o_normed"], 1)
                    w = u - TURN - (6 if i == 1 else 3)
                    if 0 <= w < len(U) and w % per_o == per_o - 1:
                        o = w // per_o
                        c = slice(CTX, T) if i == 3 else slice(0, T)
                        dve.wait_ge(S["o_hi"], o + 1)
                        lo, source, hi = h_lo[:, o, c], (o32 if i == 1 else bank[6 + o % 2])[:, c], h_hi[:, o, c].bitcast(f32)
                        if i == 3:
                            rows_of = "p (r c) -> p r c"
                            lo, source, hi = lo.rearrange(rows_of, c=GRID_W), mirrored(source), hi.rearrange(rows_of, c=GRID_W)
                        nc.vector.tensor_tensor(lo, source, hi, ALU.subtract).then_inc(S["o_lo"], 1)

            def gate(S, u):
                b = 16 + C_HEADS * (u % 2) + u // 2
                dve.wait_ge(S["gate_soft"], u + 1)
                if u:
                    dve.wait_ge(S["cum"], u)
                nc.vector.tensor_scalar(gate_min[:], bank[7][:], small[:, b:b + 1], 0.0, ALU.add,
                                        ALU.min).then_inc(S["gate_min"], 1)

            def gate_sums(S, u):
                bwd = u % 2
                if u >= 2:
                    dve.wait_ge(S["decay"], 16 * (u - 1))
                dve.wait_ge(S["gate_min"], u + 1)
                link(nc.vector.tensor_tensor(gate_min[:], gate_min[:], soft[:], ALU.subtract))
                for c in range(4):
                    v = slice(CH * c, CH * c + CH)
                    src_c, dst_c = gate_min[:, v], cum[u % 2][:, v]
                    if bwd:
                        src_c, dst_c = src_c[:, ::-1], dst_c[:, ::-1]
                    ins = nc.vector.tensor_tensor_scan(dst_c, ones, src_c, 0.0, ALU.mult, ALU.add)
                ins.then_inc(S["cum"], 1)

            def query(w, l):
                S = att[2]
                hd, bwd, cw = item_of(w)
                j = 8 * w + l
                dve.wait_ge(S["decay"], j + 1)
                if l < LEVELS:
                    if l == 0 and w >= 2:
                        dve.wait_ge(S["score_full"], 2 * w - 2)
                    dst = (left if bwd else right)[w % 2][:, l, :]
                    nc.vector.tensor_tensor(half(dst, l, not bwd), half(qk[:, hd, cw], l, not bwd),
                                            half(rel[j % REL][:], l, not bwd), ALU.mult).then_inc(S["q_dec"], 1)
                else:
                    if w >= 2:
                        dve.wait_ge(S["o_full"], 2 * w - 2)
                    nc.vector.tensor_tensor(q_dec[w % 2][:], qk[:, hd, cw], start_dec[w % 2][:],
                                            ALU.mult).then_inc(S["q_dec"], 1)

            def build(w, l0, l1):
                for l in range(l0, l1):
                    query(w, l)

            def qkv_gla(n, fg):
                S = att[2]
                for ft in range(16):
                    if ft:
                        split(n + ft + AHEAD)
                    if ft == 5:
                        dve.wait_ge(S["z_hi"], 1)
                        nc.vector.tensor_tensor(z_lo[:], z_raw[:], z_hi[:].bitcast(f32), ALU.subtract).then_inc(S["z_lo"], 1)
                dve.wait_ge(S["z_full"], 1)
                nc.vector.tensor_copy(zT[:], bank[4][0:64, :]).then_inc(S["z_copied"], 1)
                for g in range(4):
                    split(n + 16 + 2 * g + AHEAD)
                    if g == 0:
                        for u in range(2):
                            gate(S, u)
                            gate_sums(S, u)
                        dve.wait_ge(s_free["act"], freed[fg + 15][1])
                        dve.wait_ge(S["zeroed"], 2)
                    elif g < 3:
                        build(g - 1, 0, (8, 4)[g - 1])
                    split(n + 16 + 2 * g + 1 + AHEAD)
                    values(n + 16, fg + 16, g)

            def gla():
                S = att[2]

                def add_levels(c):
                    dve.wait_ge(S["score_full"], c + 1)
                    if c >= 2:
                        dve.wait_ge(S["scores"], c - 1)
                    for h, v in enumerate((slice(0, 4), slice(4, PLANES))):
                        ps = bank[2 * (c % 2) + h][:].rearrange("p (l i) -> p l i", l=4)
                        ins = nc.vector.tensor_tensor(masked[c % 2][:, v, :], ps[:, 0:v.stop - v.start, :],
                                                      same_block[:, v, :], ALU.mult)
                    ins.then_inc(S["masked"], 1)
                    dve.wait_ge(S["masked"], c + 1)
                    if c:
                        dve.wait_ge(S["o_full"], c)
                    nc.vector.tensor_reduce(scores[:], masked[c % 2][:].rearrange("p l i -> p i l"), AX,
                                            ALU.add).then_inc(S["scores"], 1)

                def next_state(c):
                    if c % 4 == 3:
                        return
                    hd, bwd, p, ci, cs = chunk_of(c)
                    dve.wait_ge(S["update_full"], states(c))
                    if c % 4 == 0:
                        nc.vector.tensor_copy(state[0][:], bank[7][:, 0:C_HV]).then_inc(S["state"], 1)
                    else:
                        dve.wait_ge(S["state"], states(c) - 1)
                        end = ci.start if bwd else ci.stop - 1
                        nc.vector.scalar_tensor_tensor(state[c % 4 % 2][:], state[(c % 4 - 1) % 2][:],
                                                       start_dec[c // 2 % 2][:, end:end + 1], bank[7][:, 0:C_HV],
                                                       ALU.mult, ALU.add).then_inc(S["state"], 1)

                def head_copy(hd):
                    dve.wait_ge(S["o_full"], 8 * hd + 8)
                    if hd:
                        dve.wait_ge(S["o_lo"], 2 * hd)
                    nc.vector.tensor_copy(o_head[1][:], bank[5][:]).then_inc(S["o_copied_dve"], 1)

                def head_gated(hd):
                    dve.wait_ge(S["rs_ready"], hd + 1)
                    for v in range(2):
                        nc.vector.scalar_tensor_tensor(o_head[v][:], o_head[v][:], small[:, 3 + v:4 + v], rstd[:],
                                                       ALU.mult, ALU.mult).then_inc(S["o_normed"], 1)
                    for v in range(2):
                        dve.wait_ge(S["o_normed"], 2 * hd + v + 1)
                        nc.vector.tensor_tensor(o_head[v][:], o_head[v][:], qk[:, 8 + 2 * hd + v, :],
                                                ALU.mult).then_inc(S["o_gated"], 1)

                def head_lo(hd):
                    for v in range(2):
                        dve.wait_ge(S["o_hi"], 2 * hd + v + 1)
                        nc.vector.tensor_tensor(h_lo[:, 2 * hd + v, :], o_head[v][:],
                                                h_hi[:, 2 * hd + v, :].bitcast(f32), ALU.subtract).then_inc(S["o_lo"], 1)

                for w in range(C_ITEMS):
                    add_levels(2 * w)
                    if gates_at(w):
                        gate(S, gates_at(w))
                    if w + 1 < C_ITEMS:
                        build(w + 1, 4, 8)
                    if gates_at(w):
                        gate_sums(S, gates_at(w))
                    next_state(2 * w)
                    add_levels(2 * w + 1)
                    if w + 2 < C_ITEMS:
                        build(w + 2, 0, 4)
                    next_state(2 * w + 1)
                    if w % 4 == 0 and w:
                        head_gated(w // 4 - 1)
                    if w % 4 == 1 and w > 1:
                        head_lo(w // 4 - 1)
                    if w % 4 == 3:
                        head_copy(w // 4)
                head_gated(C_HEADS - 1)
                head_lo(C_HEADS - 1)

            nc.vector.memset(unit_gb[:, 0, :], 1.0)
            link(nc.vector.memset(unit_gb[:, 1, :], 0.0))
            for n in range(AHEAD):
                split(n)
            dve.wait_ge(s_cond_a, 2)
            for s in range(2):
                ins = nc.vector.tensor_tensor(cond4[:, :, 2 * s + 1], cond[:, s, :],
                                              cond4[:, :, 2 * s].bitcast(f32), ALU.subtract)
            ins.then_inc(s_cond_v, 1)
            dve.wait_ge(s_cond_t, 2)
            link(nc.vector.tensor_copy(small[:], bank[5][:, 0:32]))
            nc.vector.tensor_tensor(small[0:HD, 9:10], small[0:HD, 5:6], small[0:HD, 6:7], ALU.mult)
            nc.vector.tensor_tensor(small[0:HD, 10:11], small[0:HD, 7:8], small[0:HD, 8:9], ALU.mult).then_inc(s_lam_p, 1)
            nc.vector.tensor_scalar(small[:, 14:15], small[:, 0:1], SCALE, None, ALU.mult)
            link(nc.vector.tensor_scalar(small[:, 15:16], small[:, 2:3], 1.0 - LAM_INIT, None, ALU.mult))
            for g in range(4):
                for q in range(4):
                    split(4 * g + q + AHEAD)
                mod_row_copy(g, 4 * g + 3)
                if g == 0:
                    for b in range(2):
                        dve.wait_ge(s_rows_t, b + 1)
                        nc.vector.tensor_copy(prm[:, NB * b:NB * b + NB], bank[2 + b][:]).then_inc(s_rows_v, 1)
                if g in (1, 2):
                    for k in range(4 * g - 4, 4 * g):
                        dve.wait_ge(s_tok_t, k + 1)
                        nc.vector.tensor_copy(xn[:, k, :], bank[k % 2][:]).then_inc(s_xn, 1)
            dve.wait_ge(s_rows_v, 2)
            dve.wait_ge(s_lam_e, 1)
            link(nc.vector.tensor_tensor(small[:, 13:14], small[:, 12:13], small[:, 11:12], ALU.subtract))
            link(nc.vector.tensor_scalar(small[:, 13:14], small[:, 13:14], LAM_INIT, None, ALU.subtract))
            mod_evacuate(0, 0, 16, 4)
            for i in range(layers):
                st = 2 * i
                coefficients(st, mod_events(i, 0))
                n, fg = start["qkv", i]
                make_h(st, cols(i, "head"), n + AHEAD)
                if i == 0:
                    qkv_norm_rope(n, fg)
                elif i == 2:
                    qkv_gla(n, fg)
                else:
                    qkv_plain(i, n, fg)
                gla() if i == 2 else attention(i)
                n, fg = start["wo", i]
                c = cols(i, "tail")
                residual(st, n, fg, 1, c)
                coefficients(st + 1, mod_events(i, 2))
                make_h(st + 1, c, start["up", i][0] + AHEAD)
                n, fg = start["up", i]
                per = 8 if i + 1 < layers else 4

                def round_rest(j, u):
                    dve.wait_ge(s_ghi, FT * i + 1 + j)
                    nc.vector.tensor_tensor(g_lo[:, bass.ds(j, 1), c], g32[u][:, c].unsqueeze(1),
                                            g_hi[:, bass.ds(j, 1), c].bitcast(f32), ALU.subtract).then_inc(s_glo, 1)

                def two_tiles(it, first=False):
                    for u in range(2):
                        for k in range(2):
                            at_slab = n + per // 2 * u + k
                            if not (first and u == k == 0):
                                split(at_slab + AHEAD, it, per)
                            if per == 8 and u == 1 and k == 0:
                                dve.wait_ge(s_used, n + 4 + per * it)
                                dve.wait_ge(s_mod_t, 12 * (i + 1) + it)
                                nc.vector.tensor_copy(mod_row[:], MOD_ACC[0:4, :]).then_inc(s_mod_row, 1)
                            group = 2 * u + k
                            dve.wait_ge(s_tap1, 2 * FT * i + group + 1 + 4 * it)
                            w = R_LAYER * i + R_CW + FT * k + u + 2 * it
                            runs = "p (s t) -> p s t"
                            ps = bank[group][:, c].rearrange(runs, t=LAT)
                            dst = conv[k][u][:, c].rearrange(runs, t=LAT)
                            nc.vector.scalar_tensor_tensor(dst[:, :, 1:LAT], ps[:, :, 0:LAT - 1], prm[:, bass.ds(w, 1)],
                                                           dst[:, :, 1:LAT], ALU.mult, ALU.add).then_inc(s_tap2, 1)
                            dve.wait_ge(s_tap2, 2 * FT * i + group + 1 + 4 * it)
                            nc.vector.scalar_tensor_tensor(dst[:, :, 0:LAT - 1], ps[:, :, 1:LAT],
                                                           prm[:, bass.ds(4 * FT + w, 1)],
                                                           dst[:, :, 0:LAT - 1], ALU.mult, ALU.add).then_inc(s_free["dve"], 1)
                        if not (first and u == 0):
                            round_rest(2 * it - 1 + u, 1 - u)
                        if per == 8:
                            for q in range(2):
                                split(n + 4 * u + 2 + q + AHEAD, it, per)

                two_tiles(0, first=True)
                with dve.Fori(1, FT // 2) as it:
                    two_tiles(it)
                n, fg = start["postmod", i]
                for q in range(PREMOD if i + 1 < layers else 0):
                    split(n + q + AHEAD)
                round_rest(FT - 1, 1)
                if i + 1 < layers:
                    mod_row_copy(12 * (i + 1) + 11, n + 1)
                n, fg = start["down", i]
                residual(st + 1, n, fg, 3, c)
            for k in range(DT):
                scale_xn(2 * layers, k, slice(CTX, T))
            for q in range(4):
                dve.wait_ge(s_outt, q + 1)
                nc.vector.tensor_copy(out_tok[:, q // 2, NB * (q % 2):NB * (q % 2) + NB], bank[q][:]).then_inc(s_outv, 1)

        @block.gpsimd
        def _(pool):
            def residual(st, c):
                for dt in range(DT - 1):
                    pool.wait_ge(s_y, DT * st + dt + 1)
                    if dt == 0:
                        nc.gpsimd.tensor_copy(acc_s[:, c], xn[:, 0, c]).then_inc(s_sum, 1)
                    else:
                        pool.wait_ge(s_sum, 7 * st + dt)
                        nc.gpsimd.tensor_tensor(acc_s[:, c], acc_s[:, c], xn[:, dt, c], ALU.add).then_inc(s_sum, 1)
                pool.wait_ge(s_mean, st + 1)
                for k in range(DT):
                    nc.gpsimd.tensor_tensor(xn[:, k, c], xn[:, k, c], mean[:, c], ALU.subtract).then_inc(s_cen, 1)

            def gla():
                S = att[2]
                nc.gpsimd.memset(z_raw[:], 0.0).then_inc(S["zeroed"], 1)
                for s in range(2):
                    nc.gpsimd.memset(right[s][:], 0.0)
                    ins = nc.gpsimd.memset(left[s][:], 0.0)
                ins.then_inc(S["zeroed"], 1)
                pool.wait_ge(S["zeroed"], 2)
                pool.wait_ge(s_free["act"], freed[start["qkv", 2][1] + 15][1])

                def relative(w, l):
                    hd, bwd, cw = item_of(w)
                    j = 8 * w + l
                    if l in (0, LEVELS):
                        return
                    if j >= REL:
                        pool.wait_ge(S["k_dec"], j - REL + 1)
                        pool.wait_ge(S["q_dec"], j - REL + 1)
                    if w % 2 == 0 and l == 1:
                        pool.wait_ge(S["cum"], w // 2 + 1)
                    s = 64 >> l
                    ref = s if bwd else s - 1
                    v = cum[w // 2 % 2][:, cw].rearrange("p (n s) -> p n s", s=2 * s)
                    nc.gpsimd.tensor_tensor(rel[j % REL][:].rearrange("p (n s) -> p n s", s=2 * s), v,
                                            v[:, :, ref:ref + 1].broadcast_to([P, CH // s, 2 * s]),
                                            ALU.subtract).then_inc(S["rel"], 1)

                for l in range(REL_AHEAD):
                    relative(0, l)
                for w in range(C_ITEMS):
                    hd, bwd, cw = item_of(w)
                    for l in range(8):
                        j = 8 * w + l
                        if j + REL_AHEAD < 8 * C_ITEMS:
                            relative((j + REL_AHEAD) // 8, (j + REL_AHEAD) % 8)
                        pool.wait_ge(S["decay"], j + 1)
                        if l < LEVELS:
                            if l == 0 and w >= 2:
                                pool.wait_ge(S["score_full"], 2 * w - 2)
                            dst = (right if bwd else left)[w % 2][:, l, :]
                            nc.gpsimd.tensor_tensor(half(dst, l, bwd), half(qk[:, 4 + hd, cw], l, bwd),
                                                    half(rel[j % REL][:], l, bwd), ALU.mult).then_inc(S["k_dec"], 1)
                        else:
                            if w >= 2:
                                pool.wait_ge(S["turned"], states(2 * w - 3))
                            nc.gpsimd.tensor_tensor(k_end[w % 2][:], qk[:, 4 + hd, cw], rel[j % REL][:],
                                                    ALU.mult).then_inc(S["k_dec"], 1)

            for i in range(layers):
                c = cols(i, "tail")
                if i == 2:
                    gla()
                if i == 3:
                    pool.wait_ge(s_bias_in, 16 * 13)
                    v = bias[:].rearrange("p h (r c) -> p (h r) c", c=GRID_W)
                    nc.gpsimd.tensor_tensor(v, v, window[:].unsqueeze(1).broadcast_to([P, 6 * D_HEADS, GRID_W]),
                                            ALU.add).then_inc(s_window, 1)
                residual(2 * i, c)
                n, fg = start["up", i]
                with pool.Fori(0, FT // 2) as it:
                    for u in range(2):
                        pool.wait_ge(s_silu, FT * i + u + 1 + 2 * it)
                        pool.wait_ge(s_free["dve"], freed[fg][1] + 2 * u + 1 + 4 * it)
                        nc.gpsimd.tensor_tensor(g32[u][:, c], conv[0][u][:, c], conv[1][u][:, c],
                                                ALU.mult).then_inc(s_gmul, 1)
                residual(2 * i + 1, c)

        @block.tensor
        def _(pe):
            mm = nc.tensor.matmul

            def three(out, w_hi, w_lo, x_hi, x_lo, first, last, moving_w=False):
                for n, (w, x) in enumerate(((w_hi, x_hi), (w_hi, x_lo), (w_lo, x_hi))):
                    l, r = (x, w) if moving_w else (w, x)
                    ins = mm(out, l, r, start=first and n == 0, stop=last and n == 2)
                return ins

            def split_ready(n, it=0, per=0):
                pe.wait_ge(s_hi, n + 1 + per * it)
                pe.wait_ge(s_lo, n + 1 + per * it)

            def project_pair(n, outs, x_hi, x_lo, c, ready):
                split_ready(n + 1)
                for k in range(DT):
                    pe.wait_ge(ready[0], ready[1] + k + 1)
                    for j in range(2):
                        slot, wc = (n + j) % SLOTS, slice(k * P, (k + 1) * P)
                        ins = three(outs[j][:, c], whi[slot][:, wc], wlo[slot][:, wc], x_hi[:, k, c], x_lo[:, k, c],
                                    k == 0, k == DT - 1)
                        if k == DT - 1:
                            ins.then_inc(s_used, 1)

            def project(n, out, x_hi, x_lo, c, k0=0, nk=8, first=True, last=True, ready=None, it=0, per=0):
                split_ready(n, it, per)
                slot = n % SLOTS
                for k in range(nk):
                    if ready:
                        pe.wait_ge(ready[0], ready[1] + k0 + k + 1)
                    wc = slice(k * P, (k + 1) * P)
                    ins = three(out[:, c], whi[slot][:, wc], wlo[slot][:, wc], x_hi[:, k0 + k, c], x_lo[:, k0 + k, c],
                                first and k == 0, last and k == nk - 1)
                ins.then_inc(s_used, 1)

            def group_free(fg):
                if fg >= 4:
                    who, count = freed[fg - 4]
                    pe.wait_ge(s_free[who], count)

            def mod_slab(n, group, q, it=0, per=0):
                split_ready(n, it, per)
                if q == 0 and group:
                    pe.wait_ge(s_mod_row, group + it)
                slot = n % SLOTS
                for k in range(2):
                    for part, w in enumerate((whi, wlo)):
                        ins = mm(MOD_ACC[0:4, :], cond4[:, 2 * q + k, :], w[slot][:, NB * k:NB * k + NB],
                                 start=q == 0 and k == 0 and part == 0, stop=q == 3 and k == 1 and part == 1)
                ins.then_inc(s_used, 1)

            def mod_turn(group, it=0):
                pe.wait_ge(s_mod_row, group + 1 + it)
                g = group % 12
                if group in (4, 9):
                    pe.wait_ge(s_mod_in, 1 if group == 4 else 2)
                elif group >= 12 and g == 0 and isinstance(it, int):
                    pe.wait_ge(s_mod_in, group // 12 + 2)
                for b in range(4):
                    ins = mm(MOD_T[:, bass.ds(8 * g + 2 * b + 8 * it, 2)], mod_row[:, b * P:(b + 1) * P], sel,
                             start=True, stop=True)
                ins.then_inc(s_mod_t, 1)

            def stats(st, c):
                pe.wait_ge(s_sum, 7 * (st + 1))
                mm(LN_SUM[:, c], ones, acc_s[:, c], start=True, stop=False)
                pe.wait_ge(s_qsum, 6 * (st + 1))
                mm(LN_SQ[:, c], ones, acc_q[:, c], start=True, stop=False)
                pe.wait_ge(s_y, DT * (st + 1))
                mm(LN_SUM[:, c], ones, xn[:, DT - 1, c], start=False, stop=True)
                pe.wait_ge(s_sqd, DT * (st + 1))
                mm(LN_SQ[:, c], ones, sq[:, c], start=False, stop=True).then_inc(s_stats, 1)

            def v_project(n, fg, groups, between={}):
                for g in range(groups):
                    split_ready(n + 1)
                    for tt in range(4):
                        if g == 0 and tt in between:
                            between[tt]()
                        if tt % 2 == 0:
                            group_free(fg + tt // 2)
                        out = bank[(fg + tt // 2) % 4][:, 256 * (tt % 2):256 * (tt % 2) + 256]
                        for k in range(DT):
                            slot, wc = (n + k // 4) % SLOTS, slice(256 * (k % 4), 256 * (k % 4) + 256)
                            tc = slice(tt * P, tt * P + P)
                            ins = three(out, whi[slot][:, wc], wlo[slot][:, wc], h_hi[:, k, tc], h_lo[:, k, tc],
                                        k == 0, k == DT - 1, moving_w=True)
                            if tt == 3 and k % 4 == 3:
                                ins.then_inc(s_used, 1)
                    n, fg = n + 2, fg + 2

            def swapped(S, ft, ps):
                mm(ps, swap, qk[:, ft, CTX:T], start=True, stop=True).then_inc(S["swapped"], 1)

            def qkv_norm_rope(n, fg):
                S = att[0]

                def squares(ft):
                    pe.wait_ge(S["squared_h"], ft + 1)
                    if ft:
                        pe.wait_ge(S["rs_ready"], ft)
                    mm(bank[4][:], heads, sqa[ft % 2][:], start=True, stop=True).then_inc(S["ss_full"], 1)

                def turn(ft):
                    pe.wait_ge(s_free["dve"], freed[fg + ft][1])
                    if ft:
                        pe.wait_ge(S["qk_ready"], ft)
                    swapped(S, ft, bank[5][:, 0:LAT])

                for ft in range(10):
                    group_free(fg + ft)
                    project(n, bank[(fg + ft) % 4], h_hi, h_lo, slice(0, T), ready=(s_hlo, 0) if ft == 0 else None)
                    n += 1
                    if ft:
                        squares(ft - 1)
                    if ft >= 2:
                        turn(ft - 2)
                    for m in mods_after("qkv", ft):
                        if m % 4 == 0 and m:
                            mod_turn(3 + m // 4)
                        mod_slab(n, 4 + m // 4, m % 4)
                        n += 1
                squares(9)
                v_project(n, fg + 10, 1, between={1: lambda: turn(8), 3: lambda: turn(9)})
                mod_turn(8)

            def qkv_plain(i, n, fg):
                S = att[i]
                for ft in range(16):
                    c = slice(CTX, T) if i == 3 and ft < 8 else slice(0, T)
                    group_free(fg + ft)
                    if ft == 1:
                        project_pair(n, (bank[fg % 4], bank[(fg + 1) % 4]), h_hi, h_lo, c, (s_hlo, 2 * i * DT))
                    elif ft:
                        project(n + ft, bank[(fg + ft) % 4], h_hi, h_lo, c)
                    if i == 1 and ft:
                        turn(S, ft - 1, fg)
                if i == 1:
                    turn(S, 15, fg)
                v_project(n + 16, fg + 16, 4)

            def turn(S, ft, fg):
                pe.wait_ge(s_free["act"], freed[fg + ft][1])
                if ft >= 2:
                    pe.wait_ge(S["qk_ready"], ft - 1)
                swapped(S, ft, bank[4 + ft % 2][:, 0:LAT])

            def attention(i):
                S, U = att[i], attention_units(i)
                maps = 2 if i == 1 else 1
                per_o = len(U) // DT
                c = slice(CTX, T) if i == 3 else slice(0, T)
                if i == 3:
                    n_last = freed[start["wo", i][1] - 9]
                    pe.wait_ge(s_free["act"], n_last[1])
                    pe.wait_ge(s_window, 1)
                else:
                    pe.wait_ge(S["qk_ready"], 10 if i == 0 else 16)
                if i == 0:
                    pe.wait_ge(s_kd, 1)
                pe.wait_ge(s_free["dve"], freed[start["wo", i][1] - 1][1])

                def score(u):
                    if not 0 <= u < len(U):
                        return
                    hd, s, q0 = U[u]
                    nk = CTX if s == 0 else T
                    if maps == 1 and u >= 4:
                        pe.wait_ge(S["context_copied" if i == 3 else "exped"], u - 3)
                    if maps == 2 and u >= 2:
                        pe.wait_ge(S["exped"], 2 * (u - 1))
                    for m in range(maps):
                        if i == 1:
                            r, qt, b = slice(HD * m, HD * m + HD), hd, bank[(2 * u + m) % 4]
                            keys = qk[r, 8 + hd, 0:nk]
                        else:
                            r, qt, b = slice(HD * (hd % 2), HD * (hd % 2) + HD), hd // 2, bank[u % 4]
                            keys = kd[r, hd // (A_HEADS // A_KV), 0:nk] if i == 0 else qk[r, 8 + qt, 0:nk]
                        mm(b[:, 0:nk], qk[r, qt, q0:q0 + P], keys, start=True, stop=True).then_inc(S["score_full"], 1)

                for u in range(-1, len(U) + TURN + 4):
                    if maps == 1:
                        score(u + 1)
                    w = u - TURN
                    if 0 <= w < len(U):
                        ring = 1 if i == 1 else 2
                        pe.wait_ge(S["p_ready"], w + 1)
                        if w >= ring:
                            pe.wait_ge(S["pt_ready"], w + 1 - ring)
                        pb = bank[4] if i == 1 else bank[4 + w % 2]
                        for kt in range(2 if U[w][1] == 0 else 4):
                            ins = nc.tensor.transpose(pb[:, kt * P:kt * P + P], p1[w % MAPS][:, kt * P:kt * P + P], ident)
                        ins.then_inc(S["p_turned"], 1)
                    if maps == 2:
                        score(u + 1)
                    w = u - TURN - 2
                    if 0 <= w < len(U) and w % 2 == 0:
                        p = w // 2
                        hd, s, _ = U[2 * p]
                        o = 2 * p // per_o
                        pe.wait_ge(S["pt_ready"], 2 * p + 2)
                        if o >= 2:
                            pe.wait_ge(S["o_lo"], o - 1)
                        if i == 1:
                            out, vc = bank[6 + o % 2][:, CTX * s:CTX * s + 256], slice(2 * HD * hd, 2 * HD * hd + 2 * HD)
                        else:
                            r0 = HD * (hd % 2)
                            vh = hd // (A_HEADS // A_KV) if i == 0 else hd
                            out, vc = bank[6 + o % 2][r0:r0 + HD, CTX * s:CTX * s + 256], slice(HD * vh, HD * vh + HD)
                        kts = 2 if s == 0 else 4
                        for kt in range(kts):
                            ins = mm(out, v_tok[:, kt, vc], pt[p % 2][:, kt, :], start=kt == 0, stop=kt == kts - 1)
                        ins.then_inc(S["pv_full"], 1)
                    w = u - TURN - 4
                    if i == 1 and w >= 0 and w % per_o == per_o - 1:
                        o = w // per_o
                        pe.wait_ge(S["squared_h"], o + 1)
                        mm(bank[5][:], ones, sqb[:], start=True, stop=True).then_inc(S["ss_full"], 1)

            def gate(S, u):
                if u:
                    pe.wait_ge(S["gate_soft"], u)
                    pe.wait_ge(S["gate_min"], u)
                if u >= 2:
                    pe.wait_ge(S["state"], states(4 * u - 7))
                rows_u = slice(32 * (u % 2), 32 * (u % 2) + C_RANK)
                mm(bank[7][:], w_gate[rows_u, CH * (u // 2):CH * (u // 2) + CH], zT[rows_u, :],
                   start=True, stop=True).then_inc(S["gate_full"], 1)

            def qkv_gla(n, fg):
                S = att[2]
                for ft in range(16):
                    group_free(fg + ft)
                    if ft == 1:
                        project_pair(n, (bank[fg % 4], bank[(fg + 1) % 4]), h_hi, h_lo, slice(0, T), (s_hlo, 4 * DT))
                    elif ft:
                        project(n + ft, bank[(fg + ft) % 4], h_hi, h_lo, slice(0, T))
                    if ft == 11:
                        pe.wait_ge(S["z_lo"], 1)
                        for k in range(DT):
                            ins = three(bank[4][0:64, :], z_hi[:, k, :], z_lo[:, k, :], h_hi[:, k, :], h_lo[:, k, :],
                                        k == 0, k == DT - 1)
                        ins.then_inc(S["z_full"], 1)
                pe.wait_ge(S["z_copied"], 1)
                gate(S, 0)
                v_project(n + 16, fg + 16, 4, between={2: lambda: gate(S, 1)})

            def gla():
                S = att[2]

                def levels(c):
                    hd, bwd, p, ci, cs = chunk_of(c)
                    w = c // 2
                    pe.wait_ge(S["q_dec"], 8 * w + LEVELS)
                    pe.wait_ge(S["k_dec"], 8 * w + LEVELS)
                    if c >= 2:
                        pe.wait_ge(S["masked"], c - 1)
                    ks, qs = (right, left) if bwd else (left, right)
                    out = bank[2 * (c % 2)]
                    for l in range(3):
                        n = CH >> l
                        for b in range(0, CH, n):
                            v = slice(ci.start + b, ci.start + b + n)
                            mm(out[b:b + n, b:b + n], ks[w % 2][:, l, v], qs[w % 2][:, l, v], start=l == 0, stop=l == 2,
                               skip_group_check=True)
                    for l in range(3, 8):
                        plane = l - 2
                        out = bank[2 * (c % 2) + plane // 4][:, CH * (plane % 4):CH * (plane % 4) + CH]
                        if l < LEVELS:
                            ins = mm(out, ks[w % 2][:, l, ci], qs[w % 2][:, l, ci], start=True, stop=True)
                        else:
                            ins = mm(out, qk[:, 4 + hd, cs], qk[:, hd, cs], start=True, stop=True)
                    ins.then_inc(S["score_full"], 1)

                def turn_keys(c):
                    hd, bwd, p, ci, cs = chunk_of(c)
                    w = c // 2
                    if c % 4 < 3:
                        pe.wait_ge(S["k_dec"], 8 * w + 8)
                        if c:
                            pe.wait_ge(S["k_endT"], states(c) - 1)
                        if c % 8 == 1 and hd:
                            pe.wait_ge(S["rs_ready"], hd)
                        nc.tensor.transpose(bank[6][:, 0:CH], k_end[w % 2][:, ci], ident).then_inc(S["turned"], 1)

                def chunk(c):
                    hd, bwd, p, ci, cs = chunk_of(c)
                    w = c // 2
                    vals = v_tok[:, cs.start // CH, C_HV * hd:C_HV * hd + C_HV]
                    pe.wait_ge(S["scores"], c + 1)
                    pe.wait_ge(S["q_dec"], 8 * w + 8)
                    if c % 8 == 0 and hd:
                        pe.wait_ge(S["o_copied_act"], hd)
                        pe.wait_ge(S["o_copied_dve"], hd)
                    if c % 4:
                        pe.wait_ge(S["state"], states(c - 1))
                    for v in range(2):
                        vc = slice(CH * v, CH * v + CH)
                        ins = mm(bank[4 + v][:, cs], vals[:, vc], scores[:], start=c % 8 == 0, stop=False,
                                 skip_group_check=True)
                        if c % 4:
                            ins = mm(bank[4 + v][:, cs], state[(c % 4 - 1) % 2][:, vc], q_dec[w % 2][:, ci], start=False,
                                     stop=c % 8 == 7, skip_group_check=True)
                    ins.then_inc(S["o_full"], 1)
                    if c % 4 < 3:
                        pe.wait_ge(S["k_endT"], states(c))
                        if c:
                            pe.wait_ge(S["state"], states(c) - 1)
                        g = min(c // 4 + 2 + (c % 4 >= 2), C_UNITS)
                        pe.wait_ge(S["gate_soft"], g)
                        pe.wait_ge(S["gate_min"], g)
                        mm(bank[7][:, 0:C_HV], k_endT[:], vals, start=True, stop=True).then_inc(S["update_full"], 1)

                def squares_sum(hd, c):
                    pe.wait_ge(S["squared"], hd + 1)
                    pe.wait_ge(S["k_endT"], states(c))
                    for v in range(2):
                        ins = mm(bank[6][:], ones, sq_head[v][:], start=v == 0, stop=v == 1)
                    ins.then_inc(S["ss_full"], 1)

                n_chunks = 2 * C_ITEMS
                pe.wait_ge(s_free["act"], freed[start["wo", 2][1] - 9][1])
                pe.wait_ge(s_free["dve"], freed[start["wo", 2][1] - 1][1])
                levels(0)
                for c in range(n_chunks):
                    if c % 2 == 0 and gates_at(c // 2):
                        gate(S, gates_at(c // 2))
                    turn_keys(c)
                    if c + 1 < n_chunks:
                        levels(c + 1)
                    chunk(c)
                    if c % 8 == 0 and c:
                        squares_sum(c // 8 - 1, c)
                squares_sum(C_HEADS - 1, n_chunks - 1)

            pe.wait_ge(s_cst, 16)
            pe.wait_ge(s_cond, 32)
            nc.tensor.transpose(bank[4][:, 0:16], cond_row[:], ident[0:16, 0:16]).then_inc(s_cond_t, 1)
            pe.wait_ge(s_small, 16)
            nc.tensor.transpose(bank[5][:, 0:32], small_row[:], ident[0:32, 0:32]).then_inc(s_cond_t, 1)
            pe.wait_ge(s_cond_v, 1)
            for g in range(4):
                for q in range(4):
                    mod_slab(4 * g + q, g, q)
                if g == 0:
                    pe.wait_ge(s_lam_p, 1)
                    mm(bank[5][:, 0:2], ones[0:HD, :], small[0:HD, 9:11], start=True, stop=True).then_inc(s_lam_d, 1)
                    pe.wait_ge(s_rows, 16)
                    for b in range(2):
                        for r in range(4):
                            ins = nc.tensor.transpose(bank[2 + b][:, r * P:r * P + P], rows[:, 4 * b + r, :], ident)
                        ins.then_inc(s_rows_t, 1)
                if g in (1, 2):
                    pe.wait_ge(s_tok, 32)
                    for k in range(4 * g - 4, 4 * g):
                        if k >= 2:
                            pe.wait_ge(s_xn, k - 1)
                        for tt in range(4):
                            ins = nc.tensor.transpose(bank[k % 2][:, tt * P:tt * P + P], tok[:, tt, k * P:k * P + P], ident)
                        ins.then_inc(s_tok_t, 1)
                mod_turn(g)
            for i in range(layers):
                st = 2 * i
                n, fg = start["qkv", i]
                if i == 0:
                    qkv_norm_rope(n, fg)
                elif i == 2:
                    qkv_gla(n, fg)
                else:
                    qkv_plain(i, n, fg)
                gla() if i == 2 else attention(i)
                n, fg = start["wo", i]
                c = cols(i, "tail")
                for dt in range(DT):
                    group_free(fg + dt)
                    project(n, bank[(fg + dt) % 4], h_hi, h_lo, c, ready=(att[i]["o_lo"], 0) if dt == 0 else None)
                    n += 1
                    for m in mods_after("wo", dt) if i == 0 else ():
                        if m in (24, 28):
                            mod_turn(3 + m // 4)
                        mod_slab(n, 4 + m // 4, m % 4)
                        n += 1
                if i == 0:
                    mod_turn(11)
                n, fg = start["premod", i]
                nxt = 12 * (i + 1)
                stats(st, c)
                for q in range(PREMOD if i + 1 < layers else 0):
                    mod_slab(n + q, nxt, q)
                n, fg = start["up", i]
                per = 8 if i + 1 < layers else 4
                group_free(fg + 3)

                def two_tiles(it, first=False):
                    for u in range(2):
                        at_slab = n + per // 2 * u
                        for k in range(2):
                            pe.wait_ge(s_free["dve"], freed[fg][1] - 4 + 2 * u + k + 4 * it)
                            if not (first and u == 0):
                                project(at_slab + k, bank[2 * u + k], h_hi, h_lo, c, it=it, per=per)
                            elif k == 1:
                                project_pair(at_slab, bank, h_hi, h_lo, c, (s_hlo, (st + 1) * DT))
                        if per == 8:
                            if u == 1:
                                mod_turn(nxt, it)
                            for q in range(2):
                                mod_slab(at_slab + 2 + q, nxt + u, (2 - 2 * u) + q, it=it, per=per)

                two_tiles(0, first=True)
                with pe.Fori(1, FT // 2) as it:
                    two_tiles(it)
                if i + 1 < layers:
                    n, fg = start["postmod", i]
                    for q in range(2):
                        mod_slab(n + q, nxt + 11, 2 + q)
                n, fg = start["down", i]
                for dt in range(DT):
                    group_free(fg + dt)
                    for q, (k0, nk) in enumerate(((0, 8), (8, 8), (16, 6))):
                        project(n + 3 * dt + q, bank[(fg + dt) % 4], g_hi, g_lo, c, k0, nk, first=q == 0, last=q == 2,
                                ready=(s_glo, FT * i) if dt == 0 else None)
                    if dt == 0 and i + 1 < layers:
                        mod_turn(nxt + 11)
                stats(st + 1, c)
            for q in range(4):
                if q == 0:
                    pe.wait_ge(s_outf, DT)
                for k in range(4):
                    ins = nc.tensor.transpose(bank[q][:, k * P:k * P + P],
                                              out_f[:, 4 * (q % 2) + k, P * (q // 2):P * (q // 2) + P], ident)
                ins.then_inc(s_outt, 1)


def kernel(**inputs):
    import numpy as _np
    import concourse.bacc as _bacc
    from concourse import mybir as _mybir
    from concourse.bass_utils import run_bass_kernel_spmd as _run

    nc = _bacc.Bacc("TRN2", target_bir_lowering=False, num_devices=1, dynamic_dma_scratch_size=1024)
    data = {k: _np.ascontiguousarray(v) for k, v in inputs.items()}
    per_layer = []
    for i in range(DEPTH):
        per_layer += [data[n][i].reshape(-1, P) for n in ("mod_b", "ln1_g", "ln1_b", "ln2_g", "ln2_b",
                                                          "ffn_conv_b", "ffn_conv_w")]
    table = _np.concatenate(per_layer, 0)
    for n in ("mod_b", "ln1_g", "ln1_b", "ln2_g", "ln2_b", "ffn_conv_b", "ffn_conv_w"):
        del data[n]
    data["rows"] = table
    zeros = _np.zeros
    lam = [data.pop("b_lambda_" + n)[0] for n in ("q1", "k1", "q2", "k2")]
    small = zeros((32, P), _np.float32)
    small[0], small[1] = _np.tile(data.pop("a_q_norm")[0], 2), _np.tile(data.pop("a_k_norm")[0], 2)
    small[2], small[3:5] = data.pop("b_subln")[0], data.pop("c_norm")[0].reshape(2, P)
    for n in range(4):
        small[5 + n, 0:HD] = lam[n]
    small[16:20], small[20:24] = data.pop("c_b_gate_fwd")[0].reshape(4, P), data.pop("c_b_gate_bwd")[0].reshape(4, P)
    data["small"] = small
    data["k_const"], data["k_window"] = constants()
    data["k_blocks"] = block_masks()
    arrays, args = {}, {}
    for name, x in data.items():
        arrays[f"in_{name}"] = x
        args[name] = nc.dram_tensor(f"in_{name}", x.shape, _mybir.dt.from_np(x.dtype), kind="ExternalInput").ap()
    args["out"] = nc.dram_tensor("out_0", (1, LAT, D), _mybir.dt.float32, kind="ExternalOutput").ap()
    build_program(nc, args)
    r = _run(nc, [arrays], core_ids=[0])
    return r.results[0]["out_0"]
```
